# Optimizing a Trainium2 kernel written in Bass

```python
import jax, jax.numpy as jnp
from jax import lax
import numpy as np

D_MODEL = 1024
BATCH = 1
SEQ = 256
DEPTH = 1

CHUNK = 64
Q_BLOCK = 128

D_A = D_MODEL // 2
N_A = 64
H_A = D_A // N_A
LORA_W = max(32, int(round(1.8 * D_A ** 0.5 / 32)) * 32)
LORA_A = max(32, int(round(1.8 * D_A ** 0.5 / 32)) * 32)
LORA_G = max(32, int(round(0.6 * D_A ** 0.8 / 32)) * 32)
LNX_EPS = 64e-5

D_B = D_MODEL // 2
HD_B = 64
H_B = D_B // HD_B

D_FF = ((8 * D_MODEL // 3 + 255) // 256) * 256
RMS_EPS = 1e-6

SHIFT_COLS = 3 * D_A + LORA_W + LORA_A + LORA_G
FOX_COLS = 3 * D_B + H_B
IN_COLS = SHIFT_COLS + FOX_COLS + 2 * D_MODEL


def rms_norm(x, g):
    xf = x.astype(jnp.float32)
    y = xf * lax.rsqrt(jnp.mean(xf * xf, axis=-1, keepdims=True) + RMS_EPS)
    return (y * g.astype(jnp.float32)).astype(x.dtype)

def swiglu(h, w1, w3, w2):
    return (jax.nn.silu(h @ w1) * (h @ w3)) @ w2

def token_shift(u, mu):
    prev = jnp.pad(u, ((0, 0), (1, 0), (0, 0)))[:, :-1]
    return u + (prev - u) * mu

def rwkv7_recurrence(r, w, k, v, a, b):
    B, S, H, N = r.shape
    n_chunks = S // CHUNK

    def to_chunks(t):
        return jnp.moveaxis(t, 1, 0).reshape(n_chunks, CHUNK, B, H, N)

    def step(state, inp):
        r_t, w_t, k_t, v_t, a_t, b_t = inp
        sa = jnp.einsum('bhvk,bhk->bhv', state, a_t)
        state = (state * w_t[:, :, None, :]
                 + sa[..., :, None] * b_t[:, :, None, :]
                 + v_t[..., :, None] * k_t[:, :, None, :])
        y_t = jnp.einsum('bhvk,bhk->bhv', state, r_t)
        return state, y_t

    def chunk_step(state, chunk_inp):
        return lax.scan(step, state, chunk_inp)

    xs = tuple(to_chunks(t) for t in (r, w, k, v, a, b))
    state0 = jnp.zeros((B, H, N, N), jnp.float32)
    _, ys = lax.scan(chunk_step, state0, xs)
    return jnp.moveaxis(ys.reshape(S, B, H, N), 0, 1)

def rwkv7_mixer(p, w0, w_up, a0, a_up, g_up, k_k, k_a, r_k, lnx_g, lnx_b):
    B, S, _ = p.shape
    f32 = jnp.float32
    r, k, v, w_lo, a_lo, g_lo = jnp.split(
        p, [D_A, 2 * D_A, 3 * D_A, 3 * D_A + LORA_W, 3 * D_A + LORA_W + LORA_A], axis=-1)
    w_log = -jax.nn.softplus(-(w0 + jnp.tanh(w_lo) @ w_up)) - 0.5
    decay = jnp.exp(-jnp.exp(w_log.astype(f32)))
    a = jax.nn.sigmoid(a0 + a_lo @ a_up)
    g = jax.nn.sigmoid(g_lo) @ g_up

    def heads(t):
        return t.astype(f32).reshape(B, S, H_A, N_A)

    r, k, v, a, decay = heads(r), heads(k), heads(v), heads(a), heads(decay)
    kk = k * k_k.astype(f32).reshape(H_A, N_A)
    kk = kk / jnp.maximum(jnp.sqrt(jnp.sum(kk * kk, axis=-1, keepdims=True)), 1e-12)
    k = k * (1.0 + (a - 1.0) * k_a.astype(f32).reshape(H_A, N_A))
    y = rwkv7_recurrence(r, decay, k, v, -kk, kk * a)
    mu = jnp.mean(y, axis=-1, keepdims=True)
    var = jnp.mean(jnp.square(y - mu), axis=-1, keepdims=True)
    y = ((y - mu) * lax.rsqrt(var + LNX_EPS)).reshape(B, S, D_A)
    y = y * lnx_g.astype(f32) + lnx_b.astype(f32)
    bonus = jnp.sum(r * k * r_k.astype(f32), axis=-1, keepdims=True) * v
    y = (y + bonus.reshape(B, S, D_A)) * g.astype(f32)
    return y.astype(p.dtype)

def forgetting_attention(q, k, v, log_f):
    B, H, S, hd = q.shape
    nb = S // Q_BLOCK
    scale = 1.0 / np.sqrt(hd).astype(np.float32)
    cum = jnp.cumsum(log_f, axis=-1)
    q_blocks = q.reshape(B, H, nb, Q_BLOCK, hd).transpose(2, 0, 1, 3, 4)
    c_blocks = cum.reshape(B, H, nb, Q_BLOCK).transpose(2, 0, 1, 3)
    pos_k = jnp.arange(S)

    def one_block(args):
        i, q_i, c_i = args
        s = jnp.einsum('bhqd,bhkd->bhqk', q_i, k, preferred_element_type=jnp.float32) * scale
        s = s + c_i[..., :, None] - cum[..., None, :]
        pos_q = i * Q_BLOCK + jnp.arange(Q_BLOCK)
        mask = pos_k[None, :] <= pos_q[:, None]
        s = jnp.where(mask, s, -jnp.inf)
        pr = jax.nn.softmax(s, axis=-1)
        return jnp.einsum('bhqk,bhkd->bhqd', pr.astype(v.dtype), v)

    out = lax.map(one_block, (jnp.arange(nb), q_blocks, c_blocks))
    return out.transpose(1, 2, 0, 3, 4).reshape(B, H, S, hd)

def fox_mixer(p, f_bias, q_norm, k_norm):
    B, S, _ = p.shape
    q, k, v, f_lo = jnp.split(p, [D_B, 2 * D_B, 3 * D_B], axis=-1)

    def heads(t):
        return t.reshape(B, S, H_B, HD_B).transpose(0, 2, 1, 3)

    q = rms_norm(heads(q), q_norm)
    k = rms_norm(heads(k), k_norm)
    v = heads(v)
    log_f = jax.nn.log_sigmoid((f_lo + f_bias).astype(jnp.float32)).transpose(0, 2, 1)
    o = forgetting_attention(q, k, v, log_f)
    return o.transpose(0, 2, 1, 3).reshape(B, S, D_B)

def first_inputs(seed: int = 0) -> dict:
    key = jax.random.key(seed)
    ks = jax.random.split(key, 28)
    L = DEPTH
    f32 = jnp.float32

    def nrm(k, shape, scale):
        return jax.random.normal(k, shape, f32) * scale

    def gain(k, shape):
        return 1.0 + 0.05 * jax.random.normal(k, shape, f32)

    return {
        "x": nrm(ks[0], (BATCH, SEQ, D_MODEL), 1.0),
        "ffn1_norm": gain(ks[1], (L, D_MODEL)),
        "ffn1_w1": nrm(ks[2], (L, D_MODEL, D_FF), D_MODEL ** -0.5),
        "ffn1_w3": nrm(ks[3], (L, D_MODEL, D_FF), D_MODEL ** -0.5),
        "ffn1_w2": nrm(ks[4], (L, D_FF, D_MODEL), D_FF ** -0.5),
        "mix_norm": gain(ks[5], (L, D_MODEL)),
        "w_in": nrm(ks[6], (L, D_MODEL, IN_COLS), D_MODEL ** -0.5),
        "shift_mu": jax.random.uniform(ks[7], (L, SHIFT_COLS), f32),
        "rwkv_w0": jax.random.uniform(ks[8], (L, D_A), f32, -6.5, -1.5),
        "rwkv_w_up": nrm(ks[9], (L, LORA_W, D_A), 0.5 * LORA_W ** -0.5),
        "rwkv_a0": nrm(ks[10], (L, D_A), 0.1),
        "rwkv_a_up": nrm(ks[11], (L, LORA_A, D_A), LORA_A ** -0.5),
        "rwkv_g_up": nrm(ks[12], (L, LORA_G, D_A), LORA_G ** -0.5),
        "rwkv_k_k": 0.85 + 0.05 * jax.random.normal(ks[13], (L, D_A), f32),
        "rwkv_k_a": gain(ks[14], (L, D_A)),
        "rwkv_r_k": nrm(ks[15], (L, H_A, N_A), 0.1),
        "rwkv_lnx_g": gain(ks[16], (L, D_A)),
        "rwkv_lnx_b": nrm(ks[17], (L, D_A), 0.02),
        "rwkv_proj": nrm(ks[18], (L, D_A, D_MODEL), D_A ** -0.5),
        "fox_f_bias": 2.0 + 0.5 * jax.random.normal(ks[19], (L, H_B), f32),
        "fox_q_norm": gain(ks[20], (L, HD_B)),
        "fox_k_norm": gain(ks[21], (L, HD_B)),
        "fox_proj": nrm(ks[22], (L, D_B, D_MODEL), D_B ** -0.5),
        "w_out": nrm(ks[23], (L, D_MODEL, D_MODEL), D_MODEL ** -0.5),
        "ffn2_norm": gain(ks[24], (L, D_MODEL)),
        "ffn2_w1": nrm(ks[25], (L, D_MODEL, D_FF), D_MODEL ** -0.5),
        "ffn2_w3": nrm(ks[26], (L, D_MODEL, D_FF), D_MODEL ** -0.5),
        "ffn2_w2": nrm(ks[27], (L, D_FF, D_MODEL), D_FF ** -0.5),
        "final_norm": gain(jax.random.fold_in(key, 99), (D_MODEL,)),
    }

def first_block(x, ffn1_norm, ffn1_w1, ffn1_w3, ffn1_w2, mix_norm, w_in, shift_mu,
              rwkv_w0, rwkv_w_up, rwkv_a0, rwkv_a_up, rwkv_g_up, rwkv_k_k, rwkv_k_a, rwkv_r_k,
              rwkv_lnx_g, rwkv_lnx_b, rwkv_proj, fox_f_bias, fox_q_norm, fox_k_norm, fox_proj,
              w_out, ffn2_norm, ffn2_w1, ffn2_w3, ffn2_w2, final_norm):
    for l in range(DEPTH):
        x = x + 0.5 * swiglu(rms_norm(x, ffn1_norm[l]), ffn1_w1[l], ffn1_w3[l], ffn1_w2[l])

        h = rms_norm(x, mix_norm[l])
        p = h @ w_in[l]
        p_rwkv = token_shift(p[..., :SHIFT_COLS], shift_mu[l])
        p_fox = p[..., SHIFT_COLS:SHIFT_COLS + FOX_COLS]
        gates = jax.nn.sigmoid(p[..., SHIFT_COLS + FOX_COLS:])
        gate_a, gate_b = gates[..., :D_MODEL], gates[..., D_MODEL:]

        y_a = rwkv7_mixer(p_rwkv, rwkv_w0[l], rwkv_w_up[l], rwkv_a0[l], rwkv_a_up[l], rwkv_g_up[l],
                          rwkv_k_k[l], rwkv_k_a[l], rwkv_r_k[l], rwkv_lnx_g[l], rwkv_lnx_b[l]) @ rwkv_proj[l]
        y_b = fox_mixer(p_fox, fox_f_bias[l], fox_q_norm[l], fox_k_norm[l]) @ fox_proj[l]
        x = x + (gate_a * y_a + gate_b * y_b) @ w_out[l]

        x = x + 0.5 * swiglu(rms_norm(x, ffn2_norm[l]), ffn2_w1[l], ffn2_w3[l], ffn2_w2[l])
    return rms_norm(x, final_norm)


GRID_W = 64
CTX_LEN = 256
RET_HEADS = 4
RET_DK = 256
RET_DV = 512
RET_CHUNK = 128
FOURIER_GROUPS = 4
FOURIER_DG = 256
D_FF_2 = 2816
ROPE_BASE = 10000.0
EPS = 1e-6
N_MOD = 9

RET_QK = RET_HEADS * RET_DK
RET_V = RET_HEADS * RET_DV
FOURIER_W = FOURIER_GROUPS * FOURIER_DG
IN_COLS_2 = 2 * RET_QK + 2 * RET_V + FOURIER_W + 2 * D_MODEL
SPLITS = (RET_QK, 2 * RET_QK, 2 * RET_QK + RET_V, 2 * RET_QK + 2 * RET_V,
          2 * RET_QK + 2 * RET_V + FOURIER_W, 2 * RET_QK + 2 * RET_V + FOURIER_W + D_MODEL)


def rmsnorm(x, w):
    xf = x.astype(jnp.float32)
    y = xf * lax.rsqrt(jnp.mean(xf * xf, axis=-1, keepdims=True) + EPS)
    return (y * w.astype(jnp.float32)).astype(x.dtype)

def modulate(h, shift, scale):
    return h * (1 + scale) + shift

def swiglu_2(h, w13, w2):
    a, b = jnp.split(h @ w13, 2, axis=-1)
    return (jax.nn.silu(a) * b) @ w2

def heads(a, dh):
    B, L, _ = a.shape
    return a.reshape(B, L, -1, dh).transpose(0, 2, 1, 3)

def project(h, w_in):
    u = h @ w_in
    q, k, v, g, f, ga, gf = jnp.split(u, SPLITS, axis=-1)
    q = heads(q, RET_DK).astype(jnp.float32) * (RET_DK ** -0.5)
    k = heads(k, RET_DK).astype(jnp.float32)
    v = heads(v, RET_DV).astype(jnp.float32)
    return q, k, v, g, f, ga, gf

def rope_2d(a, rows):
    row = jnp.repeat(jnp.arange(rows, dtype=jnp.float32), GRID_W)
    col = jnp.tile(jnp.arange(GRID_W, dtype=jnp.float32), rows)
    n_freq = RET_DK // 4
    inv = ROPE_BASE ** (-jnp.arange(n_freq, dtype=jnp.float32) / n_freq)
    ang = jnp.concatenate([row[:, None] * inv, col[:, None] * inv], axis=-1)
    cos, sin = jnp.cos(ang), jnp.sin(ang)
    a1, a2 = a[..., 0::2], a[..., 1::2]
    return jnp.stack([a1 * cos - a2 * sin, a1 * sin + a2 * cos], axis=-1).reshape(a.shape)

def retention_scan(q, k, v, log_gamma, s0):
    B, H, L, dk = q.shape
    dv = v.shape[-1]
    C = RET_CHUNK
    n = L // C
    idx = jnp.arange(C, dtype=jnp.float32)
    lg = log_gamma[:, None]
    diff = idx[:, None] - idx[None, :]
    decay_intra = jnp.where(diff >= 0, jnp.exp(lg[:, :, None] * jnp.maximum(diff, 0.0)), 0.0)
    xi = jnp.exp(lg * (idx + 1.0))
    zeta = jnp.exp(lg * (C - 1.0 - idx))
    g_chunk = jnp.exp(log_gamma * C)

    def to_chunks(a):
        return jnp.moveaxis(a.reshape(B, H, n, C, a.shape[-1]), 2, 0)

    def step(s, qkv):
        qc, kc, vc = qkv
        sc = jnp.einsum('bhid,bhjd->bhij', qc, kc) * decay_intra
        o = (jnp.einsum('bhij,bhjv->bhiv', sc, vc)
             + jnp.einsum('bhid,bhdv->bhiv', qc, s) * xi[None, :, :, None])
        s = s * g_chunk[None, :, None, None] + jnp.einsum('bhjd,bhjv->bhdv', kc * zeta[None, :, :, None], vc)
        return s, o

    s, o = lax.scan(step, s0, (to_chunks(q), to_chunks(k), to_chunks(v)))
    o = jnp.moveaxis(o, 0, 2).reshape(B, H, L, dv)
    return o, s

def bidir_retention(q, k, v, lg_f, lg_b, s_f0, s_b0):
    o_f, s_f = retention_scan(q, k, v, lg_f, s_f0)
    flip = lambda a: jnp.flip(a, axis=2)
    o_b, s_b = retention_scan(flip(q), flip(k), flip(v), lg_b, s_b0)
    return o_f + flip(o_b), s_f, s_b

def retention_out(o, g, gn_w, p_ret):
    mu = jnp.mean(o, axis=-1, keepdims=True)
    var = jnp.mean(jnp.square(o - mu), axis=-1, keepdims=True)
    on = (o - mu) * lax.rsqrt(var + EPS)
    B, H, L, dv = o.shape
    on = on.transpose(0, 2, 1, 3).reshape(B, L, H * dv).astype(g.dtype) * gn_w
    return (jax.nn.silu(g) * on) @ p_ret

def fourier_branch(f, p_four):
    B, L, _ = f.shape
    fg = f.reshape(B, L, FOURIER_GROUPS, FOURIER_DG).astype(jnp.float32)
    mixed = jnp.fft.fft2(fg, axes=(1, 3), norm="ortho").real
    return mixed.reshape(B, L, FOURIER_W).astype(f.dtype) @ p_four

def merge(r, fo, ga, gf, w_out):
    return (jax.nn.sigmoid(ga) * r + jax.nn.sigmoid(gf) * fo) @ w_out

def second_inputs(seed: int = 0) -> dict:
    key = jax.random.key(seed)
    ks = jax.random.split(key, 24)

    def w(k, shape, fan_in, scale=1.0):
        return jax.random.normal(k, shape, jnp.float32) * (scale * fan_in ** -0.5)

    def gain(k, shape):
        return 1.0 + 0.02 * jax.random.normal(k, shape, jnp.float32)

    decay_base = jnp.asarray(np.log(2.0 ** (5 + np.arange(RET_HEADS)) - 1.0).astype(np.float32))
    return {
        "x": jax.random.normal(ks[0], (BATCH, SEQ, D_MODEL), jnp.float32),
        "c": jax.random.normal(ks[1], (BATCH, D_MODEL), jnp.float32),
        "ctx": jax.random.normal(ks[2], (BATCH, CTX_LEN, D_MODEL), jnp.float32),
        "c_ctx": 0.5 * jax.random.normal(ks[3], (D_MODEL,), jnp.float32),
        "w_ada": w(ks[4], (DEPTH, D_MODEL, N_MOD * D_MODEL), D_MODEL, 0.5),
        "b_ada": 0.02 * jax.random.normal(ks[5], (DEPTH, N_MOD * D_MODEL), jnp.float32),
        "norm_ffn1": gain(ks[6], (DEPTH, D_MODEL)),
        "w13_ffn1": w(ks[7], (DEPTH, D_MODEL, 2 * D_FF_2), D_MODEL),
        "w2_ffn1": w(ks[8], (DEPTH, D_FF_2, D_MODEL), D_FF_2),
        "norm_mix": gain(ks[9], (DEPTH, D_MODEL)),
        "w_in": w(ks[10], (DEPTH, D_MODEL, IN_COLS_2), D_MODEL),
        "decay_fwd": decay_base[None, :] + 0.05 * jax.random.normal(ks[11], (DEPTH, RET_HEADS), jnp.float32),
        "decay_bwd": decay_base[None, :] + 0.05 * jax.random.normal(ks[12], (DEPTH, RET_HEADS), jnp.float32),
        "ret_gn_w": gain(ks[13], (DEPTH, RET_V)),
        "p_ret": w(ks[14], (DEPTH, RET_V, D_MODEL), RET_V),
        "p_four": w(ks[15], (DEPTH, FOURIER_W, D_MODEL), FOURIER_W),
        "w_out": w(ks[16], (DEPTH, D_MODEL, D_MODEL), D_MODEL),
        "norm_ffn2": gain(ks[17], (DEPTH, D_MODEL)),
        "w13_ffn2": w(ks[18], (DEPTH, D_MODEL, 2 * D_FF_2), D_MODEL),
        "w2_ffn2": w(ks[19], (DEPTH, D_FF_2, D_MODEL), D_FF_2),
        "norm_final": gain(ks[20], (D_MODEL,)),
    }

def second_block(x, c, ctx, c_ctx, w_ada, b_ada, norm_ffn1, w13_ffn1, w2_ffn1, norm_mix, w_in,
              decay_fwd, decay_bwd, ret_gn_w, p_ret, p_four, w_out, norm_ffn2, w13_ffn2, w2_ffn2,
              norm_final):
    B, L, _ = x.shape
    rows = L // GRID_W
    for l in range(DEPTH):
        last = l == DEPTH - 1
        mod_x = (jax.nn.silu(c) @ w_ada[l] + b_ada[l])[:, None, :]
        mod_c = (jax.nn.silu(c_ctx) @ w_ada[l] + b_ada[l])[None, None, :]
        sh1x, sc1x, g1x, sh2x, sc2x, g2x, sh3x, sc3x, g3x = jnp.split(mod_x, N_MOD, axis=-1)
        sh1c, sc1c, g1c, sh2c, sc2c, g2c, sh3c, sc3c, g3c = jnp.split(mod_c, N_MOD, axis=-1)

        x = x + 0.5 * g1x * swiglu_2(modulate(rmsnorm(x, norm_ffn1[l]), sh1x, sc1x), w13_ffn1[l], w2_ffn1[l])
        ctx = ctx + 0.5 * g1c * swiglu_2(modulate(rmsnorm(ctx, norm_ffn1[l]), sh1c, sc1c), w13_ffn1[l], w2_ffn1[l])

        lg_f = jax.nn.log_sigmoid(decay_fwd[l].astype(jnp.float32))
        lg_b = jax.nn.log_sigmoid(decay_bwd[l].astype(jnp.float32))

        qc, kc, vc, gc, fc, gac, gfc = project(modulate(rmsnorm(ctx, norm_mix[l]), sh2c, sc2c), w_in[l])
        zero = jnp.zeros((ctx.shape[0], RET_HEADS, RET_DK, RET_DV), jnp.float32)
        o_c, s_f, s_b = bidir_retention(qc, kc, vc, lg_f, lg_b, zero, zero)

        qx, kx, vx, gx, fx, gax, gfx = project(modulate(rmsnorm(x, norm_mix[l]), sh2x, sc2x), w_in[l])
        qx = rope_2d(qx, rows)
        kx = rope_2d(kx, rows)
        o_x, _, _ = bidir_retention(qx, kx, vx, lg_f, lg_b, s_f, s_b)
        y_x = merge(retention_out(o_x, gx, ret_gn_w[l], p_ret[l]), fourier_branch(fx, p_four[l]), gax, gfx, w_out[l])
        x = x + g2x * y_x

        x = x + 0.5 * g3x * swiglu_2(modulate(rmsnorm(x, norm_ffn2[l]), sh3x, sc3x), w13_ffn2[l], w2_ffn2[l])

        if not last:
            y_c = merge(retention_out(o_c, gc, ret_gn_w[l], p_ret[l]), fourier_branch(fc, p_four[l]), gac, gfc, w_out[l])
            ctx = ctx + g2c * y_c
            ctx = ctx + 0.5 * g3c * swiglu_2(modulate(rmsnorm(ctx, norm_ffn2[l]), sh3c, sc3c), w13_ffn2[l], w2_ffn2[l])
    return rmsnorm(x, norm_final)


def setup_inputs(seed=0):
    out = dict(first_inputs(seed))
    for name, value in second_inputs(seed + 1).items():
        if name != "x":
            out[name + "_2"] = value
    return out


def reference(
    x, ffn1_norm, ffn1_w1, ffn1_w3, ffn1_w2, mix_norm, w_in, shift_mu, rwkv_w0, rwkv_w_up,
    rwkv_a0, rwkv_a_up, rwkv_g_up, rwkv_k_k, rwkv_k_a, rwkv_r_k, rwkv_lnx_g, rwkv_lnx_b,
    rwkv_proj, fox_f_bias, fox_q_norm, fox_k_norm, fox_proj, w_out, ffn2_norm, ffn2_w1, ffn2_w3,
    ffn2_w2, final_norm, c_2, ctx_2, c_ctx_2, w_ada_2, b_ada_2, norm_ffn1_2, w13_ffn1_2,
    w2_ffn1_2, norm_mix_2, w_in_2, decay_fwd_2, decay_bwd_2, ret_gn_w_2, p_ret_2, p_four_2,
    w_out_2, norm_ffn2_2, w13_ffn2_2, w2_ffn2_2, norm_final_2,
):
    x = first_block(
        x, ffn1_norm, ffn1_w1, ffn1_w3, ffn1_w2, mix_norm, w_in, shift_mu, rwkv_w0, rwkv_w_up,
        rwkv_a0, rwkv_a_up, rwkv_g_up, rwkv_k_k, rwkv_k_a, rwkv_r_k, rwkv_lnx_g, rwkv_lnx_b,
        rwkv_proj, fox_f_bias, fox_q_norm, fox_k_norm, fox_proj, w_out, ffn2_norm, ffn2_w1,
        ffn2_w3, ffn2_w2, final_norm,
    )
    return second_block(
        x, c_2, ctx_2, c_ctx_2, w_ada_2, b_ada_2, norm_ffn1_2, w13_ffn1_2, w2_ffn1_2,
        norm_mix_2, w_in_2, decay_fwd_2, decay_bwd_2, ret_gn_w_2, p_ret_2, p_four_2, w_out_2,
        norm_ffn2_2, w13_ffn2_2, w2_ffn2_2, norm_final_2,
    )


_drawn_inputs = setup_inputs


def setup_inputs(seed=0):
    import zlib

    import numpy as np

    out = dict(_drawn_inputs(seed))
    spreads = {}
    factors = {'rwkv_w_up': 8.0,
     'rwkv_a0': 5.093,
     'rwkv_k_k': 4.852,
     'rwkv_k_a': 3.773,
     'rwkv_lnx_g': 4.125,
     'rwkv_lnx_b': 8.0,
     'fox_q_norm': 7.586,
     'fox_k_norm': 8.0,
     'ffn2_norm': 2.987,
     'c_ctx_2': 3.62,
     'b_ada_2': 3.15,
     'norm_ffn1_2': 8.0,
     'norm_mix_2': 8.0,
     'ret_gn_w_2': 25.451,
     'norm_ffn2_2': 30.2,
     'norm_final_2': 8.094}
    for name, (base, spread) in spreads.items():
        noise = np.random.default_rng([zlib.crc32(name.encode()), seed]).standard_normal(out[name].shape)
        drawn = base * np.exp(spread * noise) if base else spread * noise
        out[name] = __import__('jax').numpy.asarray(drawn.astype(out[name].dtype))
    for name, factor in factors.items():
        out[name] = (out[name] * factor).astype(out[name].dtype)
    return out
```

```python
from contextlib import ExitStack

import numpy as np
import concourse.bass as bass
from concourse import mybir

F32 = mybir.dt.float32
F32R = mybir.dt.float32r
ALU = mybir.AluOpType
ACT = mybir.ActivationFunctionType
AX_X = mybir.AxisListType.X

P = 128
ROWS = 256
DM = 1024
KT = DM // P
FF = 2816
FT = FF // P
DA = 512
IT = DA // P
NH = 8
CH = 64
NC = ROWS // CH
RH, RDV = 4, 512
UNIT = 2048
RING = 3
DECAY = float(np.exp(-0.5))

FFN_MARKS = [2, 2] + [2, 8, 2] * 10 + [8]
MARKS = []
PHASE = {}


def _phase(name, marks):
    PHASE[name] = len(MARKS)
    MARKS.extend(marks)


_phase("ffn1", FFN_MARKS)
_phase("rwkv_in", [2] * 7)
_phase("fox_qk", [2] * 4)
_phase("fox_v", [1, 2])
_phase("rwkv_proj", [4] * 2)
_phase("fox_proj", [4] * 2)
_phase("gates", [2] * 8)
_phase("out", [2] * 4)
_phase("ffn2", FFN_MARKS)
_phase("ffn3", FFN_MARKS)
_phase("ret_k", [2] * 4)
_phase("ret_v", [1, 4] * 4)
_phase("ret_q", [2] * 4)
_phase("ret_g", [2] * 8)
_phase("four_in", [1, 2] * 2)
_phase("ret_proj", [1] * 8)
_phase("four_proj", [2] * 4)
_phase("gates2", [2] * 8)
_phase("out2", [2] * 4)
_phase("ffn4", FFN_MARKS)
NW = len(MARKS)
MARK0 = [0]
for _m in MARKS:
    MARK0.append(MARK0[-1] + _m)

ADA = 36
MODR = 36
ADA_NB = 3
ADA_AFTER = {PHASE["rwkv_in"] - 1: ADA_NB, PHASE["rwkv_proj"] - 1: ADA - ADA_NB}
ORDER = []
for _s in range(NW):
    ORDER.append(("w", _s))
    if _s - 2 in ADA_AFTER:
        _d = sum(1 for o in ORDER if o[0] == "a")
        ORDER.extend(("a", _d + n) for n in range(ADA_AFTER[_s - 2]))
RAW_OF = {o: n for n, o in enumerate(ORDER)}
NU = len(ORDER)

NORM = {n: k for k, n in enumerate(("na", "nb", "nc", "nd", "ne", "nf", "ng", "nh", "ni", "nj"))}
NORM_H = {n: k for k, n in enumerate(("na", "nb", "nc", "ne", "nf", "ng", "nh", "ni"))}
STAT = {n: k for k, n in enumerate(("kk", "bon", "fq", "fk", "mu", "var"))}

PCOLS = {}
_n = 0
for _name, _w in [("n1", 8), ("nm", 8), ("mu", 14), ("w0", 4), ("a0", 4), ("kk", 4), ("ka", 4), ("rk", 4),
                  ("lnxg", 4), ("lnxb", 4), ("fb", 1), ("qn", 1), ("kn", 1), ("n2", 8), ("nf", 8),
                  ("c", 16), ("m1", 8), ("m2", 8), ("gn", 16), ("m3", 8), ("mf", 8),
                  ("dec", 8), ("epsr", 1), ("epsl", 1), ("epsq", 1), ("one", 1), ("jcol", 6)]:
    PCOLS[_name] = (_n, _n + _w)
    _n += _w
NPAR = _n
CCOLS = {}
_n = 0
for _name, _w in [("ident", 128), ("ones", 128), ("sel", 32), ("bc", 512), ("tmask", 128), ("lmask", 384),
                  ("l0t", 64), ("causal", 128)]:
    CCOLS[_name] = (_n, _n + _w)
    _n += _w
NCON = _n


def build(nc, stream, xin, params, consts, lora, bada, rope, dft, iota, out):
    with ExitStack() as ctx:
        sems = {}

        def S(name):
            if name not in sems:
                sems[name] = ctx.enter_context(nc.semaphore(name))
            return sems[name]

        def sb(name, shape, off, dt=F32):
            return nc.alloc_sbuf_tensor_at(name, shape, dt, offset=off)

        RAW0 = 16512
        HI0 = RAW0 + RING * UNIT * 4
        LO0 = HI0 + RING * UNIT * 4
        HHI0 = LO0 + RING * UNIT * 4
        HLO0 = HHI0 + 16384
        XC0 = HLO0 + 16384
        D0 = XC0 + 16384
        CON0 = D0 + 16384
        A0 = CON0 + 9216
        B1, B2, C0 = HHI0 + 8192, HLO0 + 8192, XC0 + 8192

        RAW = [sb(f"RAW{i}", [P, UNIT], RAW0 + i * UNIT * 4) for i in range(RING)]
        W_HI = [sb(f"W_HI{i}", [P, UNIT], HI0 + i * UNIT * 4, F32R) for i in range(RING)]
        W_LO = [sb(f"W_LO{i}", [P, UNIT], LO0 + i * UNIT * 4, F32R) for i in range(RING)]
        H_HI = sb("H_HI", [P, 2, KT, ROWS], HHI0, F32R)
        H_LO = sb("H_LO", [P, 2, KT, ROWS], HLO0, F32R)
        XC = sb("XC", [P, 2, KT, ROWS], XC0)
        HID_HI = sb("HID_HI", [P, 2, 512], D0, F32R)
        HID_LO = sb("HID_LO", [P, 2, 512], D0 + 4096, F32R)
        SILU = sb("SILU", [P, 2, 512], D0 + 8192)
        PROD = sb("PROD", [P, 2, 512], D0 + 12288)
        NT = sb("NT", [P, KT, ROWS], D0 + 8192)
        CON = sb("CON", [P, NCON], CON0)
        PAR = sb("PAR", [P, NPAR], CON0 + NCON * 4)
        off = (CON0 + (NCON + NPAR) * 4 + 31) // 32 * 32
        MOD = sb("MOD", [P, 72, 2], off)
        off += 576
        SCZ = sb("SCZ", [P, MODR * (KT + 1) - 2], off)
        off += (MODR * (KT + 1) - 2) * 4
        off = (off + 31) // 32 * 32
        GAIN = sb("GAIN", [P, 5, 8], off)
        off += 160
        GATE = sb("GATE", [P, 4, 8], off)
        off += 128
        LG = sb("LG", [P, 5, 8], off)
        off += 160
        LB = sb("LB", [P, RH, 4], off)
        off += 64
        assert off <= A0

        def con(name, rows=P):
            a, b = CCOLS[name]
            return CON[0:rows, a:b]

        def par(name, i=0, n=1, rows=P):
            a = PCOLS[name][0]
            return PAR[0:rows, a + i:a + i + n]

        STD = sb("STD", [P, ROWS], A0 + 61440)
        RSTD = sb("RSTD", [P, ROWS], A0 + 62464)

        PRE = sb("PRE", [P, 14, ROWS + 1], A0)
        RKV = sb("RKV", [P, 3, IT, ROWS], A0 + 14400)
        LOR = sb("LOR", [P, 2, ROWS], A0 + 26688)
        FQ = sb("FQ", [P, IT, ROWS], A0 + 28736)
        FK = sb("FK", [P, IT, ROWS], A0 + 32832)
        FV = sb("FV", [P, 2, DA], A0 + 36928)
        LW = sb("LW", [P, 2, DA], A0 + 41024)
        SG = sb("SG", [P, IT, ROWS], A0 + 45120)
        AA = sb("AA", [P, IT, ROWS], A0 + 49216)
        KK = sb("KK", [P, IT, ROWS], A0 + 53312)
        TMP = sb("TMP", [P, IT, ROWS], A0 + 57408)
        STA = sb("STA", [NH, ROWS], A0 + 61504)
        STB = sb("STB", [NH, ROWS], A0 + 62528)
        GG = sb("GG", [P, IT, ROWS], B1)
        BO = sb("BO", [P, IT, ROWS], B1 + 4096)
        AR = sb("AR", [P, IT, NC, 2, CH], B2)
        BK = sb("BK", [P, IT, NC, 2, CH], C0)
        AV = sb("AV", [P, IT, NC, 2, CH], D0)
        LS = sb("LS", [P, IT, ROWS], D0 + 8192)
        PC = sb("PC", [P, IT, ROWS], D0 + 12288)
        F1 = sb("F1", [NH, ROWS], A0 + 41024)
        F2 = sb("F2", [NH, ROWS], A0 + 42048)
        F3 = sb("F3", [NH, ROWS], A0 + 43072)
        F4 = sb("F4", [NH, ROWS], A0 + 44096)
        NCB = sb("NCB", [P, NH, ROWS], A0)
        SCO = sb("SCO", [P, 2, 384], A0 + 8192)
        PRT = sb("PRT", [P, 2, 384], A0 + 11264)
        YB = sb("YB", [P, IT, ROWS], D0 + 8192)
        FST = sb("FST", [P, 2, 6], A0 + 14336)
        TT = sb("TT", [P, NC, NH, 2 * CH], A0)
        XM = sb("XM", [CH, 2, 16, CH], A0 + 16384)
        XT = sb("XT", [CH, 2, 16, CH], A0 + 24576)
        ZM = sb("ZM", [CH, 2, 16, CH], A0 + 32768)
        BKR = sb("BKR", [P, NC, DA], A0 + 40960)
        AVR = sb("AVR", [P, NC, DA], A0 + 49152)
        GT = sb("GT", [P, NC, IT, CH], A0 + 57344)
        WM = sb("WM", [CH, NC * NH, CH], C0)
        UM = sb("UM", [CH, NC, NH, CH], D0)
        ST = sb("ST", [P, NC + 1, IT, CH], A0 + 32768)
        YY = sb("YY", [P, IT, ROWS], A0 + 16384)
        YS = sb("YS", [P, IT, ROWS], A0 + 20480)
        YA_HI = sb("YA_HI", [P, IT, ROWS], C0, F32R)
        YA_LO = sb("YA_LO", [P, IT, ROWS], C0 + 4096, F32R)
        YB_HI = sb("YB_HI", [P, IT, ROWS], D0, F32R)
        YB_LO = sb("YB_LO", [P, IT, ROWS], D0 + 4096, F32R)
        MROW = sb("MROW", [MODR, 512], A0 + 45056)
        OA = sb("OA", [P, KT, ROWS], A0)
        OB = sb("OB", [P, KT, ROWS], A0 + 8192)
        M_HI = sb("M_HI", [P, KT, ROWS], A0 + 16384, F32R)
        M_LO = sb("M_LO", [P, KT, ROWS], A0 + 24576, F32R)
        SGA = sb("SGA", [P, 4, ROWS], A0 + 32768)
        MT = sb("MT", [P, 2, 3, ROWS], A0 + 36864)

        RK = sb("RK", [P, 2, KT, ROWS], A0)
        RV = sb("RV", [P, 4, RH * RDV], A0 + 16384)
        RQ = sb("RQ", [P, KT, ROWS], A0 + 49152)
        ROPE = sb("ROPE", [P, 2, ROWS], A0 + 57344)
        RT = sb("RT", [P, 4, ROWS], A0 + 59392)
        RO = sb("RO", [P, 16, ROWS], D0)
        PT = sb("PT", [P, 4, ROWS], C0)
        DD = sb("DD", [P, 4, ROWS], C0 + 4096)
        T1 = sb("T1", [P, 2, ROWS], B1)
        T2 = sb("T2", [P, 2, ROWS], B1 + 2048)
        EB = sb("EB", [P, 2, ROWS], B1 + 4096)
        IOTA = sb("IOTA", [P, ROWS], B1 + 6144)
        SQ = sb("SQ", [P, 4, ROWS], B2)
        RST = sb("RST", [P, 2, ROWS], B2 + 4096)
        SGG = sb("SGG", [P, 2, ROWS], B2 + 6144)
        R_HI = sb("R_HI", [P, 16, ROWS], A0 + 16384, F32R)
        R_LO = sb("R_LO", [P, 16, ROWS], A0 + 32768, F32R)
        FX = sb("FX", [P, 2, DM], A0)
        DFT = sb("DFT", [P, 2, 512], A0 + 8192)
        ZZ = sb("ZZ", [P, 2, 2, 512], A0 + 49152)
        X_HI = sb("X_HI", [P, KT, ROWS], D0, F32R)
        X_LO = sb("X_LO", [P, KT, ROWS], D0 + 8192, F32R)
        FM = sb("FM", [P, 2, 2, ROWS], B2)
        OR = sb("OR", [P, KT, ROWS], C0)
        OF = sb("OF", [P, KT, ROWS], B1)
        M2_HI = sb("M2_HI", [P, KT, ROWS], A0, F32R)
        M2_LO = sb("M2_LO", [P, KT, ROWS], A0 + 8192, F32R)
        SG2 = sb("SG2", [P, 4, ROWS], A0 + 49152)
        MT2 = sb("MT2", [P, 2, 3, ROWS], A0 + 53248)

        PS = ctx.enter_context(nc.psum_tensor("PS", [P, 8, 512], F32))
        BK8 = [PS[:, i] for i in range(8)]
        ADAP = BK8[7]

        def pair(b):
            return PS[:, b:b + 2].rearrange("p b (i n) -> p (b i) n", n=ROWS)

        NORM_BANK = {n: BK8[b][:, 0:ROWS] for n, b in (("na", 4), ("nb", 0), ("nc", 4), ("nd", 4), ("ne", 5), ("nf", 6),
                                                       ("ng", 4), ("nh", 5), ("ni", 4), ("nj", 4))}
        psum_ready = S("psum_ready")
        landed = [S(f"landed{i}") for i in range(RING)]
        hi_done, lo_done = S("hi_done"), S("lo_done")
        ada_used = S("ada_used")

        def raw(s):
            return RAW_OF[("w", s)]

        def split_hi(act, s, j=None, j0=0):
            if s >= NW:
                return
            u = raw(s)
            if j is None:
                act.wait_ge(landed[u % RING], 16 * (u // RING + 1))
                if s >= RING:
                    act.wait_ge(psum_ready, MARK0[s - RING + 1])
            else:
                act.wait_ge(landed[u % RING], (j - j0) * 16 + 16 * (u // RING + 1))
                act.wait_ge(psum_ready, (j - j0) * 12 + MARK0[s - RING + 1])
            nc.scalar.activation(W_HI[s % RING][:], RAW[u % RING][:], ACT.Copy).then_inc(hi_done, 1)

        def split_lo(dve, s, j=None, j0=0):
            if s >= NW:
                return
            u = raw(s)
            dve.wait_ge(hi_done, s + 1 if j is None else (j - j0) * 3 + s + 1)
            nc.vector.tensor_tensor(W_LO[s % RING][:], RAW[u % RING][:], W_HI[s % RING][:].bitcast(F32),
                                    ALU.subtract).then_inc(lo_done, 1)

        def three(acc, w_hi, w_lo, x_hi, x_lo, first, last):
            nc.tensor.matmul(acc, w_hi, x_hi, start=first, stop=False)
            nc.tensor.matmul(acc, w_hi, x_lo, start=False, stop=False)
            return nc.tensor.matmul(acc, w_lo, x_hi, start=False, stop=last)

        block = ctx.enter_context(nc.Block())

        @block.sync
        def _(sp):
            sp.dma_start(XC[:, 0], xin[0]).then_inc(S("x_in"), 16)
            sp.dma_start(PAR[:], params).then_inc(S("par_in"), 16)
            sp.dma_start(CON[:], consts).then_inc(S("con_in"), 16)

            def free_raw(u, j=None, j0=0):
                if u < RING:
                    return
                kind, n = ORDER[u - RING]
                if kind == "w":
                    sp.wait_ge(lo_done, n + 1 if j is None else (j - j0) * 3 + n + 1)
                else:
                    sp.wait_ge(ada_used, n + 1)

            def load(u, j=None, j0=0):
                free_raw(u, j, j0)
                src = stream[u] if j is None else \
                    stream[bass.ds((j - j0) * 3 + u, 1)].rearrange("a p n -> (a p) n")
                sp.dma_start(RAW[u % RING][:], src).then_inc(landed[u % RING], 16)

            u = 0
            while u < NU:
                n = 0
                while u >= RING and u + n < NU and ORDER[u + n][0] == "w" and ORDER[u + n - RING][0] == "w":
                    n += 1
                if n >= 6:
                    with sp.Fori(0, n // 3) as j:
                        for i in range(3):
                            load(u + i, j, 0)
                    u += n // 3 * 3
                else:
                    load(u)
                    u += 1

        @block.gpsimd
        def _(pool):
            pool.dma_start(LW[:], lora).then_inc(S("lw_in"), 16)
            pool.dma_start(MOD[:], bada).then_inc(S("bada_in"), 16)
            pool.wait_ge(S("x_out1"), 8)
            pool.dma_start(XC[:, 1], xin[1]).then_inc(S("ctx_in"), 16)
            pool.dma_start(ROPE[:], rope).then_inc(S("rope_in"), 16)
            pool.wait_ge(psum_ready, MARK0[PHASE["ret_q"]])
            pool.dma_start(IOTA[:], iota).then_inc(S("iota_in"), 16)
            pool.wait_ge(S("pv_done"), RH)
            pool.dma_start(DFT[:], dft).then_inc(S("dft_in"), 16)
            pool.wait_ge(S("final"), 1)
            pool.dma_start(out, NT[:]).then_inc(S("stored"), 16)
            pool.wait_ge(S("stored"), 16)

        @block.tensor
        def _(pe):
            def wait_unit(s, j=None, j0=0):
                pe.wait_ge(lo_done, s + 1 if j is None else (j - j0) * 3 + s + 1)

            def norm(name, half, bank):
                for q in range(2):
                    pe.wait_ge(S("norm_sq"), 2 * NORM[name] + q + 1)
                    for k in range(4 * q, 4 * q + 4):
                        last = nc.tensor.matmul(BK8[bank][:, 0:ROWS], con("ones"), NT[:, k], start=(k == 0), stop=(k == 7))
                last.then_inc(S("norm_ssq"), 1)

            def ffn(f, name, halves, h_names):
                n = halves * ROWS
                s0 = PHASE[name]
                rh = (lambda k: H_HI[:, 0:halves, k])
                rl = (lambda k: H_LO[:, 0:halves, k])

                def up(t, s, j=None, j0=0):
                    wait_unit(s, j, j0)
                    tt = f * FT + t
                    if tt >= 2:
                        pe.wait_ge(S("hid_prod"), tt - 1 if j is None else (j - j0) * 2 + tt - 1)
                    sl = s % RING
                    for w in range(2):
                        acc = BK8[2 * (t % 2) + w][:, 0:n]
                        for k in range(KT):
                            if t == 0 and w == 0 and k % 4 == 0:
                                for h in h_names:
                                    pe.wait_ge(S("norm_h"), 2 * NORM_H[h] + k // 4 + 1)
                            c = (w * KT + k) * P
                            last = three(acc, W_HI[sl][:, c:c + P], W_LO[sl][:, c:c + P], rh(k), rl(k), k == 0, k == KT - 1)
                        last.then_inc(psum_ready, 1)

                def down(i, s, j=None, j0=0):
                    wait_unit(s, j, j0)
                    a = f * FT + 2 * i + 2
                    pe.wait_ge(S("hid_lo"), a if j is None else (j - j0) * 2 + a)
                    sl = s % RING
                    for m in range(KT):
                        d = f * 88 + i * 8 + m
                        if d >= 4:
                            pe.wait_ge(S("down_added"), d - 3 if j is None else (j - j0) * 8 + d - 3)
                        for t in range(2):
                            c = (t * KT + m) * P
                            last = three(BK8[4 + m % 4][:, 0:n], W_HI[sl][:, c:c + P], W_LO[sl][:, c:c + P],
                                         HID_HI[:, t, 0:n], HID_LO[:, t, 0:n], t == 0, t == 1)
                        last.then_inc(psum_ready, 1)

                up(0, s0)
                up(1, s0 + 1)
                with pe.Fori(1, 11) as j:
                    up(2, s0 + 2, j, 1)
                    down(0, s0 + 3, j, 1)
                    up(3, s0 + 4, j, 1)
                down(10, s0 + 32)

            def cols(name, banks, rhs_hi, rhs_lo, n, out_sem, kt=KT, tiles=2, first=None):
                s0 = PHASE[name]
                units = [s for s in range(s0, NW) if s < s0 + {"rwkv_in": 7, "fox_qk": 4, "rwkv_proj": 2, "fox_proj": 2,
                         "gates": 8, "out": 4, "ret_k": 4, "ret_q": 4, "ret_g": 8, "ret_proj": 8, "four_proj": 4,
                         "gates2": 8, "out2": 4}[name]]
                tile = 0
                for s in units:
                    wait_unit(s)
                    for w in range(tiles):
                        if tile >= len(banks):
                            pe.wait_ge(S(out_sem), tile - len(banks) + 1)
                        acc = BK8[banks[tile % len(banks)]][:, 0:n]
                        for k in range(kt):
                            if tile == 0 and first is not None and k % 4 == 0:
                                for sem, v in first:
                                    pe.wait_ge(S(sem), v + k // 4 + 1)
                            c = (w * kt + k) * P
                            sl = s % RING
                            last = three(acc, W_HI[sl][:, c:c + P], W_LO[sl][:, c:c + P], rhs_hi(k), rhs_lo(k),
                                         k == 0, k == kt - 1)
                        last.then_inc(psum_ready, 1)
                        tile += 1

            def rows(name, chunk, n_chunks, rts, banks, out_sem, k0):
                for q in range(n_chunks):
                    s = PHASE[name] + 2 * q
                    for half in range(2):
                        wait_unit(s + half)
                        for r, (h, r0) in enumerate(rts):
                            if half == 0 and (q * len(rts) + r) >= len(banks):
                                pe.wait_ge(S(out_sem), q * len(rts) + r - len(banks) + 1)
                            bank = BK8[banks[(q * len(rts) + r) % len(banks)]]
                            for k4 in range(4):
                                k = half * 4 + k4
                                sl = (s + half) % RING
                                c = k4 * 512
                                st, sp_ = (k == 0), (k == 7)
                                xh, xl = H_HI[:, h, k, r0:r0 + P], H_LO[:, h, k, r0:r0 + P]
                                wh, wl = W_HI[sl][:, c:c + 512], W_LO[sl][:, c:c + 512]
                                nc.tensor.matmul(bank[:], xh, wh, start=st, stop=False)
                                nc.tensor.matmul(bank[:], xh, wl, start=False, stop=False)
                                last = nc.tensor.matmul(bank[:], xl, wh, start=False, stop=sp_)
                            if half == 1 or r == len(rts) - 1:
                                last.then_inc(psum_ready, 1)

            ada_at = [0]

            def ada(n):
                for m in range(ada_at[0], min(ada_at[0] + n, ADA * 4)):
                    d, k, q = m // 4, m % 8, m // 8
                    u = RAW_OF[("a", d)]
                    if m == 0:
                        pe.wait_ge(S("sc_done"), 1)
                    if m % 4 == 0:
                        pe.wait_ge(landed[u % RING], 16 * (u // RING + 1))
                    z = MODR - 2 + MODR * k - 2 * q
                    last = nc.tensor.matmul(ADAP[0:MODR], SCZ[:, z:z + MODR], RAW[u % RING][:, (m % 4) * 512:(m % 4 + 1) * 512],
                                            start=(m == 0), stop=(m == ADA * 4 - 1))
                    if m % 4 == 3:
                        last.then_inc(ada_used, 1)
                ada_at[0] = min(ada_at[0] + n, ADA * 4)

            pe.wait_ge(S("con_in"), 16)
            norm("na", 0, 4)
            ffn(0, "ffn1", 1, ["na"])
            norm("nb", 0, 0)
            ada(4 * ADA_NB)
            xh, xl = (lambda k: H_HI[:, 0, k]), (lambda k: H_LO[:, 0, k])
            cols("rwkv_in", [4, 5, 6, 0], xh, xl, ROWS, "pre_out", first=[("norm_h", 2 * NORM_H["nb"])])
            pe.wait_ge(S("pre_out"), 14)
            cols("fox_qk", [4, 5, 6, 0], xh, xl, ROWS, "fqk_out")
            rows("fox_v", DA, 1, [(0, 0), (0, P)], [1, 2], "fv_out", 0)
            pe.wait_ge(S("fqk_out"), 8)
            pe.wait_ge(S("lw_in"), 16)
            pe.wait_ge(S("lora_act"), 1)
            for i in range(IT):
                last = nc.tensor.matmul(BK8[3 + i // 2][:, (i % 2) * ROWS:(i % 2 + 1) * ROWS], LW[0:32, 0, i * P:(i + 1) * P],
                                        LOR[0:32, 0], start=True, stop=True)
            last.then_inc(S("lora_z"), 1)
            for i in range(IT):
                last = nc.tensor.matmul(BK8[5 + i // 2][:, (i % 2) * ROWS:(i % 2 + 1) * ROWS], LW[32:64, 0, i * P:(i + 1) * P],
                                        LOR[32:64, 0], start=True, stop=True)
            last.then_inc(S("lora_a"), 1)
            pe.wait_ge(S("lora_act"), 2)
            pe.wait_ge(S("fv_out"), 2)
            for i in range(IT):
                last = nc.tensor.matmul(BK8[[0, 1][i // 2]][:, (i % 2) * ROWS:(i % 2 + 1) * ROWS], LW[0:96, 1, i * P:(i + 1) * P],
                                        LOR[0:96, 1], start=True, stop=True)
            last.then_inc(S("lora_g"), 1)
            ada(48)

            def stat(src, banks, name):
                pe.wait_ge(S("stat_in"), STAT[name] + 1)
                for i in range(IT):
                    last = nc.tensor.matmul(BK8[banks][0:NH, 0:ROWS], con("sel")[:, 8 * i:8 * i + 8], src[:, i],
                                            start=(i == 0), stop=(i == IT - 1))
                last.then_inc(S("stat_sum"), 1)

            def spread(src, b0, name):
                pe.wait_ge(S("stat_st"), STAT[name] + 1)
                for i in range(IT):
                    last = nc.tensor.matmul(BK8[b0 + i // 2][:, (i % 2) * ROWS:(i % 2 + 1) * ROWS],
                                            con("bc", NH)[:, i * P:(i + 1) * P], src, start=True, stop=True)
                last.then_inc(S("stat_bc"), 1)

            stat(TMP, 2, "kk")
            pe.wait_ge(S("sg_done"), 1)
            spread(STA[:], 3, "kk")
            stat(TMP, 2, "bon")
            pe.wait_ge(S("aa_done"), 1)
            spread(STA[:], 5, "bon")
            stat(TMP, 2, "fq")
            spread(STA[:], 3, "fq")
            stat(TMP, 2, "fk")
            spread(STA[:], 5, "fk")
            pe.wait_ge(S("lf_cum"), 1)
            pe.wait_ge(S("fq_norm"), 1)
            pe.wait_ge(S("fk_norm"), 1)
            pe.wait_ge(S("gg_done"), 1)
            for h in range(NH):
                if h >= 4 and h % 2 == 0:
                    pe.wait_ge(S("ncb_out"), h // 2 - 1)
                last = nc.tensor.matmul(BK8[[0, 1][(h // 2) % 2]][:, (h % 2) * ROWS:(h % 2 + 1) * ROWS],
                                        con("ident", NH)[:, h:h + 1].to_broadcast([NH, P]), STB[:],
                                        start=True, stop=True)
                if h % 2:
                    last.then_inc(S("ncb"), 1)
            for h in range(NH + 1):
                if h < NH:
                    i, p0 = h // 2, 64 * (h % 2)
                    if h >= 2:
                        pe.wait_ge(S("sco_out"), h - 1)
                    b = BK8[3 + h % 2]
                    nc.tensor.matmul(b[:, 0:P], FQ[p0:p0 + 64, i, 0:P], FK[p0:p0 + 64, i, 0:P], start=True, stop=True)
                    last = nc.tensor.matmul(b[:, P:384], FQ[p0:p0 + 64, i, P:ROWS], FK[p0:p0 + 64, i, :], start=True, stop=True)
                    last.then_inc(S("scores"), 1)
                if h >= 1:
                    g = h - 1
                    i, p0 = g // 2, 64 * (g % 2)
                    pe.wait_ge(S("probs"), g + 1)
                    if g >= 2:
                        pe.wait_ge(S("fo_out"), g - 1)
                    for q in range(3):
                        last = nc.tensor.transpose(BK8[5 + g % 2][:, q * P:(q + 1) * P], SCO[:, g % 2, q * P:(q + 1) * P],
                                                   con("ident"))
                    last.then_inc(S("prt"), 1)
                    pe.wait_ge(S("prt_out"), g + 1)
                    o = BK8[1 + g % 2][p0:p0 + 64, 0:ROWS]
                    v = (lambda kt: FV[:, kt, 64 * g:64 * g + 64])
                    nc.tensor.matmul(o[:, 0:P], v(0), PRT[:, g % 2, 0:P], start=True, stop=True)
                    nc.tensor.matmul(o[:, P:ROWS], v(0), PRT[:, g % 2, P:2 * P], start=True, stop=False)
                    last = nc.tensor.matmul(o[:, P:ROWS], v(1), PRT[:, g % 2, 2 * P:3 * P], start=False, stop=True)
                    last.then_inc(S("fox_o"), 1)
            ada(24)
            pe.wait_ge(S("bk_ready"), 1)
            pe.wait_ge(S("av_ready"), 1)
            pe.wait_ge(S("fo_out"), NH)
            for c in range(NC):
                for n, src in enumerate((BK, AV)):
                    q = 2 * c + n
                    if q >= 2:
                        pe.wait_ge(S("tr_out"), q - 1)
                    for i in range(IT):
                        last = nc.tensor.transpose(BK8[q % 2][:, i * P:(i + 1) * P],
                                                   src[:, i, c].rearrange("p a b -> p (a b)"), con("ident"))
                    last.then_inc(S("tr"), 1)
            for c in range(NC):
                for p in range(2):
                    q = 2 * c + p
                    if q >= 4:
                        pe.wait_ge(S("tt_out"), q - 3)
                    for i in range(IT):
                        last = nc.tensor.matmul(BK8[2 + q % 4][:, i * P:(i + 1) * P],
                                                BK[64 * p:64 * p + 64, i, c].rearrange("p a b -> p (a b)"),
                                                AR[64 * p:64 * p + 64, i, c].rearrange("p a b -> p (a b)"),
                                                start=True, stop=True)
                    last.then_inc(S("tt"), 1)
            pe.wait_ge(S("tr_out"), 8)
            for lev in range(6):
                for g in range(2):
                    if lev == 0:
                        pe.wait_ge(S("tt_out"), 4 * g + 4)
                        if g == 1:
                            pe.wait_ge(S("z_out"), 1)
                    else:
                        pe.wait_ge(S("x_out"), 4 * lev - 4 + 2 * g + 2)
                        pe.wait_ge(S("z_out"), 2 * lev + g)
                    for m in range(16):
                        c, h = 2 * g + m // 8, m % 8
                        rhs = con("ident", CH)[:, 0:CH] if lev == 0 else XM[:, g, m]
                        last = nc.tensor.matmul(BK8[m // 8][0:CH, (m % 8) * CH:(m % 8 + 1) * CH], TT[0:CH, c, h, 0:CH], rhs,
                                                start=True, stop=True)
                    last.then_inc(S("z"), 1)
                    if lev == 0:
                        continue
                    pe.wait_ge(S("z_out"), 2 * lev + g + 1)
                    if lev == 1 and g == 0:
                        pe.wait_ge(S("tt_out"), 8)
                    if not (lev == 1 and g == 0):
                        pe.wait_ge(S("x_out"), 4 * lev + (2 * g if lev < 5 else g))
                    if lev < 5:
                        for m in range(16):
                            last = nc.tensor.matmul(BK8[2 + m // 8][0:CH, (m % 8) * CH:(m % 8 + 1) * CH], XT[:, g, m], ZM[:, g, m],
                                                    start=True, stop=True)
                        last.then_inc(S("xz"), 1)
                    for m in range(16):
                        last = nc.tensor.matmul(BK8[4 + m // 8][0:CH, (m % 8) * CH:(m % 8 + 1) * CH], ZM[:, g, m], XT[:, g, m],
                                                start=True, stop=True)
                    last.then_inc(S("zx"), 1)
            for c in range(NC):
                if c >= 2:
                    pe.wait_ge(S("w_out"), c - 1)
                elif c == 0:
                    pe.wait_ge(S("x_out"), 22)
                for h in range(NH):
                    last = nc.tensor.matmul(BK8[c % 2][0:CH, h * CH:(h + 1) * CH], TT[CH:P, c, h, 0:CH],
                                            AVR[CH:P, c, h * CH:(h + 1) * CH], start=True, stop=True)
                last.then_inc(S("w"), 1)
            for c in range(NC):
                pe.wait_ge(S("w_out"), c + 1)
                if c >= 2:
                    pe.wait_ge(S("u_out"), c - 1)
                for h in range(NH):
                    last = nc.tensor.matmul(BK8[2 + c % 2][0:CH, h * CH:(h + 1) * CH], XT[:, c // 2, (c % 2) * 8 + h],
                                            WM[:, c * NH + h], start=True, stop=True)
                last.then_inc(S("u"), 1)
                if c >= 2:
                    pe.wait_ge(S("gt_out"), c - 1)
                for h in range(NH):
                    i, p0 = h // 2, 64 * (h % 2)
                    last = nc.tensor.matmul(BK8[4 + c % 2][p0:p0 + CH, i * CH:(i + 1) * CH], AVR[0:CH, c, h * CH:(h + 1) * CH],
                                            XT[:, c // 2, (c % 2) * 8 + h], start=True, stop=True)
                last.then_inc(S("gt"), 1)
            pe.wait_ge(S("gt_out"), 4)
            pe.wait_ge(S("u_out"), 4)
            for c in range(NC):
                pe.wait_ge(S("state"), c + 1)
                for p in range(2):
                    for i in range(IT):
                        last = nc.tensor.matmul(BK8[p][0:CH, i * CH:(i + 1) * CH], GT[64 * p:64 * p + 64, c, i],
                                                ST[64 * p:64 * p + 64, c, i], start=True, stop=True)
                last.then_inc(S("sa"), 1)
                pe.wait_ge(S("sa_out"), 2 * c + 2)
                if c < NC - 1:
                    for h in range(NH):
                        i, p0 = h // 2, 64 * (h % 2)
                        last = nc.tensor.matmul(BK8[2][p0:p0 + CH, i * CH:(i + 1) * CH], BKR[:, c, h * CH:(h + 1) * CH],
                                                AVR[:, c, h * CH:(h + 1) * CH], start=True, stop=True)
                    last.then_inc(S("st"), 1)
            for p in range(2):
                for c in range(NC):
                    for i in range(IT):
                        b = BK8[(3 if p == 0 else 5) + i // 2]
                        c0 = (i % 2) * ROWS + c * CH
                        last = nc.tensor.matmul(b[64 * p:64 * p + 64, c0:c0 + CH], ST[64 * p:64 * p + 64, c, i],
                                                AR[64 * p:64 * p + 64, i, c, 1], start=True, stop=True)
            last.then_inc(S("y_s"), 1)
            for c in range(NC):
                for h in range(NH):
                    i, p0 = h // 2, 64 * (h % 2)
                    c0 = (i % 2) * ROWS + c * CH
                    last = nc.tensor.matmul(BK8[i // 2][p0:p0 + CH, c0:c0 + CH], AVR[:, c, h * CH:(h + 1) * CH],
                                            TT[:, c, h, CH:2 * CH], start=True, stop=True)
            last.then_inc(S("y_t"), 1)
            ada(ADA * 4)
            stat(YY, 2, "mu")
            spread(STA[:], 3, "mu")
            stat(YS, 2, "var")
            spread(STA[:], 5, "var")
            pe.wait_ge(S("mod_rows"), 1)
            for j in range(4):
                last = nc.tensor.transpose(ADAP[:, j * MODR:(j + 1) * MODR], MROW[:, j * P:(j + 1) * P], con("ident", MODR)[:, 0:MODR])
            last.then_inc(S("mod_tr"), 1)
            pe.wait_ge(S("ya_split"), 1)
            cols("rwkv_proj", [0, 1, 2, 3], lambda k: YA_HI[:, k], lambda k: YA_LO[:, k], ROWS, "oa_out", kt=4, tiles=4)
            pe.wait_ge(S("yb_split"), 1)
            pe.wait_ge(S("oa_out"), 8)
            cols("fox_proj", [4, 5, 6, 0], lambda k: YB_HI[:, k], lambda k: YB_LO[:, k], ROWS, "ob_out", kt=4, tiles=4)
            pe.wait_ge(S("ob_out"), 8)
            cols("gates", [0, 1, 2, 3], xh, xl, ROWS, "gate_out")
            cols("out", [4, 5, 6, 3], lambda k: M_HI[:, k], lambda k: M_LO[:, k], ROWS, "x_out1", first=[("m_split", 0)])
            norm("nc", 0, 4)
            ffn(1, "ffn2", 1, ["nc"])
            norm("nd", 0, 4)
            norm("ne", 0, 5)
            norm("nf", 1, 6)
            ffn(2, "ffn3", 2, ["ne", "nf"])
            norm("ng", 0, 4)
            norm("nh", 1, 5)
            cols("ret_k", [0, 1, 2, 3], lambda k: H_HI[:, :, k], lambda k: H_LO[:, :, k], 512, "rk_out", first=[("norm_h", 2 * NORM_H["ng"]), ("norm_h", 2 * NORM_H["nh"])])
            pe.wait_ge(S("rk_out"), 8)
            rows("ret_v", 512, 4, [(0, 0), (0, P), (1, 0), (1, P)], [4, 5, 6, 7, 0, 1, 2, 3], "rv_out", 0)
            pe.wait_ge(S("rv_out"), 16)
            cols("ret_q", [0, 1, 2, 3], xh, xl, ROWS, "rq_out")
            pe.wait_ge(S("rq_out"), 8)
            for h in range(RH + 1):
                if h < RH:
                    if h >= 1:
                        pe.wait_ge(S("pt_out"), h)
                    for kt in range(4):
                        half, k0 = kt // 2, (kt % 2) * P
                        for d in range(2):
                            last = nc.tensor.matmul(BK8[kt // 2][:, (kt % 2) * ROWS:(kt % 2 + 1) * ROWS],
                                                    RK[:, half, 2 * h + d, k0:k0 + P], RQ[:, 2 * h + d],
                                                    start=(d == 0), stop=(d == 1))
                    last.then_inc(S("rscores"), 1)
                if h >= 1:
                    pe.wait_ge(S("ro_out"), h)
                    for i in range(4):
                        last = nc.tensor.matmul(BK8[6][:, 0:ROWS], con("ones"), RO[:, 4 * (h - 1) + i], start=(i == 0), stop=(i == 3))
                    last.then_inc(S("mean_sum"), 1)
                if h < RH:
                    pe.wait_ge(S("pt_out"), h + 1)
                    for i in range(4):
                        for kt in range(4):
                            last = nc.tensor.matmul(BK8[2 + i // 2][:, (i % 2) * ROWS:(i % 2 + 1) * ROWS],
                                                    RV[:, kt, h * RDV + i * P:h * RDV + (i + 1) * P], PT[:, kt],
                                                    start=(kt == 0), stop=(kt == 3))
                    last.then_inc(S("pv_done"), 1)
                if h >= 1:
                    pe.wait_ge(S("rvar_in"), h)
                    for i in range(4):
                        last = nc.tensor.matmul(BK8[7][:, 0:ROWS], con("ones"), SQ[:, i], start=(i == 0), stop=(i == 3))
                    last.then_inc(S("rvar_sum"), 1)
            pe.wait_ge(S("rn_done"), RH)
            cols("ret_g", [4, 5, 6, 0], xh, xl, ROWS, "rg_out")
            pe.wait_ge(S("rg_out"), 16)
            rows("four_in", 512, 2, [(0, 0), (0, P)], [0, 1, 2, 3], "fx_out", 0)
            pe.wait_ge(S("dft_in"), 16)
            pe.wait_ge(S("fx_out"), 4)
            for g in range(4):
                for t in range(2):
                    q = 2 * g + t
                    if q >= 2:
                        pe.wait_ge(S("zz_out"), q - 1)
                    for k in range(2):
                        last = nc.tensor.matmul(BK8[4 + q % 2][:], FX[:, k, q * P:(q + 1) * P], DFT[:, k], start=(k == 0), stop=(k == 1))
                    last.then_inc(S("zz"), 1)
                pe.wait_ge(S("zz_out"), 2 * g + 2)
                for t in range(2):
                    q = 2 * g + t
                    if q >= 2:
                        pe.wait_ge(S("xm_out"), q - 1)
                    n = 0
                    for part in range(2):
                        for k in range(2):
                            last = nc.tensor.matmul(BK8[q % 2][:, 0:ROWS], DFT[:, k, part * 256 + t * P:part * 256 + (t + 1) * P],
                                                    ZZ[:, g % 2, k, part * ROWS:(part + 1) * ROWS], start=(n == 0), stop=(n == 3))
                            n += 1
                    last.then_inc(S("xm"), 1)
            pe.wait_ge(S("r_split"), 16)
            cols("ret_proj", [2, 3, 6, 7], lambda k: R_HI[:, k], lambda k: R_LO[:, k], ROWS, "or_out", kt=16, tiles=1)
            pe.wait_ge(S("xm_out"), 8)
            pe.wait_ge(S("or_out"), 8)
            cols("four_proj", [4, 5, 0, 1], lambda k: X_HI[:, k], lambda k: X_LO[:, k], ROWS, "of_out")
            cols("gates2", [2, 3, 6, 7], xh, xl, ROWS, "gate2_out")
            pe.wait_ge(S("of_out"), 8)
            cols("out2", [4, 5, 0, 1], lambda k: M2_HI[:, k], lambda k: M2_LO[:, k], ROWS, "x_out2", first=[("m2_split", 0)])
            norm("ni", 0, 4)
            ffn(3, "ffn4", 1, ["ni"])
            norm("nj", 0, 4)

        @block.scalar
        def _(act):
            A = nc.scalar.activation

            def norm(name, half, ready, out=None, shift=None):
                for sem, v in ready:
                    act.wait_ge(S(sem), v)
                for q in range(2):
                    A(NT[:, 4 * q:4 * q + 4], XC[:, half, 4 * q:4 * q + 4], ACT.Square).then_inc(S("norm_sq"), 1)
                act.wait_ge(S("norm_ssq"), NORM[name] + 1)
                A(STD[:], NORM_BANK[name], ACT.Sqrt, scale=1.0 / DM, bias=par("epsr")).then_inc(S("norm_std"), 1)
                if out is not None:
                    return
                for q in range(2):
                    act.wait_ge(S("norm_t"), 2 * NORM_H[name] + q + 1)
                    if shift is not None:
                        for k in range(4 * q, 4 * q + 4):
                            last = A(NT[:, k], NT[:, k], ACT.Identity, bias=MOD[:, shift[0] + k, shift[1]:shift[1] + 1])
                        last.then_inc(S("norm_m"), 1)
                        act.wait_ge(S("norm_m"), 2 * (NORM_H[name] - NORM_H["ne"]) + q + 1)
                    A(H_HI[:, half, 4 * q:4 * q + 4], NT[:, 4 * q:4 * q + 4], ACT.Copy).then_inc(S("norm_hi"), 1)

            def ffn(f, name, halves):
                n = halves * ROWS
                s0 = PHASE[name]

                def silu(t, mark, j=None, j0=0):
                    tt = f * FT + t
                    if tt >= 2:
                        act.wait_ge(S("hid_prod"), tt - 1 if j is None else (j - j0) * 2 + tt - 1)
                    act.wait_ge(psum_ready, mark if j is None else (j - j0) * 12 + mark)
                    A(SILU[:, t % 2, 0:n], BK8[2 * (t % 2)][:, 0:n], ACT.Silu).then_inc(S("silu"), 1)

                m0 = MARK0[s0]
                split_hi(act, s0 + 2)
                silu(0, m0 + 1)
                split_hi(act, s0 + 3)
                silu(1, m0 + 3)

                def body(j, j0, i):
                    s, m = s0 + 2 + 3 * (i - 1), m0 + 4 + 12 * (i - 1)
                    split_hi(act, s + 2, j, j0)
                    split_hi(act, s + 3, j, j0)
                    silu(2 * i, m + 1, j, j0)
                    split_hi(act, s + 4, j, j0)
                    silu(2 * i + 1, m + 11, j, j0)

                with act.Fori(1, 10) as j:
                    body(j, 1, 1)
                body(None, 0, 10)
                split_hi(act, s0 + 34)

            act.wait_ge(S("par_in"), 16)
            act.wait_ge(S("scz_zero"), 1)
            A(SCZ[:, MODR - 2:].rearrange("p (k n) -> p k n", n=MODR)[:, :, 0:2],
              par("c", 0, 16).rearrange("p (k n) -> p k n", n=2), ACT.Silu).then_inc(S("sc_done"), 1)
            split_hi(act, 0)
            split_hi(act, 1)
            norm("na", 0, [("x_in", 16)])
            ffn(0, "ffn1", 1)
            norm("nb", 0, [("down_added", 88)])
            s0 = PHASE["rwkv_in"]
            m0 = MARK0[s0]
            for t in range(14):
                if t % 2 == 0:
                    split_hi(act, s0 + t // 2 + 2)
                act.wait_ge(psum_ready, m0 + t + 1)
                A(PRE[:, t, 1:ROWS + 1], BK8[[4, 5, 6, 0][t % 4]][:, 0:ROWS], ACT.Copy).then_inc(S("pre_out"), 1)
            s0 = PHASE["fox_qk"]
            m0 = MARK0[s0]
            for t in range(8):
                if t % 2 == 0:
                    split_hi(act, s0 + t // 2 + 2)
                act.wait_ge(psum_ready, m0 + t + 1)
                A((FQ, FK)[t // 4][:, t % 4], BK8[[4, 5, 6, 0][t % 4]][:, 0:ROWS], ACT.Copy).then_inc(S("fqk_out"), 1)
            s0 = PHASE["fox_v"]
            m0 = MARK0[s0]
            split_hi(act, s0 + 2)
            split_hi(act, s0 + 3)
            for r in range(2):
                act.wait_ge(psum_ready, m0 + 2 + r)
                A(FV[:, r], BK8[1 + r], ACT.Copy).then_inc(S("fv_out"), 1)
            act.wait_ge(S("lor"), 1)
            A(LOR[0:32, 0], LOR[0:32, 0], ACT.Tanh).then_inc(S("lora_act"), 1)
            A(LOR[0:96, 1], LOR[0:96, 1], ACT.Sigmoid).then_inc(S("lora_act"), 1)
            act.wait_ge(S("lora_z"), 1)
            for i in range(IT):
                last = A(SG[:, i], pair(3)[:, i], ACT.Sigmoid, bias=par("w0", i))
            last.then_inc(S("sg_done"), 1)
            act.wait_ge(S("lora_a"), 1)
            for i in range(IT):
                last = A(AA[:, i], pair(5)[:, i], ACT.Sigmoid, bias=par("a0", i))
            last.then_inc(S("aa_done"), 1)
            act.wait_ge(S("lora_g"), 1)
            A(GG[:], pair(0), ACT.Copy).then_inc(S("gg_done"), 1)
            act.wait_ge(S("kk_max"), 1)
            A(STA[:], STA[:], ACT.Sqrt).then_inc(S("kk_rt"), 1)
            act.wait_ge(S("stat_sum"), STAT["fq"] + 1)
            act.wait_ge(S("stat_bc"), STAT["bon"] + 1)
            A(STA[:], BK8[2][0:NH, 0:ROWS], ACT.Sqrt, scale=1.0, bias=par("epsq", 0, 1, NH)).then_inc(S("fq_rt"), 1)
            act.wait_ge(S("stat_sum"), STAT["fk"] + 1)
            act.wait_ge(S("stat_bc"), STAT["fq"] + 1)
            A(STA[:], BK8[2][0:NH, 0:ROWS], ACT.Sqrt, scale=1.0 / 64, bias=par("epsr", 0, 1, NH)).then_inc(S("fk_rt"), 1)
            act.wait_ge(S("f_x"), 1)
            A(F3[:], F1[:], ACT.Abs).then_inc(S("f_act"), 1)
            act.wait_ge(S("f_act"), 1)
            A(F3[:], F3[:], ACT.Exp, scale=-1.0).then_inc(S("f_act"), 1)
            act.wait_ge(S("f_act"), 2)
            A(F3[:], F3[:], ACT.Ln, bias=par("one", 0, 1, NH)).then_inc(S("f_act"), 1)
            act.wait_ge(S("ls_done"), 2)
            A(PC[:], LS[:], ACT.Exp, scale=-DECAY).then_inc(S("ex"), 1)
            act.wait_ge(S("ex"), 1)
            A(LS[:], LS[:], ACT.Exp, scale=DECAY).then_inc(S("ex"), 1)
            A(TMP[:], TMP[:], ACT.Exp, scale=-DECAY).then_inc(S("ex"), 1)
            act.wait_ge(S("ar_a"), 1)
            A(AV[:, :, :, 0], AR[:, :, :, 0], ACT.Copy)
            A(AV[:, :, :, 1], RKV[:, 2].rearrange("p i (c t) -> p i c t", c=NC), ACT.Copy).then_inc(S("av_ready"), 1)
            for q in range(4):
                act.wait_ge(S("ncb"), q + 1)
                A(NCB[:, 2 * q:2 * q + 2], BK8[q % 2].rearrange("p (h n) -> p h n", h=2), ACT.Copy).then_inc(S("ncb_out"), 1)
            for h in range(NH + 2):
                if h < NH:
                    act.wait_ge(S("fmax"), h + 1)
                    for r, (a, b) in enumerate(((0, P), (P, 384))):
                        last = A(SCO[:, h % 2, a:b], SCO[:, h % 2, a:b], ACT.Exp, bias=FST[:, h % 2, r:r + 1],
                                 accum_out=FST[:, h % 2, 2 + r:3 + r])
                    last.then_inc(S("fexp"), 1)
                if 1 <= h <= NH:
                    act.wait_ge(S("prt"), h)
                    if h >= 3:
                        act.wait_ge(S("fox_o"), h - 2)
                    A(PRT[:, (h - 1) % 2], BK8[5 + (h - 1) % 2][:, 0:384], ACT.Copy).then_inc(S("prt_out"), 1)
                if h >= 2:
                    g = h - 2
                    p0 = 64 * (g % 2)
                    act.wait_ge(S("fox_o"), g + 1)
                    if g == 0:
                        act.wait_ge(S("bk_ready"), 1)
                    A(YB[p0:p0 + 64, g // 2], BK8[1 + g % 2][p0:p0 + 64, 0:ROWS], ACT.Copy).then_inc(S("fo_out"), 1)
            for q in range(8):
                act.wait_ge(S("tr"), q + 1)
                A((BKR, AVR)[q % 2][:, q // 2], BK8[q % 2], ACT.Copy).then_inc(S("tr_out"), 1)
            for c in range(NC):
                act.wait_ge(S("w"), c + 1)
                A(WM[:, c * NH:(c + 1) * NH], BK8[c % 2][0:CH].rearrange("p (h n) -> p h n", h=NH), ACT.Copy).then_inc(S("w_out"), 1)
            for c in range(NC):
                act.wait_ge(S("u"), c + 1)
                A(UM[:, c], BK8[2 + c % 2][0:CH].rearrange("p (h n) -> p h n", h=NH), ACT.Copy).then_inc(S("u_out"), 1)
            act.wait_ge(S("y_s"), 1)
            A(YY[0:CH], pair(3)[0:CH], ACT.Copy)
            A(YY[CH:P], pair(5)[CH:P], ACT.Copy).then_inc(S("yy_s"), 1)
            act.wait_ge(ada_used, ADA)
            A(MROW[:], ADAP[0:MODR], ACT.Copy).then_inc(S("mod_rows"), 1)
            act.wait_ge(S("stat_sum"), STAT["var"] + 1)
            act.wait_ge(S("stat_bc"), STAT["mu"] + 1)
            A(STA[:], BK8[2][0:NH, 0:ROWS], ACT.Sqrt, scale=1.0 / 64, bias=par("epsl", 0, 1, NH)).then_inc(S("var_rt"), 1)
            for name, dst, banks, sem in (("rwkv_proj", OA, [0, 1, 2, 3], "oa_out"), ("fox_proj", OB, [4, 5, 6, 0], "ob_out")):
                s0 = PHASE[name]
                m0 = MARK0[s0]
                for t in range(8):
                    if t % 4 == 0:
                        split_hi(act, s0 + t // 4 + 2)
                    act.wait_ge(psum_ready, m0 + t + 1)
                    A(dst[:, t], BK8[banks[t % 4]][:, 0:ROWS], ACT.Copy).then_inc(S(sem), 1)

            def gates(name, dst, banks, out_sem, used_sem):
                s0 = PHASE[name]
                m0 = MARK0[s0]
                for t in range(16):
                    if t % 2 == 0:
                        split_hi(act, s0 + t // 2 + 2)
                    if t >= 4:
                        act.wait_ge(S(used_sem), (t - 4) // 2 + 1)
                    act.wait_ge(psum_ready, m0 + t + 1)
                    A(dst[:, t % 4], BK8[banks[t % 4]][:, 0:ROWS], ACT.Sigmoid).then_inc(S(out_sem), 1)

            gates("gates", SGA, [0, 1, 2, 3], "gate_out", "gate_used")
            for s in range(PHASE["out"], PHASE["out"] + 4):
                split_hi(act, s + 2)
            norm("nc", 0, [("x_out1", 8)])
            ffn(1, "ffn2", 1)
            A(LG[:, 0], par("dec", 0, 8), ACT.Abs).then_inc(S("dec_a"), 1)
            act.wait_ge(S("dec_a"), 1)
            A(LG[:, 0], LG[:, 0], ACT.Exp, scale=-1.0).then_inc(S("dec_a"), 1)
            norm("nd", 0, [("down_added", 176)], out=1)
            norm("ne", 0, [("nd_x", 1)], shift=(0, 0))
            norm("nf", 1, [("ctx_in", 16), ("norm_h", 2 * NORM_H["ne"] + 2)], shift=(0, 1))
            ffn(2, "ffn3", 2)
            norm("ng", 0, [("down_added", 264)], shift=(24, 0))
            norm("nh", 1, [("norm_h", 2 * NORM_H["ng"] + 2)], shift=(24, 1))
            s0 = PHASE["ret_k"]
            for h in range(RH):
                split_hi(act, s0 + h + 2)
                for w in range(2):
                    act.wait_ge(S("rk_x"), 2 * h + w + 1)
                    A(RK[:, 1, 2 * h + w], BK8[(2 * h + w) % 4][:, ROWS:512], ACT.Copy).then_inc(S("rk_out"), 1)
            s0 = PHASE["ret_v"]
            for q in range(4):
                split_hi(act, s0 + 2 * q + 2)
                split_hi(act, s0 + 2 * q + 3)
                for r in range(4):
                    act.wait_ge(psum_ready, MARK0[s0 + 2 * q + 1] + r + 1)
                    A(RV[:, r, 512 * q:512 * (q + 1)], BK8[[4, 5, 6, 7, 0, 1, 2, 3][(4 * q + r) % 8]], ACT.Copy).then_inc(S("rv_out"), 1)
            s0 = PHASE["ret_q"]
            for s in range(s0, s0 + 4):
                split_hi(act, s + 2)
            for h in range(RH + 1):
                if h < RH:
                    act.wait_ge(S("d_arg"), h + 1)
                    A(DD[:, 0:2], DD[:, 0:2], ACT.Exp)
                    for kt in range(2):
                        A(DD[:, 2 + kt], IOTA[:], ACT.Exp, scale=LG[:, 4, h:h + 1], bias=LB[:, h, kt:kt + 1])
                        last = A(EB[:, kt], IOTA[:], ACT.Exp, scale=LG[:, 3, 4 + h:5 + h], bias=LB[:, h, 2 + kt:3 + kt])
                    last.then_inc(S("d_exp"), 1)
                if h >= 1:
                    act.wait_ge(S("ro_c"), h)
                    A(SQ[:], RO[:, 4 * (h - 1):4 * h], ACT.Square).then_inc(S("rvar_in"), 1)
                if h < RH:
                    act.wait_ge(S("pv_done"), h + 1)
                    A(RO[:, 4 * h:4 * h + 4], pair(2), ACT.Copy).then_inc(S("ro_out"), 1)
                if h >= 1:
                    act.wait_ge(S("rvar_sum"), h)
                    if h >= 2:
                        act.wait_ge(S("rn_rec"), h - 1)
                    A(RST[:, 0], BK8[7][:, 0:ROWS], ACT.Sqrt, scale=1.0 / RDV, bias=par("epsr")).then_inc(S("rvar_rt"), 1)
            s0 = PHASE["ret_g"]
            m0 = MARK0[s0]
            for t in range(16):
                if t % 2 == 0:
                    split_hi(act, s0 + t // 2 + 2)
                if t >= 2:
                    act.wait_ge(S("rg_used"), t - 1)
                act.wait_ge(psum_ready, m0 + t + 1)
                A(SGG[:, t % 2], BK8[[4, 5, 6, 0][t % 4]][:, 0:ROWS], ACT.Silu).then_inc(S("rg_out"), 1)
            s0 = PHASE["four_in"]
            for q in range(2):
                split_hi(act, s0 + 2 * q + 2)
                split_hi(act, s0 + 2 * q + 3)
                for r in range(2):
                    act.wait_ge(psum_ready, MARK0[s0 + 2 * q + 1] + r + 1)
                    A(FX[:, r, 512 * q:512 * (q + 1)], BK8[2 * q + r], ACT.Copy).then_inc(S("fx_out"), 1)
            for q in range(8):
                act.wait_ge(S("zz"), q + 1)
                if q >= 4:
                    act.wait_ge(S("xm"), 2 * (q // 2) - 2)
                A(ZZ[:, (q // 2) % 2, q % 2, 0:ROWS], BK8[4 + q % 2][:, 0:ROWS], ACT.Copy)
                A(ZZ[:, (q // 2) % 2, q % 2, ROWS:512], BK8[4 + q % 2][:, ROWS:512], ACT.Copy, scale=-1.0).then_inc(S("zz_out"), 1)
            s0 = PHASE["ret_proj"]
            for t in range(8):
                split_hi(act, s0 + t + 2)
                act.wait_ge(psum_ready, MARK0[s0] + t + 1)
                A(OR[:, t], BK8[[2, 3, 6, 7][t % 4]][:, 0:ROWS], ACT.Copy).then_inc(S("or_out"), 1)
            s0 = PHASE["four_proj"]
            for t in range(8):
                if t % 2 == 0:
                    split_hi(act, s0 + t // 2 + 2)
                act.wait_ge(psum_ready, MARK0[s0] + t + 1)
                A(OF[:, t], BK8[[4, 5, 0, 1][t % 4]][:, 0:ROWS], ACT.Copy).then_inc(S("of_out"), 1)
            gates("gates2", SG2, [2, 3, 6, 7], "gate2_out", "gate2_used")
            for s in range(PHASE["out2"], PHASE["out2"] + 4):
                split_hi(act, s + 2)
            norm("ni", 0, [("x_out2", 8)], shift=(48, 0))
            ffn(3, "ffn4", 1)
            norm("nj", 0, [("down_added", 352)], out=1)

        @block.vector
        def _(dve):
            V = nc.vector
            count = [0]

            def link(ins):
                count[0] += 1
                ins.then_inc(S("dve_link"), 1)
                dve.wait_ge(S("dve_link"), count[0])

            def norm(name, half, gain, out=None):
                dve.wait_ge(S("norm_std"), NORM[name] + 1)
                link(V.reciprocal(RSTD[:], STD[:]))
                for q in range(2):
                    for k in range(4 * q, 4 * q + 4):
                        dst = NT[:, k] if out is None or out is NT else out[:, k]
                        last = V.scalar_tensor_tensor(out=dst, in0=XC[:, half, k], scalar=gain(k), in1=RSTD[:],
                                                      op0=ALU.mult, op1=ALU.mult)
                    if out is None:
                        last.then_inc(S("norm_t"), 1)
                if out is not None:
                    last.then_inc(S("final" if out is NT else f"{name}_x"), 1)
                    return
                for q in range(2):
                    dve.wait_ge(S("norm_hi"), 2 * NORM_H[name] + q + 1)
                    V.tensor_tensor(H_LO[:, half, 4 * q:4 * q + 4], NT[:, 4 * q:4 * q + 4],
                                    H_HI[:, half, 4 * q:4 * q + 4].bitcast(F32), ALU.subtract).then_inc(S("norm_h"), 1)

            def ffn(f, name, halves, gate):
                n = halves * ROWS
                s0 = PHASE[name]
                m0 = MARK0[s0]

                def hidden(t, mark, dmark, j=None, j0=0):
                    tt = f * FT + t
                    x = (lambda a, m: a if j is None else (j - j0) * m + a)
                    dve.wait_ge(S("silu"), x(tt + 1, 2))
                    dve.wait_ge(psum_ready, x(mark, 12))
                    V.tensor_tensor(PROD[:, t % 2, 0:n], SILU[:, t % 2, 0:n], BK8[2 * (t % 2) + 1][:, 0:n],
                                    ALU.mult).then_inc(S("hid_prod"), 1)
                    dve.wait_ge(S("hid_prod"), x(tt + 1, 2))
                    if dmark is not None:
                        dve.wait_ge(psum_ready, x(dmark, 12))
                    V.tensor_copy(HID_HI[:, t % 2, 0:n], PROD[:, t % 2, 0:n]).then_inc(S("hid_hi"), 1)
                    dve.wait_ge(S("hid_hi"), x(tt + 1, 2))
                    V.tensor_tensor(HID_LO[:, t % 2, 0:n], PROD[:, t % 2, 0:n], HID_HI[:, t % 2, 0:n].bitcast(F32),
                                    ALU.subtract).then_inc(S("hid_lo"), 1)

                def add(i, ms, mark, j=None, j0=0):
                    for m in ms:
                        d = f * 88 + 8 * i + m
                        if m == 0 and d > 0:
                            dve.wait_ge(S("down_added"), d if j is None else (j - j0) * 8 + d)
                        dve.wait_ge(psum_ready, mark + m + 1 if j is None else (j - j0) * 12 + mark + m + 1)
                        for h in range(halves):
                            last = V.scalar_tensor_tensor(out=XC[:, h, m], in0=BK8[4 + m % 4][:, h * ROWS:(h + 1) * ROWS],
                                                          scalar=gate(h, m), in1=XC[:, h, m], op0=ALU.mult, op1=ALU.add)
                        last.then_inc(S("down_added"), 1)

                split_lo(dve, s0 + 2)
                hidden(0, m0 + 2, m0 if f else None)
                split_lo(dve, s0 + 3)

                def body(j, j0, i):
                    s, m = s0 + 2 + 3 * (i - 1), m0 + 4 + 12 * (i - 1)
                    hidden(2 * i - 1, m, m - 2, j, j0)
                    split_lo(dve, s + 2, j, j0)
                    add(i - 1, range(0, 4), m + 2, j, j0)
                    split_lo(dve, s + 3, j, j0)
                    add(i - 1, range(4, 8), m + 2, j, j0)
                    hidden(2 * i, m + 2, m + 10, j, j0)
                    split_lo(dve, s + 4, j, j0)

                with dve.Fori(1, 10) as j:
                    body(j, 1, 1)
                body(None, 0, 10)
                hidden(21, m0 + 124, m0 + 122)
                split_lo(dve, s0 + 34)
                add(10, range(8), m0 + 124)

            half_ = (lambda h, m: 0.5)
            V.memset(SCZ[:], 0.0).then_inc(S("scz_zero"), 1)
            V.memset(PRE[:, :, 0:1], 0.0)
            split_lo(dve, 0)
            split_lo(dve, 1)
            dve.wait_ge(S("par_in"), 16)
            dve.wait_ge(S("con_in"), 16)
            norm("na", 0, lambda k: par("n1", k))
            ffn(0, "ffn1", 1, half_)
            norm("nb", 0, lambda k: par("nm", k))

            def shift(dst, t0, nt):
                cur, prev = PRE[:, t0:t0 + nt, 1:ROWS + 1], PRE[:, t0:t0 + nt, 0:ROWS]
                link(V.tensor_tensor(TMP[:, 0:nt], prev, cur, ALU.subtract))
                for t in range(nt):
                    last = V.scalar_tensor_tensor(out=dst[:, t], in0=TMP[:, t], scalar=par("mu", t0 + t), in1=cur[:, t],
                                                  op0=ALU.mult, op1=ALU.add)
                if dst is LOR:
                    last.then_inc(S("lor"), 1)
                    dve.wait_ge(S("lor"), 1)
                else:
                    link(last)

            s0 = PHASE["rwkv_in"]
            for u in range(7):
                split_lo(dve, s0 + u + 2)
                if u in (1, 3, 5, 6):
                    dve.wait_ge(S("pre_out"), 2 * u + 2)
                    if u < 6:
                        shift(RKV[:, u // 2], 2 * u - 2, 4)
                    else:
                        shift(LOR, 12, 2)
            R_, K_, V_ = RKV[:, 0], RKV[:, 1], RKV[:, 2]
            s0 = PHASE["fox_qk"]
            for u in range(4):
                split_lo(dve, s0 + u + 2)
                if u == 1:
                    for i in range(IT):
                        last = V.tensor_scalar(KK[:, i], K_[:, i], par("kk", i), None, ALU.mult)
                    link(last)
                    V.tensor_tensor(TMP[:], KK[:], KK[:], ALU.mult).then_inc(S("stat_in"), 1)
            s0 = PHASE["fox_v"]
            split_lo(dve, s0 + 2)
            split_lo(dve, s0 + 3)
            dve.wait_ge(S("stat_sum"), STAT["kk"] + 1)
            V.tensor_scalar(STA[:], BK8[2][0:NH, 0:ROWS], 1e-24, None, ALU.max).then_inc(S("kk_max"), 1)
            dve.wait_ge(S("aa_done"), 1)
            for i in range(IT):
                last = V.tensor_scalar(TMP[:, i], AA[:, i], 1.0, par("ka", i), ALU.subtract, ALU.mult)
            link(last)
            link(V.scalar_tensor_tensor(out=K_, in0=TMP[:], scalar=1.0, in1=K_, op0=ALU.add, op1=ALU.mult))
            for i in range(IT):
                last = V.scalar_tensor_tensor(out=TMP[:, i], in0=R_[:, i], scalar=par("rk", i), in1=K_[:, i],
                                              op0=ALU.mult, op1=ALU.mult)
            last.then_inc(S("stat_in"), 1)
            dve.wait_ge(S("kk_rt"), 1)
            V.reciprocal(STA[:], STA[:]).then_inc(S("stat_st"), 1)
            dve.wait_ge(S("stat_bc"), STAT["kk"] + 1)
            link(V.tensor_tensor(KK[:], KK[:], pair(3), ALU.mult))
            dve.wait_ge(S("stat_sum"), STAT["bon"] + 1)
            V.tensor_copy(STA[:], BK8[2][0:NH, 0:ROWS]).then_inc(S("stat_st"), 1)
            dve.wait_ge(S("gg_done"), 1)
            dve.wait_ge(S("stat_bc"), STAT["bon"] + 1)
            link(V.tensor_tensor(BO[:], V_, pair(5), ALU.mult))
            dve.wait_ge(S("fqk_out"), 8)
            for name, X, g in (("fq", FQ, "qn"), ("fk", FK, "kn")):
                V.tensor_tensor(TMP[:], X[:], X[:], ALU.mult).then_inc(S("stat_in"), 1)
                dve.wait_ge(S(f"{name}_rt"), 1)
                V.reciprocal(STA[:], STA[:]).then_inc(S("stat_st"), 1)
                dve.wait_ge(S("stat_bc"), STAT[name] + 1)
                V.scalar_tensor_tensor(out=X[:], in0=pair(3 if name == "fq" else 5), scalar=par(g), in1=X[:],
                                       op0=ALU.mult, op1=ALU.mult).then_inc(S(f"{name}_norm"), 1)
            dve.wait_ge(S("lora_g"), 1)
            link(V.tensor_scalar(F1[:], LOR[96:96 + NH, 1], par("fb")[96:96 + NH], None, ALU.add))
            V.tensor_scalar(F2[:], F1[:], 0.0, None, ALU.min).then_inc(S("f_x"), 1)
            link(V.memset(F4[:], 1.0))
            dve.wait_ge(S("sg_done"), 1)
            for i in range(IT):
                for c in range(0, ROWS, CH):
                    last = V.tensor_tensor_scan(LS[:, i, c:c + CH], con("ones")[:, 0:CH], SG[:, i, c:c + CH], 0.0, ALU.mult, ALU.add)
            last.then_inc(S("ls_done"), 1)
            dve.wait_ge(S("ls_done"), 1)
            V.tensor_tensor(TMP[:], LS[:], SG[:], ALU.subtract).then_inc(S("ls_done"), 1)
            dve.wait_ge(S("f_act"), 3)
            link(V.tensor_tensor(F3[:], F3[:], F2[:], ALU.subtract))
            V.tensor_tensor_scan(STB[:], F4[:], F3[:], 0.0, ALU.mult, ALU.add).then_inc(S("lf_cum"), 1)
            by_chunk = (lambda x: x.rearrange("p i (c t) -> p i c t", c=NC))
            dve.wait_ge(S("ex"), 3)
            V.scalar_tensor_tensor(out=AR[:, :, :, 0], in0=by_chunk(KK[:]), scalar=-1.0, in1=by_chunk(TMP[:]),
                                   op0=ALU.mult, op1=ALU.mult).then_inc(S("ar_a"), 1)
            V.tensor_tensor(AR[:, :, :, 1], by_chunk(R_), by_chunk(PC[:]), ALU.mult)
            V.tensor_tensor(BK[:, :, :, 1], by_chunk(K_), by_chunk(LS[:]), ALU.mult)
            link(V.tensor_tensor(KK[:], KK[:], AA[:], ALU.mult))
            V.tensor_tensor(BK[:, :, :, 0], by_chunk(KK[:]), by_chunk(LS[:]), ALU.mult).then_inc(S("bk_ready"), 1)
            diag = (lambda h: SCO[:, h % 2].rearrange("p (b n) -> p b n", n=P)[:, 0:3:2])
            for h in range(NH + 1):
                if h < NH:
                    dve.wait_ge(S("scores"), h + 1)
                    if h < 8 and h % 2 == 0:
                        dve.wait_ge(S("ncb_out"), h // 2 + 1)
                    if h >= 2:
                        dve.wait_ge(S("prt"), h - 1)
                    b = BK8[3 + h % 2]
                    V.tensor_tensor(SCO[:, h % 2, 0:P], b[:, 0:P], NCB[:, h, 0:P], ALU.add)
                    V.tensor_tensor(SCO[:, h % 2, P:384], b[:, P:384], NCB[:, h], ALU.add).then_inc(S("sco_out"), 1)
                    dve.wait_ge(S("sco_out"), h + 1)
                    link(V.tensor_tensor(diag(h), diag(h), con("causal").unsqueeze(1).to_broadcast([P, 2, P]), ALU.add))
                    V.tensor_reduce(FST[:, h % 2, 0:1], SCO[:, h % 2, 0:P], AX_X, ALU.max, negate=True)
                    V.tensor_reduce(FST[:, h % 2, 1:2], SCO[:, h % 2, P:384], AX_X, ALU.max, negate=True).then_inc(S("fmax"), 1)
                if h >= 1:
                    g = (h - 1) % 2
                    dve.wait_ge(S("fexp"), h)
                    link(V.reciprocal(FST[:, g, 4:6], FST[:, g, 2:4]))
                    V.tensor_scalar(SCO[:, g, 0:P], SCO[:, g, 0:P], FST[:, g, 4:5], None, ALU.mult)
                    V.tensor_scalar(SCO[:, g, P:384], SCO[:, g, P:384], FST[:, g, 5:6], None, ALU.mult).then_inc(S("probs"), 1)
            for q in range(8):
                c, p = q // 2, q % 2
                dve.wait_ge(S("tt"), q + 1)
                V.tensor_tensor(TT[:, c].rearrange("p (i q) n -> p i q n", q=2)[:, :, p],
                                BK8[2 + q % 4].rearrange("p (i n) -> p i n", n=P),
                                con("tmask").unsqueeze(1).to_broadcast([P, IT, P]), ALU.mult).then_inc(S("tt_out"), 1)
            dve.wait_ge(S("tt_out"), 8)
            eye = con("ident", CH)[:, 0:CH].unsqueeze(1).to_broadcast([CH, 16, CH])
            sixteen = (lambda b: PS[0:CH, b:b + 2].rearrange("p b (m n) -> p (b m) n", n=CH))
            for lev in range(6):
                mask = con("lmask", CH)[:, lev * CH:(lev + 1) * CH].unsqueeze(1).to_broadcast([CH, 16, CH])
                for g in range(2):
                    dve.wait_ge(S("z"), 2 * lev + g + 1)
                    dst = XM if lev == 0 else ZM
                    V.tensor_tensor(dst[:, g], sixteen(0), mask, ALU.mult).then_inc(S("z_out"), 1)
                    if lev == 0:
                        dve.wait_ge(S("z_out"), g + 1)
                        V.tensor_tensor(XM[:, g], XM[:, g], eye, ALU.add).then_inc(S("x_out"), 1)
                        link(V.tensor_tensor(XT[:, g].rearrange("p (c h) n -> p c h n", c=2), TT[0:CH, 2 * g:2 * g + 2, :, 0:CH],
                                             con("l0t", CH).unsqueeze(1).unsqueeze(1).to_broadcast([CH, 2, 8, CH]), ALU.mult))
                        V.tensor_tensor(XT[:, g], XT[:, g], eye, ALU.add).then_inc(S("x_out"), 1)
                        continue
                    n = 2 * (lev - 1) + g
                    if lev < 5:
                        dve.wait_ge(S("xz"), n + 1)
                        dve.wait_ge(S("x_out"), 2 * n + 2)
                        V.tensor_tensor(XM[:, g], XM[:, g], sixteen(2), ALU.add).then_inc(S("x_out"), 1)
                    dve.wait_ge(S("zx"), n + 1)
                    V.tensor_tensor(XT[:, g], XT[:, g], sixteen(4), ALU.add).then_inc(S("x_out"), 1)
            dve.wait_ge(S("x_out"), 22)
            V.memset(ST[:, 0], 0.0).then_inc(S("state"), 1)
            for c in range(NC):
                dve.wait_ge(S("gt"), c + 1)
                V.tensor_copy(GT[:, c], BK8[4 + c % 2][:, 0:256].rearrange("p (i n) -> p i n", n=CH)).then_inc(S("gt_out"), 1)
            dve.wait_ge(S("u_out"), 4)
            for c in range(NC):
                dve.wait_ge(S("sa"), c + 1)
                for p in range(2):
                    V.tensor_tensor(AVR[0:CH, c].rearrange("p (i q v) -> p i q v", q=2, v=CH)[:, :, p],
                                    BK8[p][0:CH, 0:256].rearrange("p (i v) -> p i v", v=CH),
                                    UM[:, c].rearrange("p (i q) v -> p i q v", q=2)[:, :, p], ALU.add).then_inc(S("sa_out"), 1)
                if c < NC - 1:
                    dve.wait_ge(S("st"), c + 1)
                    link(V.tensor_tensor(ST[:, c + 1], BK8[2][:, 0:256].rearrange("p (i v) -> p i v", v=CH), ST[:, c], ALU.add))
                    pc = PC[:].rearrange("p i (c t) -> p i c t", c=NC)[:, :, c, CH - 1:CH].to_broadcast([P, IT, CH])
                    V.tensor_tensor(ST[:, c + 1], ST[:, c + 1], pc, ALU.mult).then_inc(S("state"), 1)
            dve.wait_ge(S("yy_s"), 1)
            dve.wait_ge(S("y_t"), 1)
            V.tensor_tensor(YY[:], YY[:], pair(0), ALU.add).then_inc(S("stat_in"), 1)
            dve.wait_ge(S("stat_sum"), STAT["mu"] + 1)
            V.tensor_scalar(STA[:], BK8[2][0:NH, 0:ROWS], 1.0 / CH, None, ALU.mult).then_inc(S("stat_st"), 1)
            dve.wait_ge(S("stat_bc"), STAT["mu"] + 1)
            link(V.tensor_tensor(YY[:], YY[:], pair(3), ALU.subtract))
            V.tensor_tensor(YS[:], YY[:], YY[:], ALU.mult).then_inc(S("stat_in"), 1)
            dve.wait_ge(S("var_rt"), 1)
            V.reciprocal(STA[:], STA[:]).then_inc(S("stat_st"), 1)
            dve.wait_ge(S("stat_bc"), STAT["var"] + 1)
            link(V.tensor_tensor(YY[:], YY[:], pair(5), ALU.mult))
            for i in range(IT):
                last = V.tensor_scalar(YY[:, i], YY[:, i], par("lnxg", i), par("lnxb", i), ALU.mult, ALU.add)
            link(last)
            link(V.tensor_tensor(YY[:], YY[:], BO[:], ALU.add))
            link(V.tensor_tensor(YY[:], YY[:], GG[:], ALU.mult))
            link(V.tensor_copy(YA_HI[:], YY[:]))
            V.tensor_tensor(YA_LO[:], YY[:], YA_HI[:].bitcast(F32), ALU.subtract).then_inc(S("ya_split"), 1)
            link(V.tensor_copy(YB_HI[:], YB[:]))
            V.tensor_tensor(YB_LO[:], YB[:], YB_HI[:].bitcast(F32), ALU.subtract).then_inc(S("yb_split"), 1)
            for name in ("rwkv_proj", "fox_proj"):
                for u in range(2):
                    split_lo(dve, PHASE[name] + u + 2)

            dve.wait_ge(S("mod_tr"), 1)
            dve.wait_ge(S("bada_in"), 16)
            link(V.tensor_tensor(MOD[:].rearrange("p (q j) n -> p j q n", j=4), MOD[:].rearrange("p (q j) n -> p j q n", j=4),
                                 ADAP[:, 0:4 * MODR].rearrange("p (j q n) -> p j q n", j=4, n=2), ALU.add))
            for g, (chunk, who, m) in enumerate(((1, 0, "m1"), (1, 1, "m1"), (4, 0, "m2"), (4, 1, "m2"), (7, 0, "m3"))):
                V.scalar_tensor_tensor(out=GAIN[:, g], in0=MOD[:, 8 * chunk:8 * chunk + 8, who], scalar=1.0, in1=par(m, 0, 8),
                                       op0=ALU.add, op1=ALU.mult)
            for g, (chunk, who, f) in enumerate(((2, 0, 0.5), (2, 1, 0.5), (5, 0, 1.0), (8, 0, 0.5))):
                last = V.tensor_scalar(GATE[:, g], MOD[:, 8 * chunk:8 * chunk + 8, who], f, None, ALU.mult)
            link(last)

            def gates(name, sg, mt, oa, ob, hi, lo, out_sem, used_sem, split_sem, oa_sem, ob_sem):
                s0 = PHASE[name]
                dve.wait_ge(S(oa_sem), 8)
                dve.wait_ge(S(ob_sem), 8)
                for m in range(KT):
                    split_lo(dve, s0 + m + 2)
                    dve.wait_ge(S(out_sem), 2 * m + 2)
                    w = mt[:, m % 2]
                    V.tensor_tensor(w[:, 0], sg[:, (2 * m) % 4], oa[:, m], ALU.mult)
                    V.tensor_tensor(w[:, 1], sg[:, (2 * m + 1) % 4], ob[:, m], ALU.mult).then_inc(S(used_sem), 1)
                    dve.wait_ge(S(used_sem), m + 1)
                    link(V.tensor_tensor(w[:, 2], w[:, 0], w[:, 1], ALU.add))
                    link(V.tensor_copy(hi[:, m], w[:, 2]))
                    last = V.tensor_tensor(lo[:, m], w[:, 2], hi[:, m].bitcast(F32), ALU.subtract)
                    if m % 4 == 3:
                        last.then_inc(S(split_sem), 1)

            def out_add(name, banks, gate, sem):
                s0 = PHASE[name]
                for m in range(KT):
                    if m % 2 == 0:
                        split_lo(dve, s0 + m // 2 + 2)
                    dve.wait_ge(psum_ready, MARK0[s0] + m + 1)
                    V.scalar_tensor_tensor(out=XC[:, 0, m], in0=BK8[banks[m % 4]][:, 0:ROWS], scalar=gate(m), in1=XC[:, 0, m],
                                           op0=ALU.mult, op1=ALU.add).then_inc(S(sem), 1)

            gates("gates", SGA, MT, OA, OB, M_HI, M_LO, "gate_out", "gate_used", "m_split", "oa_out", "ob_out")
            out_add("out", [4, 5, 6, 3], lambda m: 1.0, "x_out1")
            norm("nc", 0, lambda k: par("n2", k))
            ffn(1, "ffn2", 1, half_)
            dve.wait_ge(S("dec_a"), 2)
            link(V.tensor_scalar(LG[:, 1], LG[:, 0], 2.0, None, ALU.add))
            link(V.reciprocal(LG[:, 1], LG[:, 1]))
            link(V.tensor_tensor(LG[:, 0], LG[:, 0], LG[:, 1], ALU.mult))
            link(V.tensor_tensor(LG[:, 1], LG[:, 0], LG[:, 0], ALU.mult))
            link(V.tensor_scalar(LG[:, 2], LG[:, 1], 1.0 / 17, None, ALU.mult))
            for n in (15, 13, 11, 9, 7, 5, 3):
                link(V.scalar_tensor_tensor(out=LG[:, 2], in0=LG[:, 2], scalar=1.0 / n, in1=LG[:, 1], op0=ALU.add, op1=ALU.mult))
            link(V.scalar_tensor_tensor(out=LG[:, 2], in0=LG[:, 2], scalar=1.0, in1=LG[:, 0], op0=ALU.add, op1=ALU.mult))
            link(V.tensor_scalar(LG[:, 1], par("dec", 0, 8), 0.0, None, ALU.min))
            link(V.scalar_tensor_tensor(out=LG[:, 4], in0=LG[:, 2], scalar=-2.0, in1=LG[:, 1], op0=ALU.mult, op1=ALU.add))
            link(V.tensor_scalar(LG[:, 3], LG[:, 4], -1.0, None, ALU.mult))
            for h in range(RH):
                V.tensor_scalar(LB[:, h, 0:2], par("jcol", 2, 2), LG[:, 4, h:h + 1], None, ALU.mult)
                last = V.tensor_scalar(LB[:, h, 2:4], par("jcol", 4, 2), LG[:, 4, 4 + h:5 + h], None, ALU.mult)
            link(last)
            norm("nd", 0, lambda k: par("nf", k), out=XC[:, 0])
            norm("ne", 0, lambda k: GAIN[:, 0, k:k + 1])
            norm("nf", 1, lambda k: GAIN[:, 1, k:k + 1])
            ffn(2, "ffn3", 2, lambda h, m: GATE[:, h, m:m + 1])
            norm("ng", 0, lambda k: GAIN[:, 2, k:k + 1])
            norm("nh", 1, lambda k: GAIN[:, 3, k:k + 1])

            def rotate(ps_e, ps_o, dst, h, sem):
                link(V.tensor_tensor(RT[:, 0], ps_e, ROPE[:, 0], ALU.mult))
                V.tensor_tensor(RT[:, 2], ps_e, ROPE[:, 1], ALU.mult).then_inc(S(sem), 1)
                link(V.tensor_tensor(RT[:, 1], ps_o, ROPE[:, 1], ALU.mult))
                V.tensor_tensor(RT[:, 3], ps_o, ROPE[:, 0], ALU.mult).then_inc(S(sem), 1)
                dve.wait_ge(S(sem), 2 * h + 2)
                V.tensor_tensor(dst[:, 2 * h], RT[:, 0], RT[:, 1], ALU.subtract)
                link(V.tensor_tensor(dst[:, 2 * h + 1], RT[:, 2], RT[:, 3], ALU.add))

            dve.wait_ge(S("rope_in"), 16)
            s0 = PHASE["ret_k"]
            for h in range(RH):
                split_lo(dve, s0 + h + 2)
                dve.wait_ge(psum_ready, MARK0[s0] + 2 * h + 2)
                rotate(BK8[(2 * h) % 4][:, 0:ROWS], BK8[(2 * h + 1) % 4][:, 0:ROWS], RK[:, 0], h, "rk_x")
            for s in range(PHASE["ret_v"], PHASE["ret_v"] + 8):
                split_lo(dve, s + 2)
            s0 = PHASE["ret_q"]
            for h in range(RH):
                split_lo(dve, s0 + h + 2)
                dve.wait_ge(psum_ready, MARK0[s0] + 2 * h + 2)
                rotate(BK8[(2 * h) % 4][:, 0:ROWS], BK8[(2 * h + 1) % 4][:, 0:ROWS], RQ, h, "rq_out")
            dve.wait_ge(S("iota_in"), 16)
            for kt in range(2):
                V.tensor_scalar(T1[:, kt], IOTA[:], par("jcol", kt), 0.0, ALU.subtract, ALU.max)
                last = V.tensor_scalar(T2[:, kt], IOTA[:], par("jcol", kt), 0.0, ALU.subtract, ALU.min)
            link(last)

            def decay_arg(h):
                link(V.tensor_scalar(DD[:, 0:2], T1[:], LG[:, 4, h:h + 1], None, ALU.mult))
                V.scalar_tensor_tensor(out=DD[:, 0:2], in0=T2[:], scalar=LG[:, 3, 4 + h:5 + h], in1=DD[:, 0:2],
                                       op0=ALU.mult, op1=ALU.add).then_inc(S("d_arg"), 1)

            decay_arg(0)
            for h in range(RH + 1):
                if h < RH:
                    dve.wait_ge(S("d_exp"), h + 1)
                    V.tensor_tensor(DD[:, 2:4], DD[:, 2:4], EB[:], ALU.add)
                    for kt in range(2):
                        blk = DD[:, kt, kt * P:(kt + 1) * P]
                        last = V.tensor_tensor(blk, blk, con("ident"), ALU.add)
                    link(last)
                    dve.wait_ge(S("rscores"), h + 1)
                    if h >= 1:
                        dve.wait_ge(S("pv_done"), h)
                    V.scalar_tensor_tensor(out=PT[:], in0=pair(0), scalar=1.0 / 16, in1=DD[:], op0=ALU.mult, op1=ALU.mult)\
                        .then_inc(S("pt_out"), 1)
                    dve.wait_ge(S("pt_out"), h + 1)
                if h >= 1:
                    g = h - 1
                    dve.wait_ge(S("mean_sum"), h)
                    ro = RO[:, 4 * g:4 * g + 4]
                    V.scalar_tensor_tensor(out=ro, in0=BK8[6][:, 0:ROWS].unsqueeze(1).to_broadcast([P, 4, ROWS]), scalar=-1.0 / RDV,
                                           in1=ro, op0=ALU.mult, op1=ALU.add).then_inc(S("ro_c"), 1)
                    dve.wait_ge(S("ro_c"), h)
                if h < RH - 1:
                    decay_arg(h + 1)
                if h >= 1:
                    dve.wait_ge(S("rvar_rt"), h)
                    V.reciprocal(RST[:, 1], RST[:, 0]).then_inc(S("rn_rec"), 1)
                    dve.wait_ge(S("rn_rec"), h)
                    V.tensor_tensor(ro, ro, RST[:, 1].unsqueeze(1).to_broadcast([P, 4, ROWS]), ALU.mult).then_inc(S("rn_done"), 1)
            dve.wait_ge(S("rn_done"), RH)
            s0 = PHASE["ret_g"]
            for t in range(16):
                if t % 2 == 0:
                    split_lo(dve, s0 + t // 2 + 2)
                dve.wait_ge(S("rg_out"), t + 1)
                V.scalar_tensor_tensor(out=RO[:, t], in0=SGG[:, t % 2], scalar=par("gn", t), in1=RO[:, t],
                                       op0=ALU.mult, op1=ALU.mult).then_inc(S("rg_used"), 1)
                dve.wait_ge(S("rg_used"), t + 1)
                link(V.tensor_copy(R_HI[:, t], RO[:, t]))
                V.tensor_tensor(R_LO[:, t], RO[:, t], R_HI[:, t].bitcast(F32), ALU.subtract).then_inc(S("r_split"), 1)
            for s in range(PHASE["four_in"], PHASE["four_in"] + 4):
                split_lo(dve, s + 2)
            dve.wait_ge(S("r_split"), 16)
            for q in range(8):
                dve.wait_ge(S("xm"), q + 1)
                link(V.tensor_copy(X_HI[:, q], BK8[q % 2][:, 0:ROWS]))
                V.tensor_tensor(X_LO[:, q], BK8[q % 2][:, 0:ROWS], X_HI[:, q].bitcast(F32), ALU.subtract).then_inc(S("xm_out"), 1)
            for s in range(PHASE["ret_proj"], PHASE["ret_proj"] + 8):
                split_lo(dve, s + 2)
            for s in range(PHASE["four_proj"], PHASE["four_proj"] + 4):
                split_lo(dve, s + 2)
            gates("gates2", SG2, MT2, OR, OF, M2_HI, M2_LO, "gate2_out", "gate2_used", "m2_split", "or_out", "of_out")
            out_add("out2", [4, 5, 0, 1], lambda m: GATE[:, 2, m:m + 1], "x_out2")
            norm("ni", 0, lambda k: GAIN[:, 4, k:k + 1])
            ffn(3, "ffn4", 1, lambda h, m: GATE[:, 3, m:m + 1])
            norm("nj", 0, lambda k: par("mf", k), out=NT)



def _tiles(w, kt=KT):
    k, c = w.shape
    return w.reshape(kt, P, c // P, P).transpose(2, 1, 0, 3).reshape(c // P, P, kt * P)


def _units(tiles, per):
    n = tiles.shape[0] // per
    return tiles.reshape(n, per, P, -1).transpose(0, 2, 1, 3).reshape(n, P, UNIT)


def _ffn_units(w1, w3, w2):
    a = np.concatenate([_tiles(w1)[:, :, None], _tiles(w3)[:, :, None]], axis=2).reshape(FT, P, UNIT)
    d = w2.reshape(FT // 2, 2, P, DM).transpose(0, 2, 1, 3).reshape(FT // 2, P, UNIT)
    out = [a[0], a[1]]
    for j in range(1, 11):
        out += [a[2 * j], d[j - 1], a[2 * j + 1]]
    return out + [d[10]]


def _row_units(w):
    c = w.shape[1]
    t = w.reshape(2, 4, P, c // 512, 512).transpose(3, 0, 2, 1, 4)
    return list(t.reshape(c // 512 * 2, P, UNIT))


def _gate_units(w):
    a, b = _tiles(w[:, :DM]), _tiles(w[:, DM:])
    return list(np.concatenate([a[:, :, None], b[:, :, None]], axis=2).reshape(KT, P, UNIT))


def _columns(v, n):
    return np.asarray(v).reshape(n, P).T


def _stream(i):
    w = {n: np.asarray(a) for n, a in i.items()}
    win, win2 = w["w_in"][0], w["w_in_2"][0]
    z = np.zeros((DM, 64), np.float32)
    r0 = 3 * DA
    s0 = r0 + 32 + 32 + 96
    low = np.concatenate([win[:, r0:r0 + 64], z, win[:, r0 + 64:s0], win[:, s0 + 3 * DA:s0 + 3 * DA + NH],
                          z[:, :P - 96 - NH]], axis=1)
    out = _ffn_units(w["ffn1_w1"][0], w["ffn1_w3"][0], w["ffn1_w2"][0])
    out += list(_units(_tiles(np.concatenate([win[:, :r0], low], axis=1)), 2))
    out += list(_units(_tiles(win[:, s0:s0 + 2 * DA]), 2))
    out += _row_units(win[:, s0 + 2 * DA:s0 + 3 * DA])
    out += list(_units(_tiles(w["rwkv_proj"][0], 4), 4)) + list(_units(_tiles(w["fox_proj"][0], 4), 4))
    out += _gate_units(win[:, s0 + 3 * DA + NH:])
    out += list(_units(_tiles(w["w_out"][0]), 2))
    out += _ffn_units(w["ffn2_w1"][0], w["ffn2_w3"][0], w["ffn2_w2"][0])
    a, b = w["w13_ffn1_2"][0], w["w13_ffn2_2"][0]
    out += _ffn_units(a[:, :FF], a[:, FF:], w["w2_ffn1_2"][0])

    def even_odd(x):
        return x.reshape(DM, RH, P, 2).transpose(0, 1, 3, 2).reshape(DM, DM)

    out += list(_units(_tiles(even_odd(win2[:, DM:2 * DM])), 2))
    out += _row_units(win2[:, 2 * DM:4 * DM])
    out += list(_units(_tiles(even_odd(win2[:, :DM])), 2))
    out += list(_units(_tiles(win2[:, 4 * DM:6 * DM]), 2))
    out += _row_units(win2[:, 6 * DM:7 * DM])
    out += list(_tiles(w["p_ret_2"][0], 16))
    out += list(_units(_tiles(w["p_four_2"][0]), 2))
    out += _gate_units(win2[:, 7 * DM:])
    out += list(_units(_tiles(w["w_out_2"][0]), 2))
    out += _ffn_units(b[:, :FF], b[:, FF:], w["w2_ffn2_2"][0])
    ada = _row_units(w["w_ada_2"][0])
    assert len(out) == NW and len(ada) == ADA
    return np.ascontiguousarray(np.stack([out[n] if kind == "w" else ada[n] for kind, n in ORDER]))


def _params(i):
    w = {n: np.asarray(a) for n, a in i.items()}
    par = np.zeros((P, NPAR), np.float32)

    def put(name, cols):
        a, b = PCOLS[name]
        par[:, a:b] = cols

    for name, key, n in (("n1", "ffn1_norm", 8), ("nm", "mix_norm", 8), ("w0", "rwkv_w0", 4), ("a0", "rwkv_a0", 4),
                         ("kk", "rwkv_k_k", 4), ("ka", "rwkv_k_a", 4), ("rk", "rwkv_r_k", 4), ("lnxg", "rwkv_lnx_g", 4),
                         ("lnxb", "rwkv_lnx_b", 4), ("n2", "ffn2_norm", 8), ("nf", "final_norm", 8), 
                         ("m1", "norm_ffn1_2", 8), ("m2", "norm_mix_2", 8), ("gn", "ret_gn_w_2", 16),
                         ("m3", "norm_ffn2_2", 8), ("mf", "norm_final_2", 8)):
        put(name, _columns(w[key], n))
    mu = w["shift_mu"][0]
    z = np.zeros(64, np.float32)
    put("mu", _columns(np.concatenate([mu[:3 * DA + 64], z, mu[3 * DA + 64:], z[:32]]), 14))
    fb = np.zeros((P, 1), np.float32)
    fb[96:96 + NH, 0] = w["fox_f_bias"][0]
    put("fb", fb)
    for name, key in (("qn", "fox_q_norm"), ("kn", "fox_k_norm")):
        put(name, np.concatenate([w[key][0], w[key][0]])[:, None])
    c = np.stack([w["c_2"][0].reshape(KT, P).T, w["c_ctx_2"].reshape(KT, P).T], axis=2)
    put("c", c.reshape(P, 16))
    put("dec", np.broadcast_to(np.concatenate([w["decay_fwd_2"][0], w["decay_bwd_2"][0]])[None], (P, 8)))
    put("epsr", 1e-6)
    put("epsl", 64e-5)
    put("epsq", 64e-6)
    put("one", 1.0)
    j = np.arange(2)[None] * P + np.arange(P)[:, None]
    put("jcol", np.concatenate([j, ROWS - j, ROWS + j], axis=1))
    return par


def _consts():
    con = np.zeros((P, NCON), np.float32)

    def put(name, x):
        a, b = CCOLS[name]
        con[:x.shape[0], a:b] = x.reshape(x.shape[0], -1)

    r = np.arange(P)
    put("ident", np.eye(P))
    put("ones", np.ones((P, P)))
    head = np.arange(IT)[None] * 2 + r[:, None] // 64
    put("sel", (head[:, :, None] == np.arange(NH)).astype(np.float32))
    put("bc", (head.T[None] == np.arange(NH)[:, None, None]).astype(np.float32))
    s, t = (r % CH)[:, None], np.arange(CH)[None]
    put("tmask", np.concatenate([t > s, t >= s], axis=1).astype(np.float32))
    a, b = np.arange(CH)[:, None], np.arange(CH)[None]
    lev = [((a // m == b // m + 1) & (a // (2 * m) == b // (2 * m))) for m in (1, 2, 4, 8, 16, 32)]
    put("lmask", np.stack(lev, axis=1).astype(np.float32))
    put("l0t", lev[0].T.astype(np.float32))
    put("causal", np.where(r[None] <= r[:, None], 0.0, -3.0e38))
    return con


def _rope_table():
    inv = 10000.0 ** (-np.arange(64, dtype=np.float32) / 64)
    pos = np.arange(ROWS)
    ang = np.concatenate([(pos // 64)[None] * inv[:, None], (pos % 64)[None] * inv[:, None]], axis=0).astype(np.float32)
    return np.stack([np.cos(ang), np.sin(ang)], axis=1).astype(np.float32)


def _dft_table():
    n = np.arange(256)
    ang = 2 * np.pi * ((n[:, None] * n[None]) % 256) / 256
    t = np.concatenate([np.cos(ang), np.sin(ang)], axis=1) / 16
    return np.ascontiguousarray(t.reshape(2, P, 512).transpose(1, 0, 2)).astype(np.float32)


def _arrays(i):
    w = {n: np.asarray(i[n]) for n in ("x", "ctx_2", "rwkv_w_up", "rwkv_a_up", "rwkv_g_up")}
    xin = np.stack([w[n][0].T.reshape(KT, P, ROWS).transpose(1, 0, 2) for n in ("x", "ctx_2")])
    lora = np.zeros((P, 2, DA), np.float32)
    lora[0:32, 0], lora[32:64, 0], lora[0:96, 1] = w["rwkv_w_up"][0], w["rwkv_a_up"][0], w["rwkv_g_up"][0]
    return {"stream": _stream(i), "xin": np.ascontiguousarray(xin), "params": _params(i), "consts": _consts(), "lora": lora,
            "bada": np.ascontiguousarray(np.repeat(_columns(i["b_ada_2"][0], 72)[:, :, None], 2, axis=2)),
            "rope": _rope_table(), "dft": _dft_table(),
            "iota": np.ascontiguousarray(np.broadcast_to(np.arange(ROWS, dtype=np.float32)[None], (P, ROWS)))}


def kernel(**inputs):
    import concourse.bacc as bacc
    from concourse.bass_utils import run_bass_kernel_spmd

    nc = bacc.Bacc("TRN2", target_bir_lowering=False, num_devices=1)
    arrays = _arrays(inputs)
    aps = {n: nc.dram_tensor(n, a.shape, F32, kind="ExternalInput").ap() for n, a in arrays.items()}
    out = nc.dram_tensor("out", (P, KT, ROWS), F32, kind="ExternalOutput").ap()
    build(nc, out=out, **aps)
    got = run_bass_kernel_spmd(nc, [arrays], core_ids=[0]).results[0]["out"]
    return np.ascontiguousarray(got.transpose(1, 0, 2).reshape(DM, ROWS).T)[None]
```

```python
from contextlib import ExitStack

import numpy as np
import concourse.bass as bass
from concourse import mybir

F32 = mybir.dt.float32
F32R = mybir.dt.float32r
ALU = mybir.AluOpType
ACT = mybir.ActivationFunctionType
AX_X = mybir.AxisListType.X

P = 128
ROWS = 256
DM = 1024
KT = DM // P
FF = 2816
FT = FF // P
DA = 512
IT = DA // P
NH = 8
CH = 64
NC = ROWS // CH
RH, RDV = 4, 512
UNIT = 2048
RING = 3
DECAY = float(np.exp(-0.5))

FFN_MARKS = [2, 2] + [2, 8, 2] * 10 + [8]
MARKS = []
PHASE = {}


def _phase(name, marks):
    PHASE[name] = len(MARKS)
    MARKS.extend(marks)


_phase("ffn1", FFN_MARKS)
_phase("rwkv_in", [2] * 7)
_phase("fox_qk", [2] * 4)
_phase("fox_v", [1, 2])
_phase("rwkv_proj", [4] * 2)
_phase("fox_proj", [4] * 2)
_phase("gates", [2] * 8)
_phase("out", [2] * 4)
_phase("ffn2", FFN_MARKS)
_phase("ffn3", FFN_MARKS)
_phase("ret_q", [2] * 4)
_phase("ret_k", [2] * 4)
_phase("ret_v", [1, 4] * 4)
_phase("ret_g", [2] * 8)
_phase("four_in", [1, 2] * 2)
_phase("ret_proj", [1] * 8)
_phase("four_proj", [2] * 4)
_phase("gates2", [2] * 8)
_phase("out2", [2] * 4)
_phase("ffn4", FFN_MARKS)
NW = len(MARKS)
MARK0 = [0]
for _m in MARKS:
    MARK0.append(MARK0[-1] + _m)

ADA = 36
MODR = 36
ADA_NB = 3
ADA_AFTER = {PHASE["rwkv_in"] - 1: ADA_NB, PHASE["rwkv_proj"] - 1: ADA - ADA_NB}
ORDER = []
for _s in range(NW):
    ORDER.append(("w", _s))
    if _s - 2 in ADA_AFTER:
        _d = sum(1 for o in ORDER if o[0] == "a")
        ORDER.extend(("a", _d + n) for n in range(ADA_AFTER[_s - 2]))
RAW_OF = {o: n for n, o in enumerate(ORDER)}
NU = len(ORDER)

NORM = {n: k for k, n in enumerate(("na", "nb", "nf", "nc", "nd", "ne", "ng", "nh", "ni", "nj"))}
NORM_H = {n: k for k, n in enumerate(("na", "nb", "nf", "nc", "ne", "ng", "nh", "ni"))}
STAT = {n: k for k, n in enumerate(("kk", "bon", "fq", "fk", "mu", "var"))}

PCOLS = {}
_n = 0
for _name, _w in [("n1", 8), ("nm", 8), ("mu", 14), ("w0", 4), ("a0", 4), ("kk", 4), ("ka", 4), ("rk", 4),
                  ("lnxg", 4), ("lnxb", 4), ("fb", 1), ("qn", 1), ("kn", 1), ("n2", 8), ("nf", 8),
                  ("c", 16), ("m1", 8), ("m2", 8), ("gn", 16), ("m3", 8), ("mf", 8),
                  ("dec", 8), ("epsr", 1), ("epsl", 1), ("epsq", 1), ("one", 1), ("jcol", 6)]:
    PCOLS[_name] = (_n, _n + _w)
    _n += _w
NPAR = _n
CCOLS = {}
_n = 0
for _name, _w in [("ident", 128), ("ones", 128), ("sel", 32), ("bc", 512), ("tmask", 128), ("lmask", 384),
                  ("l0t", 64), ("causal", 128)]:
    CCOLS[_name] = (_n, _n + _w)
    _n += _w
NCON = _n


def build(nc, stream, xin, params, consts, lora, bada, rope, dft, iota, out):
    with ExitStack() as ctx:
        sems = {}

        def S(name):
            if name not in sems:
                sems[name] = ctx.enter_context(nc.semaphore(name))
            return sems[name]

        def sb(name, shape, off, dt=F32):
            return nc.alloc_sbuf_tensor_at(name, shape, dt, offset=off)

        RAW0 = 16512
        HI0 = RAW0 + RING * UNIT * 4
        LO0 = HI0 + RING * UNIT * 4
        HHI0 = LO0 + RING * UNIT * 4
        HLO0 = HHI0 + 16384
        XC0 = HLO0 + 16384
        D0 = XC0 + 16384
        CON0 = D0 + 16384
        A0 = CON0 + 9216
        B1, B2, C0 = HHI0 + 8192, HLO0 + 8192, XC0 + 8192

        RAW = [sb(f"RAW{i}", [P, UNIT], RAW0 + i * UNIT * 4) for i in range(RING)]
        W_HI = [sb(f"W_HI{i}", [P, UNIT], HI0 + i * UNIT * 4, F32R) for i in range(RING)]
        W_LO = [sb(f"W_LO{i}", [P, UNIT], LO0 + i * UNIT * 4, F32R) for i in range(RING)]
        H_HI = sb("H_HI", [P, 2, KT, ROWS], HHI0, F32R)
        H_LO = sb("H_LO", [P, 2, KT, ROWS], HLO0, F32R)
        XC = sb("XC", [P, 2, KT, ROWS], XC0)
        HID_HI = sb("HID_HI", [P, 2, 512], D0, F32R)
        HID_LO = sb("HID_LO", [P, 2, 512], D0 + 4096, F32R)
        SILU = sb("SILU", [P, 2, 512], D0 + 8192)
        PROD = sb("PROD", [P, 2, 512], D0 + 12288)
        NT = sb("NT", [P, KT, ROWS], D0 + 8192)
        NT2 = sb("NT2", [P, KT, ROWS], A0 + 47104)
        CON = sb("CON", [P, NCON], CON0)
        PAR = sb("PAR", [P, NPAR], CON0 + NCON * 4)
        off = (CON0 + (NCON + NPAR) * 4 + 31) // 32 * 32
        MOD = sb("MOD", [P, 72, 2], off)
        off += 576
        SCZ = sb("SCZ", [P, MODR * (KT + 1) - 2], off)
        off += (MODR * (KT + 1) - 2) * 4
        off = (off + 31) // 32 * 32
        GAIN = sb("GAIN", [P, 5, 8], off)
        off += 160
        GATE = sb("GATE", [P, 4, 8], off)
        off += 128
        LG = sb("LG", [P, 5, 8], off)
        off += 160
        LB = sb("LB", [P, RH, 4], off)
        off += 64
        assert off <= A0

        def con(name, rows=P):
            a, b = CCOLS[name]
            return CON[0:rows, a:b]

        def par(name, i=0, n=1, rows=P):
            a = PCOLS[name][0]
            return PAR[0:rows, a + i:a + i + n]

        STD = sb("STD", [P, ROWS], A0 + 61440)
        RSTD = sb("RSTD", [P, ROWS], A0 + 62464)

        PRE = sb("PRE", [P, 14, ROWS + 1], A0)
        RKV = sb("RKV", [P, 3, IT, ROWS], A0 + 14400)
        LOR = sb("LOR", [P, 2, ROWS], A0 + 26688)
        FQ = sb("FQ", [P, IT, ROWS], A0 + 28736)
        FK = sb("FK", [P, IT, ROWS], A0 + 32832)
        FV = sb("FV", [P, 2, DA], A0 + 36928)
        LW = sb("LW", [P, 2, DA], A0 + 41024)
        SG = sb("SG", [P, IT, ROWS], A0 + 45120)
        AA = sb("AA", [P, IT, ROWS], A0 + 49216)
        KK = sb("KK", [P, IT, ROWS], A0 + 53312)
        TMP = sb("TMP", [P, IT, ROWS], A0 + 57408)
        STA = sb("STA", [NH, ROWS], A0 + 61504)
        STB = sb("STB", [NH, ROWS], A0 + 62528)
        GG = sb("GG", [P, IT, ROWS], B1)
        BO = sb("BO", [P, IT, ROWS], B1 + 4096)
        AR = sb("AR", [P, IT, NC, 2, CH], B2)
        BK = sb("BK", [P, IT, NC, 2, CH], C0)
        AV = sb("AV", [P, IT, NC, 2, CH], D0)
        LS = sb("LS", [P, IT, ROWS], D0 + 8192)
        PC = sb("PC", [P, IT, ROWS], D0 + 12288)
        F1 = sb("F1", [NH, ROWS], A0 + 41024)
        F2 = sb("F2", [NH, ROWS], A0 + 42048)
        F3 = sb("F3", [NH, ROWS], A0 + 43072)
        F4 = sb("F4", [NH, ROWS], A0 + 44096)
        NCB = sb("NCB", [P, NH, ROWS], A0)
        SCO = sb("SCO", [P, 2, 384], A0 + 8192)
        PRT = sb("PRT", [P, 2, 384], A0 + 11264)
        YB = sb("YB", [P, IT, ROWS], D0 + 8192)
        FST = sb("FST", [P, 2, 6], A0 + 14336)
        TT = sb("TT", [P, NC, NH, 2 * CH], A0)
        XM = sb("XM", [CH, NC, NH, CH], A0 + 16384)
        XT = sb("XT", [CH, NC, NH, CH], A0 + 24576)
        ZM = sb("ZM", [CH, NC, NH, CH], A0 + 32768)
        BKR = sb("BKR", [P, NC, DA], A0 + 40960)
        AVR = sb("AVR", [P, NC, DA], A0 + 49152)
        GT = sb("GT", [P, NC, IT, CH], A0 + 57344)
        WM = sb("WM", [CH, NC * NH, CH], C0)
        UM = sb("UM", [CH, NC, NH, CH], D0)
        ST = sb("ST", [P, NC + 1, IT, CH], A0 + 32768)
        YY = sb("YY", [P, IT, ROWS], A0 + 16384)
        YS = sb("YS", [P, IT, ROWS], A0 + 20480)
        YA_HI = sb("YA_HI", [P, IT, ROWS], C0, F32R)
        YA_LO = sb("YA_LO", [P, IT, ROWS], C0 + 4096, F32R)
        YB_HI = sb("YB_HI", [P, IT, ROWS], D0, F32R)
        YB_LO = sb("YB_LO", [P, IT, ROWS], D0 + 4096, F32R)
        MROW = sb("MROW", [MODR, 512], A0 + 45056)
        OA = sb("OA", [P, KT, ROWS], A0)
        OB = sb("OB", [P, KT, ROWS], A0 + 8192)
        M_HI = sb("M_HI", [P, KT, ROWS], A0 + 16384, F32R)
        M_LO = sb("M_LO", [P, KT, ROWS], A0 + 24576, F32R)
        SGA = sb("SGA", [P, 4, ROWS], A0 + 32768)
        MT = sb("MT", [P, 2, 3, ROWS], A0 + 36864)

        RK = sb("RK", [P, 2, KT, ROWS], A0)
        RV = sb("RV", [P, 4, RH * RDV], A0 + 16384)
        RQ = sb("RQ", [P, KT, ROWS], A0 + 49152)
        ROPE = sb("ROPE", [P, 2, ROWS], A0 + 57344)
        RT = sb("RT", [P, 4, ROWS], A0 + 59392)
        RO = sb("RO", [P, 16, ROWS], D0)
        PT = sb("PT", [P, 4, ROWS], C0)
        DD = sb("DD", [P, 4, ROWS], C0 + 4096)
        T1 = sb("T1", [P, 2, ROWS], B1)
        T2 = sb("T2", [P, 2, ROWS], B1 + 2048)
        EB = sb("EB", [P, 2, ROWS], B1 + 4096)
        IOTA = sb("IOTA", [P, ROWS], B1 + 6144)
        SQ = sb("SQ", [P, 4, ROWS], B2)
        RST = sb("RST", [P, 2, ROWS], B2 + 4096)
        SGG = sb("SGG", [P, 2, ROWS], B2 + 6144)
        R_HI = sb("R_HI", [P, 16, ROWS], A0 + 16384, F32R)
        R_LO = sb("R_LO", [P, 16, ROWS], A0 + 32768, F32R)
        FX = sb("FX", [P, 2, DM], A0)
        DFT = sb("DFT", [P, 2, 512], A0 + 8192)
        ZZ = sb("ZZ", [P, 2, 2, 512], A0 + 49152)
        X_HI = sb("X_HI", [P, KT, ROWS], D0, F32R)
        X_LO = sb("X_LO", [P, KT, ROWS], D0 + 8192, F32R)
        FM = sb("FM", [P, 2, 2, ROWS], B2)
        OR = sb("OR", [P, KT, ROWS], C0)
        OF = sb("OF", [P, KT, ROWS], B1)
        M2_HI = sb("M2_HI", [P, KT, ROWS], A0, F32R)
        M2_LO = sb("M2_LO", [P, KT, ROWS], A0 + 8192, F32R)
        SG2 = sb("SG2", [P, 4, ROWS], A0 + 49152)
        MT2 = sb("MT2", [P, 2, 3, ROWS], A0 + 53248)

        PS = ctx.enter_context(nc.psum_tensor("PS", [P, 8, 512], F32))
        BK8 = [PS[:, i] for i in range(8)]
        ADAP = BK8[7]

        def pair(b):
            return PS[:, b:b + 2].rearrange("p b (i n) -> p (b i) n", n=ROWS)

        NORM_BANK = {n: BK8[b][:, 0:ROWS] for n, b in (("na", 4), ("nb", 3), ("nf", 7), ("nc", 2), ("nd", 3), ("ne", 2),
                                                       ("ng", 3), ("nh", 2), ("ni", 2), ("nj", 3))}
        psum_ready = S("psum_ready")
        landed = [S(f"landed{i}") for i in range(RING)]
        hi_done, lo_done = S("hi_done"), S("lo_done")
        ada_used = S("ada_used")

        def raw(s):
            return RAW_OF[("w", s)]

        def split_hi(act, s, j=None, j0=0):
            if s >= NW:
                return
            u = raw(s)
            if j is None:
                act.wait_ge(landed[u % RING], 16 * (u // RING + 1))
                if s >= RING:
                    act.wait_ge(psum_ready, MARK0[s - RING + 1])
            else:
                act.wait_ge(landed[u % RING], (j - j0) * 16 + 16 * (u // RING + 1))
                act.wait_ge(psum_ready, (j - j0) * 12 + MARK0[s - RING + 1])
            nc.scalar.activation(W_HI[s % RING][:], RAW[u % RING][:], ACT.Copy).then_inc(hi_done, 1)

        def split_lo(dve, s, j=None, j0=0):
            if s >= NW:
                return
            u = raw(s)
            dve.wait_ge(hi_done, s + 1 if j is None else (j - j0) * 3 + s + 1)
            nc.vector.tensor_tensor(W_LO[s % RING][:], RAW[u % RING][:], W_HI[s % RING][:].bitcast(F32),
                                    ALU.subtract).then_inc(lo_done, 1)

        def three(acc, w_hi, w_lo, x_hi, x_lo, first, last):
            nc.tensor.matmul(acc, w_hi, x_hi, start=first, stop=False)
            nc.tensor.matmul(acc, w_hi, x_lo, start=False, stop=False)
            return nc.tensor.matmul(acc, w_lo, x_hi, start=False, stop=last)

        block = ctx.enter_context(nc.Block())

        @block.sync
        def _(sp):
            sp.dma_start(XC[:, 0], xin[0]).then_inc(S("x_in"), 16)

            def free_raw(u, j=None, j0=0):
                if u < RING:
                    return
                kind, n = ORDER[u - RING]
                if kind == "w":
                    sp.wait_ge(lo_done, n + 1 if j is None else (j - j0) * 3 + n + 1)
                else:
                    sp.wait_ge(ada_used, n + 1)

            def load(u, j=None, j0=0):
                free_raw(u, j, j0)
                src = stream[u] if j is None else \
                    stream[bass.ds((j - j0) * 3 + u, 1)].rearrange("a p n -> (a p) n")
                sp.dma_start(RAW[u % RING][:], src).then_inc(landed[u % RING], 16)

            u = 0
            while u < NU:
                n = 0
                while u >= RING and u + n < NU and ORDER[u + n][0] == "w" and ORDER[u + n - RING][0] == "w":
                    n += 1
                if n >= 6:
                    with sp.Fori(0, n // 3) as j:
                        for i in range(3):
                            load(u + i, j, 0)
                    u += n // 3 * 3
                else:
                    load(u)
                    u += 1

        @block.gpsimd
        def _(pool):
            pool.dma_start(CON[:], consts).then_inc(S("con_in"), 16)
            pool.dma_start(PAR[:], params).then_inc(S("par_in"), 16)
            pool.dma_start(LW[:], lora).then_inc(S("lw_in"), 16)
            pool.dma_start(MOD[:], bada).then_inc(S("bada_in"), 16)
            pool.wait_ge(psum_ready, MARK0[PHASE["fox_proj"]])
            pool.dma_start(XC[:, 1], xin[1]).then_inc(S("ctx_in"), 16)
            pool.wait_ge(S("x_out1"), 8)
            pool.dma_start(ROPE[:], rope).then_inc(S("rope_in"), 16)
            pool.wait_ge(psum_ready, MARK0[PHASE["ret_g"]])
            pool.dma_start(IOTA[:], iota).then_inc(S("iota_in"), 16)
            pool.wait_ge(S("pv_done"), RH)
            pool.dma_start(DFT[:], dft).then_inc(S("dft_in"), 16)
            for k in range(0, KT, 4):
                pool.wait_ge(S("final"), k + 4)
                pool.dma_start(out[:, k:k + 4], NT[:, k:k + 4]).then_inc(S("stored"), 16)
            pool.wait_ge(S("stored"), 32)

        @block.tensor
        def _(pe):
            def wait_unit(s, j=None, j0=0):
                pe.wait_ge(lo_done, s + 1 if j is None else (j - j0) * 3 + s + 1)

            def norm_sum(name, k, tmp=NT):
                pe.wait_ge(S("norm_sq"), KT * NORM[name] + k + 1)
                last = nc.tensor.matmul(NORM_BANK[name], con("ones"), tmp[:, k], start=(k == 0), stop=(k == 7))
                if k == 7:
                    last.then_inc(S("norm_ssq"), 1)

            def norm(name, tmp=NT):
                for k in range(KT):
                    norm_sum(name, k, tmp)

            def ffn(f, name, halves, h_name, then):
                n = halves * ROWS
                s0 = PHASE[name]
                rh = (lambda k: H_HI[:, 0:halves, k])
                rl = (lambda k: H_LO[:, 0:halves, k])

                def up(t, s, j=None, j0=0):
                    wait_unit(s, j, j0)
                    tt = f * FT + t
                    if tt >= 2:
                        pe.wait_ge(S("hid_prod"), tt - 1 if j is None else (j - j0) * 2 + tt - 1)
                    sl = s % RING
                    for w in range(2):
                        acc = BK8[2 * (t % 2) + w][:, 0:n]
                        for k in range(KT):
                            if t == 0 and w == 0:
                                pe.wait_ge(S("norm_h"), KT * NORM_H[h_name] + k + 1)
                            c = (w * KT + k) * P
                            last = three(acc, W_HI[sl][:, c:c + P], W_LO[sl][:, c:c + P], rh(k), rl(k), k == 0, k == KT - 1)
                        last.then_inc(psum_ready, 1)

                def down(i, s, j=None, j0=0):
                    wait_unit(s, j, j0)
                    a = f * FT + 2 * i + 2
                    pe.wait_ge(S("hid_lo"), a if j is None else (j - j0) * 2 + a)
                    sl = s % RING
                    for m in range(KT):
                        d = f * 88 + i * 8 + m
                        if d >= 4:
                            pe.wait_ge(S("down_added"), d - 3 if j is None else (j - j0) * 8 + d - 3)
                        for t in range(2):
                            c = (t * KT + m) * P
                            last = three(BK8[4 + m % 4][:, 0:n], W_HI[sl][:, c:c + P], W_LO[sl][:, c:c + P],
                                         HID_HI[:, t, 0:n], HID_LO[:, t, 0:n], t == 0, t == 1)
                        last.then_inc(psum_ready, 1)
                        if i == 10 and m >= 3:
                            norm_sum(then, m - 3)
                    if i == 10:
                        for k in range(5, KT):
                            norm_sum(then, k)

                up(0, s0)
                up(1, s0 + 1)
                with pe.Fori(1, 11) as j:
                    up(2, s0 + 2, j, 1)
                    down(0, s0 + 3, j, 1)
                    up(3, s0 + 4, j, 1)
                down(10, s0 + 32)

            def cols(name, banks, rhs_hi, rhs_lo, n, out_sem, kt=KT, tiles=2, first=None, behind=None):
                s0 = PHASE[name]
                units = [s for s in range(s0, NW) if s < s0 + {"rwkv_in": 7, "fox_qk": 4, "rwkv_proj": 2, "fox_proj": 2,
                         "gates": 8, "out": 4, "ret_k": 4, "ret_q": 4, "ret_g": 8, "ret_proj": 8, "four_proj": 4,
                         "gates2": 8, "out2": 4}[name]]
                tile = 0
                for s in units:
                    wait_unit(s)
                    for w in range(tiles):
                        if tile >= len(banks):
                            pe.wait_ge(S(out_sem), tile - len(banks) + 1)
                        acc = BK8[banks[tile % len(banks)]][:, 0:n]
                        for k in range(kt):
                            if tile == 0 and first is not None:
                                pe.wait_ge(S(first[0]), first[1] + k + 1)
                            c = (w * kt + k) * P
                            sl = s % RING
                            last = three(acc, W_HI[sl][:, c:c + P], W_LO[sl][:, c:c + P], rhs_hi(k), rhs_lo(k),
                                         k == 0, k == kt - 1)
                        last.then_inc(psum_ready, 1)
                        tile += 1
                    if behind is not None and s - s0 in behind:
                        behind[s - s0]()

            def rows(name, chunk, n_chunks, rts, banks, out_sem, k0):
                for q in range(n_chunks):
                    s = PHASE[name] + 2 * q
                    for half in range(2):
                        wait_unit(s + half)
                        for r, (h, r0) in enumerate(rts):
                            if half == 0 and (q * len(rts) + r) >= len(banks):
                                pe.wait_ge(S(out_sem), q * len(rts) + r - len(banks) + 1)
                            bank = BK8[banks[(q * len(rts) + r) % len(banks)]]
                            for k4 in range(4):
                                k = half * 4 + k4
                                sl = (s + half) % RING
                                c = k4 * 512
                                st, sp_ = (k == 0), (k == 7)
                                xh, xl = H_HI[:, h, k, r0:r0 + P], H_LO[:, h, k, r0:r0 + P]
                                wh, wl = W_HI[sl][:, c:c + 512], W_LO[sl][:, c:c + 512]
                                nc.tensor.matmul(bank[:], xh, wh, start=st, stop=False)
                                nc.tensor.matmul(bank[:], xh, wl, start=False, stop=False)
                                last = nc.tensor.matmul(bank[:], xl, wh, start=False, stop=sp_)
                            if half == 1 or r == len(rts) - 1:
                                last.then_inc(psum_ready, 1)

            ada_at = [0]

            def ada(n):
                for m in range(ada_at[0], min(ada_at[0] + n, ADA * 4)):
                    d, k, q = m // 4, m % 8, m // 8
                    u = RAW_OF[("a", d)]
                    if m == 0:
                        pe.wait_ge(S("sc_done"), 1)
                    if m % 4 == 0:
                        pe.wait_ge(landed[u % RING], 16 * (u // RING + 1))
                    z = MODR - 2 + MODR * k - 2 * q
                    last = nc.tensor.matmul(ADAP[0:MODR], SCZ[:, z:z + MODR], RAW[u % RING][:, (m % 4) * 512:(m % 4 + 1) * 512],
                                            start=(m == 0), stop=(m == ADA * 4 - 1))
                    if m % 4 == 3:
                        last.then_inc(ada_used, 1)
                ada_at[0] = min(ada_at[0] + n, ADA * 4)

            pe.wait_ge(S("con_in"), 16)
            norm("na")
            ffn(0, "ffn1", 1, "na", "nb")
            ada(4 * ADA_NB)
            xh, xl = (lambda k: H_HI[:, 0, k]), (lambda k: H_LO[:, 0, k])
            cols("rwkv_in", [4, 5, 6, 0], xh, xl, ROWS, "pre_out", first=("norm_h", KT * NORM_H["nb"]))
            pe.wait_ge(S("pre_out"), 14)
            cols("fox_qk", [4, 5, 6, 0], xh, xl, ROWS, "fqk_out")
            rows("fox_v", DA, 1, [(0, 0), (0, P)], [1, 2], "fv_out", 0)
            pe.wait_ge(S("fqk_out"), 8)
            pe.wait_ge(S("lw_in"), 16)
            pe.wait_ge(S("lora_act"), 1)
            for i in range(IT):
                last = nc.tensor.matmul(BK8[3 + i // 2][:, (i % 2) * ROWS:(i % 2 + 1) * ROWS], LW[0:32, 0, i * P:(i + 1) * P],
                                        LOR[0:32, 0], start=True, stop=True)
            last.then_inc(S("lora_z"), 1)
            for i in range(IT):
                last = nc.tensor.matmul(BK8[5 + i // 2][:, (i % 2) * ROWS:(i % 2 + 1) * ROWS], LW[32:64, 0, i * P:(i + 1) * P],
                                        LOR[32:64, 0], start=True, stop=True)
            last.then_inc(S("lora_a"), 1)
            pe.wait_ge(S("lora_act"), 2)
            pe.wait_ge(S("fv_out"), 2)
            for i in range(IT):
                last = nc.tensor.matmul(BK8[[0, 1][i // 2]][:, (i % 2) * ROWS:(i % 2 + 1) * ROWS], LW[0:96, 1, i * P:(i + 1) * P],
                                        LOR[0:96, 1], start=True, stop=True)
            last.then_inc(S("lora_g"), 1)

            def stat(src, banks, name):
                ada(4)
                pe.wait_ge(S("stat_in"), STAT[name] + 1)
                for i in range(IT):
                    last = nc.tensor.matmul(BK8[banks][0:NH, 0:ROWS], con("sel")[:, 8 * i:8 * i + 8], src[:, i],
                                            start=(i == 0), stop=(i == IT - 1))
                last.then_inc(S("stat_sum"), 1)

            def spread(src, b0, name):
                ada(4)
                pe.wait_ge(S("stat_st"), STAT[name] + 1)
                for i in range(IT):
                    last = nc.tensor.matmul(BK8[b0 + i // 2][:, (i % 2) * ROWS:(i % 2 + 1) * ROWS],
                                            con("bc", NH)[:, i * P:(i + 1) * P], src, start=True, stop=True)
                last.then_inc(S("stat_bc"), 1)

            stat(TMP, 2, "kk")
            pe.wait_ge(S("sg_done"), 1)
            spread(STA[:], 3, "kk")
            stat(TMP, 2, "bon")
            pe.wait_ge(S("aa_done"), 1)
            spread(STA[:], 5, "bon")
            stat(TMP, 2, "fq")
            spread(STA[:], 3, "fq")
            stat(TMP, 2, "fk")
            spread(STA[:], 5, "fk")
            ada(4)
            pe.wait_ge(S("lf_cum"), 1)
            pe.wait_ge(S("fq_norm"), 1)
            pe.wait_ge(S("fk_norm"), 1)
            pe.wait_ge(S("gg_done"), 1)
            for h in range(NH):
                if h >= 4 and h % 2 == 0:
                    pe.wait_ge(S("ncb_out"), h // 2 - 1)
                last = nc.tensor.matmul(BK8[[0, 1][(h // 2) % 2]][:, (h % 2) * ROWS:(h % 2 + 1) * ROWS],
                                        con("ident", NH)[:, h:h + 1].to_broadcast([NH, P]), STB[:],
                                        start=True, stop=True)
                if h % 2:
                    last.then_inc(S("ncb"), 1)
            for h in range(NH + 1):
                if h < NH:
                    i, p0 = h // 2, 64 * (h % 2)
                    if h >= 2:
                        pe.wait_ge(S("sco_out"), h - 1)
                    b = BK8[3 + h % 2]
                    nc.tensor.matmul(b[:, 0:P], FQ[p0:p0 + 64, i, 0:P], FK[p0:p0 + 64, i, 0:P], start=True, stop=True)
                    last = nc.tensor.matmul(b[:, P:384], FQ[p0:p0 + 64, i, P:ROWS], FK[p0:p0 + 64, i, :], start=True, stop=True)
                    last.then_inc(S("scores"), 1)
                if h >= 1:
                    g = h - 1
                    i, p0 = g // 2, 64 * (g % 2)
                    ada(3)
                    pe.wait_ge(S("probs"), g + 1)
                    if g >= 2:
                        pe.wait_ge(S("fo_out"), g - 1)
                    for q in range(3):
                        last = nc.tensor.transpose(BK8[5 + g % 2][:, q * P:(q + 1) * P], SCO[:, g % 2, q * P:(q + 1) * P],
                                                   con("ident"))
                    last.then_inc(S("prt"), 1)
                    pe.wait_ge(S("prt_out"), g + 1)
                    o = BK8[1 + g % 2][p0:p0 + 64, 0:ROWS]
                    v = (lambda kt: FV[:, kt, 64 * g:64 * g + 64])
                    nc.tensor.matmul(o[:, 0:P], v(0), PRT[:, g % 2, 0:P], start=True, stop=True)
                    nc.tensor.matmul(o[:, P:ROWS], v(0), PRT[:, g % 2, P:2 * P], start=True, stop=False)
                    last = nc.tensor.matmul(o[:, P:ROWS], v(1), PRT[:, g % 2, 2 * P:3 * P], start=False, stop=True)
                    last.then_inc(S("fox_o"), 1)
            ada(4)
            pe.wait_ge(S("bk_ready"), 1)
            pe.wait_ge(S("av_ready"), 1)
            pe.wait_ge(S("fo_out"), NH)
            for c in range(NC):
                for n, src in enumerate((BK, AV)):
                    q = 2 * c + n
                    if q >= 2:
                        pe.wait_ge(S("tr_out"), q - 1)
                    for i in range(IT):
                        last = nc.tensor.transpose(BK8[q % 2][:, i * P:(i + 1) * P],
                                                   src[:, i, c].rearrange("p a b -> p (a b)"), con("ident"))
                    last.then_inc(S("tr"), 1)
            for c in range(NC):
                for p in range(2):
                    q = 2 * c + p
                    if q >= 4:
                        pe.wait_ge(S("tt_out"), q - 3)
                    for i in range(IT):
                        last = nc.tensor.matmul(BK8[2 + q % 4][:, i * P:(i + 1) * P],
                                                BK[64 * p:64 * p + 64, i, c].rearrange("p a b -> p (a b)"),
                                                AR[64 * p:64 * p + 64, i, c].rearrange("p a b -> p (a b)"),
                                                start=True, stop=True)
                    last.then_inc(S("tt"), 1)
            pe.wait_ge(S("tr_out"), 8)
            for c in range(NC):
                pe.wait_ge(S("tt_out"), 2 * c + 2)
                if c >= 2:
                    pe.wait_ge(S("w_out"), c - 1)
                for h in range(NH):
                    last = nc.tensor.matmul(BK8[c % 2][0:CH, h * CH:(h + 1) * CH], TT[CH:P, c, h, 0:CH],
                                            AVR[CH:P, c, h * CH:(h + 1) * CH], start=True, stop=True)
                last.then_inc(S("w"), 1)
            pe.wait_ge(S("w_out"), 4)

            def x_done(n):
                return 2 * n + 2 if n < 5 * NC else 5 * NC + n + 1

            def z_step(n):
                lev, c = n // NC, n % NC
                if n >= 2:
                    pe.wait_ge(S("z_out"), n - 1)
                if lev > 0:
                    pe.wait_ge(S("x_out"), x_done(n - NC))
                for h in range(NH):
                    rhs = con("ident", CH)[:, 0:CH] if lev == 0 else XM[:, c, h]
                    last = nc.tensor.matmul(BK8[n % 2][0:CH, h * CH:(h + 1) * CH], TT[0:CH, c, h, 0:CH], rhs,
                                            start=True, stop=True)
                last.then_inc(S("z"), 1)

            for n in range(NC + 2):
                z_step(n)
                ada(1)
            for n in range(NC, 6 * NC):
                lev, c = n // NC, n % NC
                pe.wait_ge(S("z_out"), n + 1)
                pe.wait_ge(S("x_out"), x_done(n - 2))
                if lev < 5:
                    for h in range(NH):
                        last = nc.tensor.matmul(BK8[2 + n % 2][0:CH, h * CH:(h + 1) * CH], XT[:, c, h], ZM[:, c, h],
                                                start=True, stop=True)
                    last.then_inc(S("xz"), 1)
                for h in range(NH):
                    last = nc.tensor.matmul(BK8[4 + n % 2][0:CH, h * CH:(h + 1) * CH], ZM[:, c, h], XT[:, c, h],
                                            start=True, stop=True)
                last.then_inc(S("zx"), 1)
                if n + 2 < 6 * NC:
                    z_step(n + 2)
            for c in range(NC):
                pe.wait_ge(S("x_out"), x_done(5 * NC + c))
                if c >= 2:
                    pe.wait_ge(S("u_out"), c - 1)
                for h in range(NH):
                    last = nc.tensor.matmul(BK8[2 + c % 2][0:CH, h * CH:(h + 1) * CH], XT[:, c, h],
                                            WM[:, c * NH + h], start=True, stop=True)
                last.then_inc(S("u"), 1)
                if c >= 2:
                    pe.wait_ge(S("gt_out"), c - 1)
                elif c == 0:
                    pe.wait_ge(S("x_out"), x_done(6 * NC - 1))
                for h in range(NH):
                    i, p0 = h // 2, 64 * (h % 2)
                    last = nc.tensor.matmul(BK8[4 + c % 2][p0:p0 + CH, i * CH:(i + 1) * CH], AVR[0:CH, c, h * CH:(h + 1) * CH],
                                            XT[:, c, h], start=True, stop=True)
                last.then_inc(S("gt"), 1)
                ada(1)
            pe.wait_ge(S("gt_out"), 4)
            pe.wait_ge(S("u_out"), 4)
            for c in range(NC):
                pe.wait_ge(S("state"), c + 1)
                for p in range(2):
                    for i in range(IT):
                        last = nc.tensor.matmul(BK8[p][0:CH, i * CH:(i + 1) * CH], GT[64 * p:64 * p + 64, c, i],
                                                ST[64 * p:64 * p + 64, c, i], start=True, stop=True)
                last.then_inc(S("sa"), 1)
                ada(1)
                pe.wait_ge(S("sa_out"), 2 * c + 2)
                if c < NC - 1:
                    for h in range(NH):
                        i, p0 = h // 2, 64 * (h % 2)
                        last = nc.tensor.matmul(BK8[2][p0:p0 + CH, i * CH:(i + 1) * CH], BKR[:, c, h * CH:(h + 1) * CH],
                                                AVR[:, c, h * CH:(h + 1) * CH], start=True, stop=True)
                    last.then_inc(S("st"), 1)
                for p in range(2):
                    for i in range(IT):
                        h = 2 * i + p
                        y = BK8[(3 if p == 0 else 5) + i // 2][64 * p:64 * p + 64, (i % 2) * ROWS + c * CH:(i % 2) * ROWS + (c + 1) * CH]
                        nc.tensor.matmul(y, ST[64 * p:64 * p + 64, c, i], AR[64 * p:64 * p + 64, i, c, 1], start=True, stop=False)
                        last = nc.tensor.matmul(y, AVR[:, c, h * CH:(h + 1) * CH], TT[:, c, h, CH:2 * CH], start=False, stop=True)
            last.then_inc(S("y"), 1)
            ada(8)
            pe.wait_ge(S("yy_even"), 1)
            stat(YY, 2, "mu")
            spread(STA[:], 3, "mu")
            stat(YS, 2, "var")
            spread(STA[:], 5, "var")
            ada(ADA * 4)
            pe.wait_ge(S("mod_rows"), 1)
            for j in range(4):
                last = nc.tensor.transpose(ADAP[:, j * MODR:(j + 1) * MODR], MROW[:, j * P:(j + 1) * P], con("ident", MODR)[:, 0:MODR])
            last.then_inc(S("mod_tr"), 1)
            pe.wait_ge(S("ya_split"), 1)
            cols("rwkv_proj", [0, 1, 2, 3], lambda k: YA_HI[:, k], lambda k: YA_LO[:, k], ROWS, "oa_out", kt=4, tiles=4)
            pe.wait_ge(S("yb_split"), 1)
            pe.wait_ge(S("oa_out"), 8)
            cols("fox_proj", [4, 5, 6, 0], lambda k: YB_HI[:, k], lambda k: YB_LO[:, k], ROWS, "ob_out", kt=4, tiles=4)
            pe.wait_ge(S("ob_out"), 8)
            pe.wait_ge(S("mod_out"), 1)
            cols("gates", [0, 1, 2, 3], xh, xl, ROWS, "gate_out", behind={2: lambda: norm("nf", NT2)})
            cols("out", [4, 5, 6, 3], lambda k: M_HI[:, k], lambda k: M_LO[:, k], ROWS, "x_out1", first=("m_split", 0),
                 behind={2: lambda: [norm_sum("nc", k) for k in range(3)], 3: lambda: [norm_sum("nc", k) for k in range(3, KT)]})
            ffn(1, "ffn2", 1, "nc", "nd")
            norm("ne")
            ffn(2, "ffn3", 2, "ne", "ng")
            cols("ret_q", [4, 5, 6, 7], xh, xl, ROWS, "rq_out", first=("norm_h", KT * NORM_H["ng"]),
                 behind={0: lambda: norm("nh", NT2)})
            cols("ret_k", [0, 1, 2, 3], lambda k: H_HI[:, :, k], lambda k: H_LO[:, :, k], 512, "rk_out", first=("norm_h", KT * NORM_H["nh"]))
            pe.wait_ge(S("rq_out"), 8)
            pe.wait_ge(S("rk_out"), 8)
            rows("ret_v", 512, 4, [(0, 0), (0, P), (1, 0), (1, P)], [4, 5, 6, 7, 0, 1, 2, 3], "rv_out", 0)
            pe.wait_ge(S("rv_out"), 16)
            for h in range(RH + 1):
                if h < RH:
                    if h >= 1:
                        pe.wait_ge(S("pt_out"), h)
                    for kt in range(4):
                        half, k0 = kt // 2, (kt % 2) * P
                        for d in range(2):
                            last = nc.tensor.matmul(BK8[kt // 2][:, (kt % 2) * ROWS:(kt % 2 + 1) * ROWS],
                                                    RK[:, half, 2 * h + d, k0:k0 + P], RQ[:, 2 * h + d],
                                                    start=(d == 0), stop=(d == 1))
                    last.then_inc(S("rscores"), 1)
                if h >= 1:
                    pe.wait_ge(S("ro_out"), h)
                    for i in range(4):
                        last = nc.tensor.matmul(BK8[6][:, 0:ROWS], con("ones"), RO[:, 4 * (h - 1) + i], start=(i == 0), stop=(i == 3))
                    last.then_inc(S("mean_sum"), 1)
                if h < RH:
                    pe.wait_ge(S("pt_out"), h + 1)
                    for i in range(4):
                        for kt in range(4):
                            last = nc.tensor.matmul(BK8[2 + i // 2][:, (i % 2) * ROWS:(i % 2 + 1) * ROWS],
                                                    RV[:, kt, h * RDV + i * P:h * RDV + (i + 1) * P], PT[:, kt],
                                                    start=(kt == 0), stop=(kt == 3))
                    last.then_inc(S("pv_done"), 1)
                if h >= 1:
                    pe.wait_ge(S("rvar_in"), h)
                    for i in range(4):
                        last = nc.tensor.matmul(BK8[7][:, 0:ROWS], con("ones"), SQ[:, i], start=(i == 0), stop=(i == 3))
                    last.then_inc(S("rvar_sum"), 1)
            pe.wait_ge(S("rn_done"), RH)
            cols("ret_g", [4, 5, 6, 0], xh, xl, ROWS, "rg_out")
            pe.wait_ge(S("rg_out"), 16)
            rows("four_in", 512, 2, [(0, 0), (0, P)], [0, 1, 2, 3], "fx_out", 0)
            pe.wait_ge(S("dft_in"), 16)
            pe.wait_ge(S("fx_out"), 4)
            for g in range(4):
                for t in range(2):
                    q = 2 * g + t
                    if q >= 2:
                        pe.wait_ge(S("zz_out"), q - 1)
                    for k in range(2):
                        last = nc.tensor.matmul(BK8[4 + q % 2][:], FX[:, k, q * P:(q + 1) * P], DFT[:, k], start=(k == 0), stop=(k == 1))
                    last.then_inc(S("zz"), 1)
                pe.wait_ge(S("zz_out"), 2 * g + 2)
                for t in range(2):
                    q = 2 * g + t
                    if q >= 2:
                        pe.wait_ge(S("xm_out"), q - 1)
                    n = 0
                    for part in range(2):
                        for k in range(2):
                            last = nc.tensor.matmul(BK8[q % 2][:, 0:ROWS], DFT[:, k, part * 256 + t * P:part * 256 + (t + 1) * P],
                                                    ZZ[:, g % 2, k, part * ROWS:(part + 1) * ROWS], start=(n == 0), stop=(n == 3))
                            n += 1
                    last.then_inc(S("xm"), 1)
            pe.wait_ge(S("r_split"), 16)
            cols("ret_proj", [2, 3, 6, 7], lambda k: R_HI[:, k], lambda k: R_LO[:, k], ROWS, "or_out", kt=16, tiles=1)
            pe.wait_ge(S("xm_out"), 8)
            pe.wait_ge(S("or_out"), 8)
            cols("four_proj", [4, 5, 0, 1], lambda k: X_HI[:, k], lambda k: X_LO[:, k], ROWS, "of_out")
            cols("gates2", [2, 3, 6, 7], xh, xl, ROWS, "gate2_out")
            pe.wait_ge(S("of_out"), 8)
            cols("out2", [4, 5, 0, 1], lambda k: M2_HI[:, k], lambda k: M2_LO[:, k], ROWS, "x_out2", first=("m2_split", 0),
                 behind={2: lambda: [norm_sum("ni", k) for k in range(3)], 3: lambda: [norm_sum("ni", k) for k in range(3, KT)]})
            ffn(3, "ffn4", 1, "ni", "nj")

        @block.scalar
        def _(act):
            A = nc.scalar.activation

            def square(name, half, k, sem, v, tmp=NT):
                act.wait_ge(S(sem), v)
                A(tmp[:, k], XC[:, half, k], ACT.Square).then_inc(S("norm_sq"), 1)

            def root(name):
                act.wait_ge(S("norm_ssq"), NORM[name] + 1)
                A(STD[:], NORM_BANK[name], ACT.Sqrt, scale=1.0 / DM, bias=par("epsr")).then_inc(S("norm_std"), 1)

            def round_rows(name, half, k, shift=None, tmp=NT):
                act.wait_ge(S("norm_t"), KT * NORM_H[name] + k + 1)
                if shift is None:
                    ins = A(H_HI[:, half, k], tmp[:, k], ACT.Copy)
                else:
                    ins = A(H_HI[:, half, k], tmp[:, k], ACT.Identity, bias=MOD[:, shift[0] + k, shift[1]:shift[1] + 1])
                ins.then_inc(S("norm_hi"), 1)

            def ffn(f, name, halves):
                n = halves * ROWS
                s0 = PHASE[name]

                def silu(t, mark, j=None, j0=0):
                    tt = f * FT + t
                    if tt >= 2:
                        act.wait_ge(S("hid_prod"), tt - 1 if j is None else (j - j0) * 2 + tt - 1)
                    act.wait_ge(psum_ready, mark if j is None else (j - j0) * 12 + mark)
                    A(SILU[:, t % 2, 0:n], BK8[2 * (t % 2)][:, 0:n], ACT.Silu).then_inc(S("silu"), 1)

                m0 = MARK0[s0]
                split_hi(act, s0 + 2)
                silu(0, m0 + 1)
                split_hi(act, s0 + 3)
                silu(1, m0 + 3)

                def body(j, j0, i):
                    s, m = s0 + 2 + 3 * (i - 1), m0 + 4 + 12 * (i - 1)
                    split_hi(act, s + 2, j, j0)
                    split_hi(act, s + 3, j, j0)
                    silu(2 * i, m + 1, j, j0)
                    split_hi(act, s + 4, j, j0)
                    silu(2 * i + 1, m + 11, j, j0)

                with act.Fori(1, 10) as j:
                    body(j, 1, 1)
                body(None, 0, 10)
                split_hi(act, s0 + 34)

            act.wait_ge(S("par_in"), 16)
            act.wait_ge(S("scz_zero"), 1)
            A(SCZ[:, MODR - 2:].rearrange("p (k n) -> p k n", n=MODR)[:, :, 0:2],
              par("c", 0, 16).rearrange("p (k n) -> p k n", n=2), ACT.Silu).then_inc(S("sc_done"), 1)
            for k in range(KT):
                square("na", 0, k, "x_in", 16)
            root("na")
            split_hi(act, 0)
            for k in range(KT):
                round_rows("na", 0, k)
            split_hi(act, 1)
            ffn(0, "ffn1", 1)
            for k in range(KT):
                square("nb", 0, k, "down_added", 80 + k + 1)
            root("nb")
            for k in range(KT):
                round_rows("nb", 0, k)
            s0 = PHASE["rwkv_in"]
            m0 = MARK0[s0]
            for t in range(14):
                if t % 2 == 0:
                    split_hi(act, s0 + t // 2 + 2)
                act.wait_ge(psum_ready, m0 + t + 1)
                A(PRE[:, t, 1:ROWS + 1], BK8[[4, 5, 6, 0][t % 4]][:, 0:ROWS], ACT.Copy).then_inc(S("pre_out"), 1)
            s0 = PHASE["fox_qk"]
            m0 = MARK0[s0]
            for t in range(8):
                if t % 2 == 0:
                    split_hi(act, s0 + t // 2 + 2)
                act.wait_ge(psum_ready, m0 + t + 1)
                A((FQ, FK)[t // 4][:, t % 4], BK8[[4, 5, 6, 0][t % 4]][:, 0:ROWS], ACT.Copy).then_inc(S("fqk_out"), 1)
            s0 = PHASE["fox_v"]
            m0 = MARK0[s0]
            split_hi(act, s0 + 2)
            split_hi(act, s0 + 3)
            for r in range(2):
                act.wait_ge(psum_ready, m0 + 2 + r)
                A(FV[:, r], BK8[1 + r], ACT.Copy).then_inc(S("fv_out"), 1)
            act.wait_ge(S("lor"), 1)
            A(LOR[0:32, 0], LOR[0:32, 0], ACT.Tanh).then_inc(S("lora_act"), 1)
            A(LOR[0:96, 1], LOR[0:96, 1], ACT.Sigmoid).then_inc(S("lora_act"), 1)
            act.wait_ge(S("lora_z"), 1)
            for i in range(IT):
                last = A(SG[:, i], pair(3)[:, i], ACT.Sigmoid, bias=par("w0", i))
            last.then_inc(S("sg_done"), 1)
            act.wait_ge(S("lora_a"), 1)
            for i in range(IT):
                last = A(AA[:, i], pair(5)[:, i], ACT.Sigmoid, bias=par("a0", i))
            last.then_inc(S("aa_done"), 1)
            act.wait_ge(S("lora_g"), 1)
            A(GG[:], pair(0), ACT.Copy).then_inc(S("gg_done"), 1)
            act.wait_ge(S("kk_max"), 1)
            A(STA[:], STA[:], ACT.Sqrt).then_inc(S("kk_rt"), 1)
            act.wait_ge(S("stat_sum"), STAT["fq"] + 1)
            act.wait_ge(S("stat_bc"), STAT["bon"] + 1)
            A(STA[:], BK8[2][0:NH, 0:ROWS], ACT.Sqrt, scale=1.0, bias=par("epsq", 0, 1, NH)).then_inc(S("fq_rt"), 1)
            act.wait_ge(S("stat_sum"), STAT["fk"] + 1)
            act.wait_ge(S("stat_bc"), STAT["fq"] + 1)
            A(STA[:], BK8[2][0:NH, 0:ROWS], ACT.Sqrt, scale=1.0 / 64, bias=par("epsr", 0, 1, NH)).then_inc(S("fk_rt"), 1)
            act.wait_ge(S("f_x"), 1)
            A(F3[:], F1[:], ACT.Abs).then_inc(S("f_act"), 1)
            act.wait_ge(S("f_act"), 1)
            A(F3[:], F3[:], ACT.Exp, scale=-1.0).then_inc(S("f_act"), 1)
            act.wait_ge(S("f_act"), 2)
            A(F3[:], F3[:], ACT.Ln, bias=par("one", 0, 1, NH)).then_inc(S("f_act"), 1)
            act.wait_ge(S("ls_done"), 2)
            A(PC[:], LS[:], ACT.Exp, scale=-DECAY).then_inc(S("ex"), 1)
            act.wait_ge(S("ex"), 1)
            A(LS[:], LS[:], ACT.Exp, scale=DECAY).then_inc(S("ex"), 1)
            A(TMP[:], TMP[:], ACT.Exp, scale=-DECAY).then_inc(S("ex"), 1)
            act.wait_ge(S("ar_a"), 1)
            A(AV[:, :, :, 0], AR[:, :, :, 0], ACT.Copy)
            A(AV[:, :, :, 1], RKV[:, 2].rearrange("p i (c t) -> p i c t", c=NC), ACT.Copy).then_inc(S("av_ready"), 1)
            for q in range(4):
                act.wait_ge(S("ncb"), q + 1)
                A(NCB[:, 2 * q:2 * q + 2], BK8[q % 2].rearrange("p (h n) -> p h n", h=2), ACT.Copy).then_inc(S("ncb_out"), 1)
            for h in range(NH + 2):
                if h < NH:
                    act.wait_ge(S("fmax"), h + 1)
                    for r, (a, b) in enumerate(((0, P), (P, 384))):
                        last = A(SCO[:, h % 2, a:b], SCO[:, h % 2, a:b], ACT.Exp, bias=FST[:, h % 2, r:r + 1],
                                 accum_out=FST[:, h % 2, 2 + r:3 + r])
                    last.then_inc(S("fexp"), 1)
                if 1 <= h <= NH:
                    act.wait_ge(S("prt"), h)
                    if h >= 3:
                        act.wait_ge(S("fox_o"), h - 2)
                    A(PRT[:, (h - 1) % 2], BK8[5 + (h - 1) % 2][:, 0:384], ACT.Copy).then_inc(S("prt_out"), 1)
                if h >= 2:
                    g = h - 2
                    p0 = 64 * (g % 2)
                    act.wait_ge(S("fox_o"), g + 1)
                    if g == 0:
                        act.wait_ge(S("bk_ready"), 1)
                    A(YB[p0:p0 + 64, g // 2], BK8[1 + g % 2][p0:p0 + 64, 0:ROWS], ACT.Copy).then_inc(S("fo_out"), 1)
            for q in range(8):
                act.wait_ge(S("tr"), q + 1)
                A((BKR, AVR)[q % 2][:, q // 2], BK8[q % 2], ACT.Copy).then_inc(S("tr_out"), 1)
            for c in range(NC):
                act.wait_ge(S("w"), c + 1)
                A(WM[:, c * NH:(c + 1) * NH], BK8[c % 2][0:CH].rearrange("p (h n) -> p h n", h=NH), ACT.Copy).then_inc(S("w_out"), 1)
            for c in range(NC):
                act.wait_ge(S("u"), c + 1)
                A(UM[:, c], BK8[2 + c % 2][0:CH].rearrange("p (h n) -> p h n", h=NH), ACT.Copy).then_inc(S("u_out"), 1)
            act.wait_ge(S("y"), 1)
            A(YY[0:CH], pair(3)[0:CH], ACT.Copy).then_inc(S("yy_even"), 1)
            act.wait_ge(S("stat_sum"), STAT["var"] + 1)
            act.wait_ge(S("stat_bc"), STAT["mu"] + 1)
            A(STA[:], BK8[2][0:NH, 0:ROWS], ACT.Sqrt, scale=1.0 / 64, bias=par("epsl", 0, 1, NH)).then_inc(S("var_rt"), 1)
            act.wait_ge(ada_used, ADA)
            A(MROW[:], ADAP[0:MODR], ACT.Copy).then_inc(S("mod_rows"), 1)
            for name, dst, banks, sem in (("rwkv_proj", OA, [0, 1, 2, 3], "oa_out"), ("fox_proj", OB, [4, 5, 6, 0], "ob_out")):
                s0 = PHASE[name]
                m0 = MARK0[s0]
                for t in range(8):
                    if t % 4 == 0:
                        split_hi(act, s0 + t // 4 + 2)
                    act.wait_ge(psum_ready, m0 + t + 1)
                    A(dst[:, t], BK8[banks[t % 4]][:, 0:ROWS], ACT.Copy).then_inc(S(sem), 1)

            def gates(name, dst, banks, out_sem, used_sem, before={}):
                s0 = PHASE[name]
                m0 = MARK0[s0]
                for t in range(16):
                    if t in before:
                        before[t]()
                    if t % 2 == 0:
                        split_hi(act, s0 + t // 2 + 2)
                    if t >= 4:
                        act.wait_ge(S(used_sem), (t - 4) // 2 + 1)
                    act.wait_ge(psum_ready, m0 + t + 1)
                    A(dst[:, t % 4], BK8[banks[t % 4]][:, 0:ROWS], ACT.Sigmoid).then_inc(S(out_sem), 1)

            act.wait_ge(S("mod_out"), 1)
            gates("gates", SGA, [0, 1, 2, 3], "gate_out", "gate_used",
                  before={1: lambda: [square("nf", 1, k, "ctx_in", 16, NT2) for k in range(KT)],
                          7: lambda: root("nf"),
                          10: lambda: [round_rows("nf", 1, k, (0, 1), NT2) for k in range(4)],
                          12: lambda: [round_rows("nf", 1, k, (0, 1), NT2) for k in range(4, KT)]})
            for n in range(4):
                split_hi(act, PHASE["out"] + n + 2)
                if n == 3:
                    for k in range(KT):
                        square("nc", 0, k, "x_out1", k + 1)
            root("nc")
            for k in range(KT):
                round_rows("nc", 0, k)
            ffn(1, "ffn2", 1)
            A(LG[:, 0], par("dec", 0, 8), ACT.Abs).then_inc(S("dec_a"), 1)
            act.wait_ge(S("dec_a"), 1)
            A(LG[:, 0], LG[:, 0], ACT.Exp, scale=-1.0).then_inc(S("dec_a"), 1)
            for k in range(KT):
                square("nd", 0, k, "down_added", 168 + k + 1)
            root("nd")
            for k in range(KT):
                square("ne", 0, k, "nd_x", k + 1)
            root("ne")
            for k in range(KT):
                round_rows("ne", 0, k, (0, 0))
            ffn(2, "ffn3", 2)
            for k in range(KT):
                square("ng", 0, k, "down_added", 256 + k + 1)
            root("ng")
            for k in range(2):
                square("nh", 1, k, "down_added", 256 + k + 1, NT2)
            for k in range(KT):
                round_rows("ng", 0, k, (24, 0))
                if k < 6:
                    square("nh", 1, k + 2, "down_added", 256 + k + 3, NT2)
            s0 = PHASE["ret_q"]
            split_hi(act, s0 + 2)
            root("nh")
            split_hi(act, s0 + 3)
            for k in range(KT):
                round_rows("nh", 1, k, (24, 1), NT2)
            split_hi(act, s0 + 4)
            split_hi(act, s0 + 5)
            s0 = PHASE["ret_k"]
            for h in range(RH):
                split_hi(act, s0 + h + 2)
                for w in range(2):
                    act.wait_ge(S("rk_x"), 2 * h + w + 1)
                    A(RK[:, 1, 2 * h + w], BK8[(2 * h + w) % 4][:, ROWS:512], ACT.Copy).then_inc(S("rk_out"), 1)
            s0 = PHASE["ret_v"]
            for q in range(4):
                split_hi(act, s0 + 2 * q + 2)
                split_hi(act, s0 + 2 * q + 3)
                for r in range(4):
                    act.wait_ge(psum_ready, MARK0[s0 + 2 * q + 1] + r + 1)
                    A(RV[:, r, 512 * q:512 * (q + 1)], BK8[[4, 5, 6, 7, 0, 1, 2, 3][(4 * q + r) % 8]], ACT.Copy).then_inc(S("rv_out"), 1)
            for h in range(RH + 1):
                if h < RH:
                    act.wait_ge(S("d_arg"), h + 1)
                    A(DD[:, 0:2], DD[:, 0:2], ACT.Exp)
                    for kt in range(2):
                        A(DD[:, 2 + kt], IOTA[:], ACT.Exp, scale=LG[:, 4, h:h + 1], bias=LB[:, h, kt:kt + 1])
                        last = A(EB[:, kt], IOTA[:], ACT.Exp, scale=LG[:, 3, 4 + h:5 + h], bias=LB[:, h, 2 + kt:3 + kt])
                    last.then_inc(S("d_exp"), 1)
                if h >= 1:
                    act.wait_ge(S("ro_c"), h)
                    A(SQ[:], RO[:, 4 * (h - 1):4 * h], ACT.Square).then_inc(S("rvar_in"), 1)
                if h < RH:
                    act.wait_ge(S("pv_done"), h + 1)
                    A(RO[:, 4 * h:4 * h + 4], pair(2), ACT.Copy).then_inc(S("ro_out"), 1)
                if h >= 1:
                    act.wait_ge(S("rvar_sum"), h)
                    if h >= 2:
                        act.wait_ge(S("rn_rec"), h - 1)
                    A(RST[:, 0], BK8[7][:, 0:ROWS], ACT.Sqrt, scale=1.0 / RDV, bias=par("epsr")).then_inc(S("rvar_rt"), 1)
            s0 = PHASE["ret_g"]
            m0 = MARK0[s0]
            for t in range(16):
                if t % 2 == 0:
                    split_hi(act, s0 + t // 2 + 2)
                if t >= 2:
                    act.wait_ge(S("rg_used"), t - 1)
                act.wait_ge(psum_ready, m0 + t + 1)
                A(SGG[:, t % 2], BK8[[4, 5, 6, 0][t % 4]][:, 0:ROWS], ACT.Silu).then_inc(S("rg_out"), 1)
            s0 = PHASE["four_in"]
            for q in range(2):
                split_hi(act, s0 + 2 * q + 2)
                split_hi(act, s0 + 2 * q + 3)
                for r in range(2):
                    act.wait_ge(psum_ready, MARK0[s0 + 2 * q + 1] + r + 1)
                    A(FX[:, r, 512 * q:512 * (q + 1)], BK8[2 * q + r], ACT.Copy).then_inc(S("fx_out"), 1)
            for q in range(8):
                act.wait_ge(S("zz"), q + 1)
                if q >= 4:
                    act.wait_ge(S("xm"), 2 * (q // 2) - 2)
                A(ZZ[:, (q // 2) % 2, q % 2, 0:ROWS], BK8[4 + q % 2][:, 0:ROWS], ACT.Copy)
                A(ZZ[:, (q // 2) % 2, q % 2, ROWS:512], BK8[4 + q % 2][:, ROWS:512], ACT.Copy, scale=-1.0).then_inc(S("zz_out"), 1)
            s0 = PHASE["ret_proj"]
            for t in range(8):
                split_hi(act, s0 + t + 2)
                act.wait_ge(psum_ready, MARK0[s0] + t + 1)
                A(OR[:, t], BK8[[2, 3, 6, 7][t % 4]][:, 0:ROWS], ACT.Copy).then_inc(S("or_out"), 1)
            s0 = PHASE["four_proj"]
            for t in range(8):
                if t % 2 == 0:
                    split_hi(act, s0 + t // 2 + 2)
                act.wait_ge(psum_ready, MARK0[s0] + t + 1)
                A(OF[:, t], BK8[[4, 5, 0, 1][t % 4]][:, 0:ROWS], ACT.Copy).then_inc(S("of_out"), 1)
            gates("gates2", SG2, [2, 3, 6, 7], "gate2_out", "gate2_used")
            for s in range(PHASE["out2"], PHASE["out2"] + 4):
                split_hi(act, s + 2)
            for k in range(KT):
                square("ni", 0, k, "x_out2", k + 1)
            root("ni")
            for k in range(KT):
                round_rows("ni", 0, k, (48, 0))
            ffn(3, "ffn4", 1)
            for k in range(KT):
                square("nj", 0, k, "down_added", 344 + k + 1)
            root("nj")

        @block.vector
        def _(dve):
            V = nc.vector
            count = [0]

            def link(ins):
                count[0] += 1
                ins.then_inc(S("dve_link"), 1)
                dve.wait_ge(S("dve_link"), count[0])

            def scale(name, half, k, gain, dst, sem="norm_t"):
                V.scalar_tensor_tensor(out=dst[:, k], in0=XC[:, half, k], scalar=gain(k), in1=RSTD[:],
                                       op0=ALU.mult, op1=ALU.mult).then_inc(S(sem), 1)

            def rest(name, half, k, shift=None, tmp=NT):
                dve.wait_ge(S("norm_hi"), KT * NORM_H[name] + k + 1)
                hi = H_HI[:, half, k].bitcast(F32)
                if shift is None:
                    ins = V.tensor_tensor(H_LO[:, half, k], tmp[:, k], hi, ALU.subtract)
                else:
                    ins = V.scalar_tensor_tensor(out=H_LO[:, half, k], in0=tmp[:, k], scalar=MOD[:, shift[0] + k, shift[1]:shift[1] + 1],
                                                 in1=hi, op0=ALU.add, op1=ALU.subtract)
                ins.then_inc(S("norm_h"), 1)

            def reciprocal(name):
                dve.wait_ge(S("norm_std"), NORM[name] + 1)
                link(V.reciprocal(RSTD[:], STD[:]))

            def norm(name, half, gain, shift=None, tmp=NT):
                reciprocal(name)
                for k in range(KT + 2):
                    if k < KT:
                        scale(name, half, k, gain, tmp)
                    if k >= 2:
                        rest(name, half, k - 2, shift, tmp)

            def ffn(f, name, halves, gate):
                n = halves * ROWS
                s0 = PHASE[name]
                m0 = MARK0[s0]

                def hidden(t, mark, dmark, j=None, j0=0):
                    tt = f * FT + t
                    x = (lambda a, m: a if j is None else (j - j0) * m + a)
                    dve.wait_ge(S("silu"), x(tt + 1, 2))
                    dve.wait_ge(psum_ready, x(mark, 12))
                    V.tensor_tensor(PROD[:, t % 2, 0:n], SILU[:, t % 2, 0:n], BK8[2 * (t % 2) + 1][:, 0:n],
                                    ALU.mult).then_inc(S("hid_prod"), 1)
                    dve.wait_ge(S("hid_prod"), x(tt + 1, 2))
                    if dmark is not None:
                        dve.wait_ge(psum_ready, x(dmark, 12))
                    V.tensor_copy(HID_HI[:, t % 2, 0:n], PROD[:, t % 2, 0:n]).then_inc(S("hid_hi"), 1)
                    dve.wait_ge(S("hid_hi"), x(tt + 1, 2))
                    V.tensor_tensor(HID_LO[:, t % 2, 0:n], PROD[:, t % 2, 0:n], HID_HI[:, t % 2, 0:n].bitcast(F32),
                                    ALU.subtract).then_inc(S("hid_lo"), 1)

                def add(i, ms, mark, j=None, j0=0):
                    for m in ms:
                        d = f * 88 + 8 * i + m
                        if m == 0 and d > 0:
                            dve.wait_ge(S("down_added"), d if j is None else (j - j0) * 8 + d)
                        dve.wait_ge(psum_ready, mark + m + 1 if j is None else (j - j0) * 12 + mark + m + 1)
                        for h in range(halves):
                            last = V.scalar_tensor_tensor(out=XC[:, h, m], in0=BK8[4 + m % 4][:, h * ROWS:(h + 1) * ROWS],
                                                          scalar=gate(h, m), in1=XC[:, h, m], op0=ALU.mult, op1=ALU.add)
                        last.then_inc(S("down_added"), 1)

                split_lo(dve, s0 + 2)
                hidden(0, m0 + 2, m0 if f else None)
                split_lo(dve, s0 + 3)

                def body(j, j0, i):
                    s, m = s0 + 2 + 3 * (i - 1), m0 + 4 + 12 * (i - 1)
                    hidden(2 * i - 1, m, m - 2, j, j0)
                    split_lo(dve, s + 2, j, j0)
                    add(i - 1, range(0, 4), m + 2, j, j0)
                    split_lo(dve, s + 3, j, j0)
                    add(i - 1, range(4, 8), m + 2, j, j0)
                    hidden(2 * i, m + 2, m + 10, j, j0)
                    split_lo(dve, s + 4, j, j0)

                with dve.Fori(1, 10) as j:
                    body(j, 1, 1)
                body(None, 0, 10)
                hidden(21, m0 + 124, m0 + 122)
                split_lo(dve, s0 + 34)
                add(10, range(8), m0 + 124)

            half_ = (lambda h, m: 0.5)
            V.memset(SCZ[:], 0.0).then_inc(S("scz_zero"), 1)
            V.memset(PRE[:, :, 0:1], 0.0)
            dve.wait_ge(S("par_in"), 16)
            dve.wait_ge(S("con_in"), 16)
            reciprocal("na")
            for k in range(KT):
                scale("na", 0, k, lambda k: par("n1", k), NT)
            split_lo(dve, 0)
            for k in range(KT):
                rest("na", 0, k)
            split_lo(dve, 1)
            ffn(0, "ffn1", 1, half_)
            norm("nb", 0, lambda k: par("nm", k))

            def shift(dst, t0, nt):
                cur, prev = PRE[:, t0:t0 + nt, 1:ROWS + 1], PRE[:, t0:t0 + nt, 0:ROWS]
                link(V.tensor_tensor(TMP[:, 0:nt], prev, cur, ALU.subtract))
                for t in range(nt):
                    last = V.scalar_tensor_tensor(out=dst[:, t], in0=TMP[:, t], scalar=par("mu", t0 + t), in1=cur[:, t],
                                                  op0=ALU.mult, op1=ALU.add)
                if dst is LOR:
                    last.then_inc(S("lor"), 1)
                    dve.wait_ge(S("lor"), 1)
                else:
                    link(last)

            s0 = PHASE["rwkv_in"]
            for u in range(7):
                split_lo(dve, s0 + u + 2)
                if u in (1, 3, 5, 6):
                    dve.wait_ge(S("pre_out"), 2 * u + 2)
                    if u < 6:
                        shift(RKV[:, u // 2], 2 * u - 2, 4)
                    else:
                        shift(LOR, 12, 2)
            R_, K_, V_ = RKV[:, 0], RKV[:, 1], RKV[:, 2]
            s0 = PHASE["fox_qk"]
            for u in range(4):
                split_lo(dve, s0 + u + 2)
                if u == 1:
                    for i in range(IT):
                        last = V.tensor_scalar(KK[:, i], K_[:, i], par("kk", i), None, ALU.mult)
                    link(last)
                    V.tensor_tensor(TMP[:], KK[:], KK[:], ALU.mult).then_inc(S("stat_in"), 1)
            s0 = PHASE["fox_v"]
            split_lo(dve, s0 + 2)
            split_lo(dve, s0 + 3)
            dve.wait_ge(S("stat_sum"), STAT["kk"] + 1)
            V.tensor_scalar(STA[:], BK8[2][0:NH, 0:ROWS], 1e-24, None, ALU.max).then_inc(S("kk_max"), 1)
            dve.wait_ge(S("aa_done"), 1)
            for i in range(IT):
                last = V.tensor_scalar(TMP[:, i], AA[:, i], 1.0, par("ka", i), ALU.subtract, ALU.mult)
            link(last)
            link(V.scalar_tensor_tensor(out=K_, in0=TMP[:], scalar=1.0, in1=K_, op0=ALU.add, op1=ALU.mult))
            for i in range(IT):
                last = V.scalar_tensor_tensor(out=TMP[:, i], in0=R_[:, i], scalar=par("rk", i), in1=K_[:, i],
                                              op0=ALU.mult, op1=ALU.mult)
            last.then_inc(S("stat_in"), 1)
            dve.wait_ge(S("kk_rt"), 1)
            V.reciprocal(STA[:], STA[:]).then_inc(S("stat_st"), 1)
            dve.wait_ge(S("stat_bc"), STAT["kk"] + 1)
            link(V.tensor_tensor(KK[:], KK[:], pair(3), ALU.mult))
            dve.wait_ge(S("stat_sum"), STAT["bon"] + 1)
            V.tensor_copy(STA[:], BK8[2][0:NH, 0:ROWS]).then_inc(S("stat_st"), 1)
            dve.wait_ge(S("gg_done"), 1)
            dve.wait_ge(S("stat_bc"), STAT["bon"] + 1)
            link(V.tensor_tensor(BO[:], V_, pair(5), ALU.mult))
            dve.wait_ge(S("fqk_out"), 8)
            for name, X, g in (("fq", FQ, "qn"), ("fk", FK, "kn")):
                V.tensor_tensor(TMP[:], X[:], X[:], ALU.mult).then_inc(S("stat_in"), 1)
                dve.wait_ge(S(f"{name}_rt"), 1)
                V.reciprocal(STA[:], STA[:]).then_inc(S("stat_st"), 1)
                dve.wait_ge(S("stat_bc"), STAT[name] + 1)
                V.scalar_tensor_tensor(out=X[:], in0=pair(3 if name == "fq" else 5), scalar=par(g), in1=X[:],
                                       op0=ALU.mult, op1=ALU.mult).then_inc(S(f"{name}_norm"), 1)
            dve.wait_ge(S("lora_g"), 1)
            link(V.tensor_scalar(F1[:], LOR[96:96 + NH, 1], par("fb")[96:96 + NH], None, ALU.add))
            V.tensor_scalar(F2[:], F1[:], 0.0, None, ALU.min).then_inc(S("f_x"), 1)
            link(V.memset(F4[:], 1.0))
            dve.wait_ge(S("sg_done"), 1)
            for i in range(IT):
                for c in range(0, ROWS, CH):
                    last = V.tensor_tensor_scan(LS[:, i, c:c + CH], con("ones")[:, 0:CH], SG[:, i, c:c + CH], 0.0, ALU.mult, ALU.add)
            last.then_inc(S("ls_done"), 1)
            dve.wait_ge(S("ls_done"), 1)
            V.tensor_tensor(TMP[:], LS[:], SG[:], ALU.subtract).then_inc(S("ls_done"), 1)
            dve.wait_ge(S("f_act"), 3)
            link(V.tensor_tensor(F3[:], F3[:], F2[:], ALU.subtract))
            V.tensor_tensor_scan(STB[:], F4[:], F3[:], 0.0, ALU.mult, ALU.add).then_inc(S("lf_cum"), 1)
            by_chunk = (lambda x: x.rearrange("p i (c t) -> p i c t", c=NC))
            dve.wait_ge(S("ex"), 3)
            V.scalar_tensor_tensor(out=AR[:, :, :, 0], in0=by_chunk(KK[:]), scalar=-1.0, in1=by_chunk(TMP[:]),
                                   op0=ALU.mult, op1=ALU.mult).then_inc(S("ar_a"), 1)
            V.tensor_tensor(AR[:, :, :, 1], by_chunk(R_), by_chunk(PC[:]), ALU.mult)
            V.tensor_tensor(BK[:, :, :, 1], by_chunk(K_), by_chunk(LS[:]), ALU.mult)
            link(V.tensor_tensor(KK[:], KK[:], AA[:], ALU.mult))
            V.tensor_tensor(BK[:, :, :, 0], by_chunk(KK[:]), by_chunk(LS[:]), ALU.mult).then_inc(S("bk_ready"), 1)
            diag = (lambda h: SCO[:, h % 2].rearrange("p (b n) -> p b n", n=P)[:, 0:3:2])
            for h in range(NH + 1):
                if h < NH:
                    dve.wait_ge(S("scores"), h + 1)
                    if h < 8 and h % 2 == 0:
                        dve.wait_ge(S("ncb_out"), h // 2 + 1)
                    if h >= 2:
                        dve.wait_ge(S("prt"), h - 1)
                    b = BK8[3 + h % 2]
                    V.tensor_tensor(SCO[:, h % 2, 0:P], b[:, 0:P], NCB[:, h, 0:P], ALU.add)
                    V.tensor_tensor(SCO[:, h % 2, P:384], b[:, P:384], NCB[:, h], ALU.add).then_inc(S("sco_out"), 1)
                    dve.wait_ge(S("sco_out"), h + 1)
                    link(V.tensor_tensor(diag(h), diag(h), con("causal").unsqueeze(1).to_broadcast([P, 2, P]), ALU.add))
                    V.tensor_reduce(FST[:, h % 2, 0:1], SCO[:, h % 2, 0:P], AX_X, ALU.max, negate=True)
                    V.tensor_reduce(FST[:, h % 2, 1:2], SCO[:, h % 2, P:384], AX_X, ALU.max, negate=True).then_inc(S("fmax"), 1)
                if h >= 1:
                    g = (h - 1) % 2
                    dve.wait_ge(S("fexp"), h)
                    link(V.reciprocal(FST[:, g, 4:6], FST[:, g, 2:4]))
                    V.tensor_scalar(SCO[:, g, 0:P], SCO[:, g, 0:P], FST[:, g, 4:5], None, ALU.mult)
                    V.tensor_scalar(SCO[:, g, P:384], SCO[:, g, P:384], FST[:, g, 5:6], None, ALU.mult).then_inc(S("probs"), 1)
            for q in range(8):
                c, p = q // 2, q % 2
                dve.wait_ge(S("tt"), q + 1)
                V.tensor_tensor(TT[:, c].rearrange("p (i q) n -> p i q n", q=2)[:, :, p],
                                BK8[2 + q % 4].rearrange("p (i n) -> p i n", n=P),
                                con("tmask").unsqueeze(1).to_broadcast([P, IT, P]), ALU.mult).then_inc(S("tt_out"), 1)
            dve.wait_ge(S("tt_out"), 8)
            eye = con("ident", CH)[:, 0:CH].unsqueeze(1).to_broadcast([CH, NH, CH])
            heads = (lambda b: BK8[b][0:CH].rearrange("p (h n) -> p h n", n=CH))
            lmask = (lambda lev: con("lmask", CH)[:, lev * CH:(lev + 1) * CH].unsqueeze(1).to_broadcast([CH, NH, CH]))
            link(V.tensor_tensor(XT[:].rearrange("p c h n -> p (c h) n"), TT[0:CH, :, :, 0:CH].rearrange("p c h n -> p (c h) n"),
                                 con("l0t", CH).unsqueeze(1).to_broadcast([CH, NC * NH, CH]), ALU.mult))
            for n in range(NC):
                dve.wait_ge(S("z"), n + 1)
                V.tensor_tensor(XM[:, n], heads(n % 2), lmask(0), ALU.mult).then_inc(S("z_out"), 1)
                V.tensor_tensor(XT[:, n], XT[:, n], eye, ALU.add).then_inc(S("x_out"), 1)
                dve.wait_ge(S("z_out"), n + 1)
                V.tensor_tensor(XM[:, n], XM[:, n], eye, ALU.add).then_inc(S("x_out"), 1)

            def z_mask(n):
                dve.wait_ge(S("z"), n + 1)
                V.tensor_tensor(ZM[:, n % NC], heads(n % 2), lmask(n // NC), ALU.mult).then_inc(S("z_out"), 1)

            z_mask(NC)
            z_mask(NC + 1)
            for n in range(NC, 6 * NC):
                c = n % NC
                if n < 5 * NC:
                    dve.wait_ge(S("xz"), n - NC + 1)
                    V.tensor_tensor(XM[:, c], XM[:, c], heads(2 + n % 2), ALU.add).then_inc(S("x_out"), 1)
                dve.wait_ge(S("zx"), n - NC + 1)
                V.tensor_tensor(XT[:, c], XT[:, c], heads(4 + n % 2), ALU.add).then_inc(S("x_out"), 1)
                if n + 2 < 6 * NC:
                    z_mask(n + 2)
            dve.wait_ge(S("x_out"), 11 * NC)
            V.memset(ST[:, 0], 0.0).then_inc(S("state"), 1)
            for c in range(NC):
                dve.wait_ge(S("gt"), c + 1)
                V.tensor_copy(GT[:, c], BK8[4 + c % 2][:, 0:256].rearrange("p (i n) -> p i n", n=CH)).then_inc(S("gt_out"), 1)
            dve.wait_ge(S("u_out"), 4)
            for c in range(NC):
                dve.wait_ge(S("sa"), c + 1)
                for p in range(2):
                    V.tensor_tensor(AVR[0:CH, c].rearrange("p (i q v) -> p i q v", q=2, v=CH)[:, :, p],
                                    BK8[p][0:CH, 0:256].rearrange("p (i v) -> p i v", v=CH),
                                    UM[:, c].rearrange("p (i q) v -> p i q v", q=2)[:, :, p], ALU.add).then_inc(S("sa_out"), 1)
                if c < NC - 1:
                    dve.wait_ge(S("st"), c + 1)
                    link(V.tensor_tensor(ST[:, c + 1], BK8[2][:, 0:256].rearrange("p (i v) -> p i v", v=CH), ST[:, c], ALU.add))
                    pc = PC[:].rearrange("p i (c t) -> p i c t", c=NC)[:, :, c, CH - 1:CH].to_broadcast([P, IT, CH])
                    V.tensor_tensor(ST[:, c + 1], ST[:, c + 1], pc, ALU.mult).then_inc(S("state"), 1)
            dve.wait_ge(S("y"), 1)
            V.tensor_copy(YY[CH:P], pair(5)[CH:P]).then_inc(S("stat_in"), 1)
            dve.wait_ge(S("stat_sum"), STAT["mu"] + 1)
            V.tensor_scalar(STA[:], BK8[2][0:NH, 0:ROWS], 1.0 / CH, None, ALU.mult).then_inc(S("stat_st"), 1)
            dve.wait_ge(S("stat_bc"), STAT["mu"] + 1)
            link(V.tensor_tensor(YY[:], YY[:], pair(3), ALU.subtract))
            V.tensor_tensor(YS[:], YY[:], YY[:], ALU.mult).then_inc(S("stat_in"), 1)
            dve.wait_ge(S("var_rt"), 1)
            V.reciprocal(STA[:], STA[:]).then_inc(S("stat_st"), 1)
            dve.wait_ge(S("stat_bc"), STAT["var"] + 1)
            link(V.tensor_tensor(YY[:], YY[:], pair(5), ALU.mult))
            for i in range(IT):
                last = V.tensor_scalar(YY[:, i], YY[:, i], par("lnxg", i), par("lnxb", i), ALU.mult, ALU.add)
            link(last)
            link(V.tensor_tensor(YY[:], YY[:], BO[:], ALU.add))
            link(V.tensor_tensor(YY[:], YY[:], GG[:], ALU.mult))
            link(V.tensor_copy(YA_HI[:], YY[:]))
            V.tensor_tensor(YA_LO[:], YY[:], YA_HI[:].bitcast(F32), ALU.subtract).then_inc(S("ya_split"), 1)
            link(V.tensor_copy(YB_HI[:], YB[:]))
            V.tensor_tensor(YB_LO[:], YB[:], YB_HI[:].bitcast(F32), ALU.subtract).then_inc(S("yb_split"), 1)
            for name in ("rwkv_proj", "fox_proj"):
                for u in range(2):
                    split_lo(dve, PHASE[name] + u + 2)

            dve.wait_ge(S("mod_tr"), 1)
            dve.wait_ge(S("bada_in"), 16)
            link(V.tensor_tensor(MOD[:].rearrange("p (q j) n -> p j q n", j=4), MOD[:].rearrange("p (q j) n -> p j q n", j=4),
                                 ADAP[:, 0:4 * MODR].rearrange("p (j q n) -> p j q n", j=4, n=2), ALU.add))
            for g, (chunk, who, m) in enumerate(((1, 0, "m1"), (1, 1, "m1"), (4, 0, "m2"), (4, 1, "m2"), (7, 0, "m3"))):
                V.scalar_tensor_tensor(out=GAIN[:, g], in0=MOD[:, 8 * chunk:8 * chunk + 8, who], scalar=1.0, in1=par(m, 0, 8),
                                       op0=ALU.add, op1=ALU.mult)
            for g, (chunk, who, f) in enumerate(((2, 0, 0.5), (2, 1, 0.5), (5, 0, 1.0), (8, 0, 0.5))):
                last = V.tensor_scalar(GATE[:, g], MOD[:, 8 * chunk:8 * chunk + 8, who], f, None, ALU.mult)
            last.then_inc(S("mod_out"), 1)
            dve.wait_ge(S("mod_out"), 1)

            def gates(name, sg, mt, oa, ob, hi, lo, out_sem, used_sem, split_sem, oa_sem, ob_sem, behind={}):
                s0 = PHASE[name]
                dve.wait_ge(S(oa_sem), 8)
                dve.wait_ge(S(ob_sem), 8)
                for m in range(KT):
                    split_lo(dve, s0 + m + 2)
                    dve.wait_ge(S(out_sem), 2 * m + 2)
                    w = mt[:, m % 2]
                    V.tensor_tensor(w[:, 0], sg[:, (2 * m) % 4], oa[:, m], ALU.mult)
                    V.tensor_tensor(w[:, 1], sg[:, (2 * m + 1) % 4], ob[:, m], ALU.mult).then_inc(S(used_sem), 1)
                    dve.wait_ge(S(used_sem), m + 1)
                    link(V.tensor_tensor(w[:, 2], w[:, 0], w[:, 1], ALU.add))
                    link(V.tensor_copy(hi[:, m], w[:, 2]))
                    last = V.tensor_tensor(lo[:, m], w[:, 2], hi[:, m].bitcast(F32), ALU.subtract)
                    last.then_inc(S(split_sem), 1)
                    if m in behind:
                        behind[m]()

            def out_add(name, banks, gate, sem):
                s0 = PHASE[name]
                for m in range(KT):
                    if m % 2 == 0:
                        split_lo(dve, s0 + m // 2 + 2)
                    dve.wait_ge(psum_ready, MARK0[s0] + m + 1)
                    V.scalar_tensor_tensor(out=XC[:, 0, m], in0=BK8[banks[m % 4]][:, 0:ROWS], scalar=gate(m), in1=XC[:, 0, m],
                                           op0=ALU.mult, op1=ALU.add).then_inc(S(sem), 1)

            gates("gates", SGA, MT, OA, OB, M_HI, M_LO, "gate_out", "gate_used", "m_split", "oa_out", "ob_out",
                  behind={3: lambda: [reciprocal("nf")] + [scale("nf", 1, k, lambda k: GAIN[:, 1, k:k + 1], NT2) for k in range(4)],
                          4: lambda: [scale("nf", 1, k, lambda k: GAIN[:, 1, k:k + 1], NT2) for k in range(4, KT)],
                          5: lambda: [rest("nf", 1, k, (0, 1), NT2) for k in range(4)],
                          6: lambda: [rest("nf", 1, k, (0, 1), NT2) for k in range(4, KT)]})
            out_add("out", [4, 5, 6, 3], lambda m: 1.0, "x_out1")
            norm("nc", 0, lambda k: par("n2", k))
            ffn(1, "ffn2", 1, half_)
            dve.wait_ge(S("dec_a"), 2)
            link(V.tensor_scalar(LG[:, 1], LG[:, 0], 2.0, None, ALU.add))
            link(V.reciprocal(LG[:, 1], LG[:, 1]))
            link(V.tensor_tensor(LG[:, 0], LG[:, 0], LG[:, 1], ALU.mult))
            link(V.tensor_tensor(LG[:, 1], LG[:, 0], LG[:, 0], ALU.mult))
            link(V.tensor_scalar(LG[:, 2], LG[:, 1], 1.0 / 17, None, ALU.mult))
            for n in (15, 13, 11, 9, 7, 5, 3):
                link(V.scalar_tensor_tensor(out=LG[:, 2], in0=LG[:, 2], scalar=1.0 / n, in1=LG[:, 1], op0=ALU.add, op1=ALU.mult))
            link(V.scalar_tensor_tensor(out=LG[:, 2], in0=LG[:, 2], scalar=1.0, in1=LG[:, 0], op0=ALU.add, op1=ALU.mult))
            link(V.tensor_scalar(LG[:, 1], par("dec", 0, 8), 0.0, None, ALU.min))
            link(V.scalar_tensor_tensor(out=LG[:, 4], in0=LG[:, 2], scalar=-2.0, in1=LG[:, 1], op0=ALU.mult, op1=ALU.add))
            link(V.tensor_scalar(LG[:, 3], LG[:, 4], -1.0, None, ALU.mult))
            for h in range(RH):
                V.tensor_scalar(LB[:, h, 0:2], par("jcol", 2, 2), LG[:, 4, h:h + 1], None, ALU.mult)
                last = V.tensor_scalar(LB[:, h, 2:4], par("jcol", 4, 2), LG[:, 4, 4 + h:5 + h], None, ALU.mult)
            link(last)
            reciprocal("nd")
            for k in range(KT):
                scale("nd", 0, k, lambda k: par("nf", k), XC[:, 0], "nd_x")
            norm("ne", 0, lambda k: GAIN[:, 0, k:k + 1], (0, 0))
            ffn(2, "ffn3", 2, lambda h, m: GATE[:, h, m:m + 1])
            norm("ng", 0, lambda k: GAIN[:, 2, k:k + 1], (24, 0))
            split_lo(dve, PHASE["ret_q"] + 2)
            norm("nh", 1, lambda k: GAIN[:, 3, k:k + 1], (24, 1), NT2)
            split_lo(dve, PHASE["ret_q"] + 3)

            def rotate(ps_e, ps_o, dst, h, sem):
                link(V.tensor_tensor(RT[:, 0], ps_e, ROPE[:, 0], ALU.mult))
                V.tensor_tensor(RT[:, 2], ps_e, ROPE[:, 1], ALU.mult).then_inc(S(sem), 1)
                link(V.tensor_tensor(RT[:, 1], ps_o, ROPE[:, 1], ALU.mult))
                V.tensor_tensor(RT[:, 3], ps_o, ROPE[:, 0], ALU.mult).then_inc(S(sem), 1)
                dve.wait_ge(S(sem), 2 * h + 2)
                V.tensor_tensor(dst[:, 2 * h], RT[:, 0], RT[:, 1], ALU.subtract)
                link(V.tensor_tensor(dst[:, 2 * h + 1], RT[:, 2], RT[:, 3], ALU.add))

            dve.wait_ge(S("rope_in"), 16)
            s0 = PHASE["ret_q"]
            for h in range(RH):
                if h >= 2:
                    split_lo(dve, s0 + h + 2)
                dve.wait_ge(psum_ready, MARK0[s0] + 2 * h + 2)
                rotate(BK8[4 + (2 * h) % 4][:, 0:ROWS], BK8[4 + (2 * h + 1) % 4][:, 0:ROWS], RQ, h, "rq_out")
            s0 = PHASE["ret_k"]
            for h in range(RH):
                split_lo(dve, s0 + h + 2)
                dve.wait_ge(psum_ready, MARK0[s0] + 2 * h + 2)
                rotate(BK8[(2 * h) % 4][:, 0:ROWS], BK8[(2 * h + 1) % 4][:, 0:ROWS], RK[:, 0], h, "rk_x")
            for s in range(PHASE["ret_v"], PHASE["ret_v"] + 8):
                split_lo(dve, s + 2)
            dve.wait_ge(S("iota_in"), 16)
            for kt in range(2):
                V.tensor_scalar(T1[:, kt], IOTA[:], par("jcol", kt), 0.0, ALU.subtract, ALU.max)
                last = V.tensor_scalar(T2[:, kt], IOTA[:], par("jcol", kt), 0.0, ALU.subtract, ALU.min)
            link(last)

            def decay_arg(h):
                link(V.tensor_scalar(DD[:, 0:2], T1[:], LG[:, 4, h:h + 1], None, ALU.mult))
                V.scalar_tensor_tensor(out=DD[:, 0:2], in0=T2[:], scalar=LG[:, 3, 4 + h:5 + h], in1=DD[:, 0:2],
                                       op0=ALU.mult, op1=ALU.add).then_inc(S("d_arg"), 1)

            decay_arg(0)
            for h in range(RH + 1):
                if h < RH:
                    dve.wait_ge(S("d_exp"), h + 1)
                    V.tensor_tensor(DD[:, 2:4], DD[:, 2:4], EB[:], ALU.add)
                    for kt in range(2):
                        blk = DD[:, kt, kt * P:(kt + 1) * P]
                        last = V.tensor_tensor(blk, blk, con("ident"), ALU.add)
                    link(last)
                    dve.wait_ge(S("rscores"), h + 1)
                    if h >= 1:
                        dve.wait_ge(S("pv_done"), h)
                    V.scalar_tensor_tensor(out=PT[:], in0=pair(0), scalar=1.0 / 16, in1=DD[:], op0=ALU.mult, op1=ALU.mult)\
                        .then_inc(S("pt_out"), 1)
                    dve.wait_ge(S("pt_out"), h + 1)
                if h >= 1:
                    g = h - 1
                    dve.wait_ge(S("mean_sum"), h)
                    ro = RO[:, 4 * g:4 * g + 4]
                    V.scalar_tensor_tensor(out=ro, in0=BK8[6][:, 0:ROWS].unsqueeze(1).to_broadcast([P, 4, ROWS]), scalar=-1.0 / RDV,
                                           in1=ro, op0=ALU.mult, op1=ALU.add).then_inc(S("ro_c"), 1)
                    dve.wait_ge(S("ro_c"), h)
                if h < RH - 1:
                    decay_arg(h + 1)
                if h >= 1:
                    dve.wait_ge(S("rvar_rt"), h)
                    V.reciprocal(RST[:, 1], RST[:, 0]).then_inc(S("rn_rec"), 1)
                    dve.wait_ge(S("rn_rec"), h)
                    V.tensor_tensor(ro, ro, RST[:, 1].unsqueeze(1).to_broadcast([P, 4, ROWS]), ALU.mult).then_inc(S("rn_done"), 1)
            dve.wait_ge(S("rn_done"), RH)
            s0 = PHASE["ret_g"]
            for t in range(16):
                if t % 2 == 0:
                    split_lo(dve, s0 + t // 2 + 2)
                dve.wait_ge(S("rg_out"), t + 1)
                V.scalar_tensor_tensor(out=RO[:, t], in0=SGG[:, t % 2], scalar=par("gn", t), in1=RO[:, t],
                                       op0=ALU.mult, op1=ALU.mult).then_inc(S("rg_used"), 1)
                dve.wait_ge(S("rg_used"), t + 1)
                link(V.tensor_copy(R_HI[:, t], RO[:, t]))
                V.tensor_tensor(R_LO[:, t], RO[:, t], R_HI[:, t].bitcast(F32), ALU.subtract).then_inc(S("r_split"), 1)
            for s in range(PHASE["four_in"], PHASE["four_in"] + 4):
                split_lo(dve, s + 2)
            dve.wait_ge(S("r_split"), 16)
            for q in range(8):
                dve.wait_ge(S("xm"), q + 1)
                link(V.tensor_copy(X_HI[:, q], BK8[q % 2][:, 0:ROWS]))
                V.tensor_tensor(X_LO[:, q], BK8[q % 2][:, 0:ROWS], X_HI[:, q].bitcast(F32), ALU.subtract).then_inc(S("xm_out"), 1)
            for s in range(PHASE["ret_proj"], PHASE["ret_proj"] + 8):
                split_lo(dve, s + 2)
            for s in range(PHASE["four_proj"], PHASE["four_proj"] + 4):
                split_lo(dve, s + 2)
            gates("gates2", SG2, MT2, OR, OF, M2_HI, M2_LO, "gate2_out", "gate2_used", "m2_split", "or_out", "of_out")
            out_add("out2", [4, 5, 0, 1], lambda m: GATE[:, 2, m:m + 1], "x_out2")
            norm("ni", 0, lambda k: GAIN[:, 4, k:k + 1], (48, 0))
            ffn(3, "ffn4", 1, lambda h, m: GATE[:, 3, m:m + 1])
            reciprocal("nj")
            for k in range(KT):
                scale("nj", 0, k, lambda k: par("mf", k), NT, "final")



def _tiles(w, kt=KT):
    k, c = w.shape
    return w.reshape(kt, P, c // P, P).transpose(2, 1, 0, 3).reshape(c // P, P, kt * P)


def _units(tiles, per):
    n = tiles.shape[0] // per
    return tiles.reshape(n, per, P, -1).transpose(0, 2, 1, 3).reshape(n, P, UNIT)


def _ffn_units(w1, w3, w2):
    a = np.concatenate([_tiles(w1)[:, :, None], _tiles(w3)[:, :, None]], axis=2).reshape(FT, P, UNIT)
    d = w2.reshape(FT // 2, 2, P, DM).transpose(0, 2, 1, 3).reshape(FT // 2, P, UNIT)
    out = [a[0], a[1]]
    for j in range(1, 11):
        out += [a[2 * j], d[j - 1], a[2 * j + 1]]
    return out + [d[10]]


def _row_units(w):
    c = w.shape[1]
    t = w.reshape(2, 4, P, c // 512, 512).transpose(3, 0, 2, 1, 4)
    return list(t.reshape(c // 512 * 2, P, UNIT))


def _gate_units(w):
    a, b = _tiles(w[:, :DM]), _tiles(w[:, DM:])
    return list(np.concatenate([a[:, :, None], b[:, :, None]], axis=2).reshape(KT, P, UNIT))


def _columns(v, n):
    return np.asarray(v).reshape(n, P).T


def _stream(i):
    w = {n: np.asarray(a) for n, a in i.items()}
    win, win2 = w["w_in"][0], w["w_in_2"][0]
    z = np.zeros((DM, 64), np.float32)
    r0 = 3 * DA
    s0 = r0 + 32 + 32 + 96
    low = np.concatenate([win[:, r0:r0 + 64], z, win[:, r0 + 64:s0], win[:, s0 + 3 * DA:s0 + 3 * DA + NH],
                          z[:, :P - 96 - NH]], axis=1)
    out = _ffn_units(w["ffn1_w1"][0], w["ffn1_w3"][0], w["ffn1_w2"][0])
    out += list(_units(_tiles(np.concatenate([win[:, :r0], low], axis=1)), 2))
    out += list(_units(_tiles(win[:, s0:s0 + 2 * DA]), 2))
    out += _row_units(win[:, s0 + 2 * DA:s0 + 3 * DA])
    out += list(_units(_tiles(w["rwkv_proj"][0], 4), 4)) + list(_units(_tiles(w["fox_proj"][0], 4), 4))
    out += _gate_units(win[:, s0 + 3 * DA + NH:])
    out += list(_units(_tiles(w["w_out"][0]), 2))
    out += _ffn_units(w["ffn2_w1"][0], w["ffn2_w3"][0], w["ffn2_w2"][0])
    a, b = w["w13_ffn1_2"][0], w["w13_ffn2_2"][0]
    out += _ffn_units(a[:, :FF], a[:, FF:], w["w2_ffn1_2"][0])

    def even_odd(x):
        return x.reshape(DM, RH, P, 2).transpose(0, 1, 3, 2).reshape(DM, DM)

    out += list(_units(_tiles(even_odd(win2[:, :DM])), 2))
    out += list(_units(_tiles(even_odd(win2[:, DM:2 * DM])), 2))
    out += _row_units(win2[:, 2 * DM:4 * DM])
    out += list(_units(_tiles(win2[:, 4 * DM:6 * DM]), 2))
    out += _row_units(win2[:, 6 * DM:7 * DM])
    out += list(_tiles(w["p_ret_2"][0], 16))
    out += list(_units(_tiles(w["p_four_2"][0]), 2))
    out += _gate_units(win2[:, 7 * DM:])
    out += list(_units(_tiles(w["w_out_2"][0]), 2))
    out += _ffn_units(b[:, :FF], b[:, FF:], w["w2_ffn2_2"][0])
    ada = _row_units(w["w_ada_2"][0])
    assert len(out) == NW and len(ada) == ADA
    return np.ascontiguousarray(np.stack([out[n] if kind == "w" else ada[n] for kind, n in ORDER]))


def _params(i):
    w = {n: np.asarray(a) for n, a in i.items()}
    par = np.zeros((P, NPAR), np.float32)

    def put(name, cols):
        a, b = PCOLS[name]
        par[:, a:b] = cols

    for name, key, n in (("n1", "ffn1_norm", 8), ("nm", "mix_norm", 8), ("w0", "rwkv_w0", 4), ("a0", "rwkv_a0", 4),
                         ("kk", "rwkv_k_k", 4), ("ka", "rwkv_k_a", 4), ("rk", "rwkv_r_k", 4), ("lnxg", "rwkv_lnx_g", 4),
                         ("lnxb", "rwkv_lnx_b", 4), ("n2", "ffn2_norm", 8), ("nf", "final_norm", 8), 
                         ("m1", "norm_ffn1_2", 8), ("m2", "norm_mix_2", 8), ("gn", "ret_gn_w_2", 16),
                         ("m3", "norm_ffn2_2", 8), ("mf", "norm_final_2", 8)):
        put(name, _columns(w[key], n))
    mu = w["shift_mu"][0]
    z = np.zeros(64, np.float32)
    put("mu", _columns(np.concatenate([mu[:3 * DA + 64], z, mu[3 * DA + 64:], z[:32]]), 14))
    fb = np.zeros((P, 1), np.float32)
    fb[96:96 + NH, 0] = w["fox_f_bias"][0]
    put("fb", fb)
    for name, key in (("qn", "fox_q_norm"), ("kn", "fox_k_norm")):
        put(name, np.concatenate([w[key][0], w[key][0]])[:, None])
    c = np.stack([w["c_2"][0].reshape(KT, P).T, w["c_ctx_2"].reshape(KT, P).T], axis=2)
    put("c", c.reshape(P, 16))
    put("dec", np.broadcast_to(np.concatenate([w["decay_fwd_2"][0], w["decay_bwd_2"][0]])[None], (P, 8)))
    put("epsr", 1e-6)
    put("epsl", 64e-5)
    put("epsq", 64e-6)
    put("one", 1.0)
    j = np.arange(2)[None] * P + np.arange(P)[:, None]
    put("jcol", np.concatenate([j, ROWS - j, ROWS + j], axis=1))
    return par


def _consts():
    con = np.zeros((P, NCON), np.float32)

    def put(name, x):
        a, b = CCOLS[name]
        con[:x.shape[0], a:b] = x.reshape(x.shape[0], -1)

    r = np.arange(P)
    put("ident", np.eye(P))
    put("ones", np.ones((P, P)))
    head = np.arange(IT)[None] * 2 + r[:, None] // 64
    put("sel", (head[:, :, None] == np.arange(NH)).astype(np.float32))
    put("bc", (head.T[None] == np.arange(NH)[:, None, None]).astype(np.float32))
    s, t = (r % CH)[:, None], np.arange(CH)[None]
    put("tmask", np.concatenate([t > s, t >= s], axis=1).astype(np.float32))
    a, b = np.arange(CH)[:, None], np.arange(CH)[None]
    lev = [((a // m == b // m + 1) & (a // (2 * m) == b // (2 * m))) for m in (1, 2, 4, 8, 16, 32)]
    put("lmask", np.stack(lev, axis=1).astype(np.float32))
    put("l0t", lev[0].T.astype(np.float32))
    put("causal", np.where(r[None] <= r[:, None], 0.0, -3.0e38))
    return con


def _rope_table():
    inv = 10000.0 ** (-np.arange(64, dtype=np.float32) / 64)
    pos = np.arange(ROWS)
    ang = np.concatenate([(pos // 64)[None] * inv[:, None], (pos % 64)[None] * inv[:, None]], axis=0).astype(np.float32)
    return np.stack([np.cos(ang), np.sin(ang)], axis=1).astype(np.float32)


def _dft_table():
    n = np.arange(256)
    ang = 2 * np.pi * ((n[:, None] * n[None]) % 256) / 256
    t = np.concatenate([np.cos(ang), np.sin(ang)], axis=1) / 16
    return np.ascontiguousarray(t.reshape(2, P, 512).transpose(1, 0, 2)).astype(np.float32)


def _arrays(i):
    w = {n: np.asarray(i[n]) for n in ("x", "ctx_2", "rwkv_w_up", "rwkv_a_up", "rwkv_g_up")}
    xin = np.stack([w[n][0].T.reshape(KT, P, ROWS).transpose(1, 0, 2) for n in ("x", "ctx_2")])
    lora = np.zeros((P, 2, DA), np.float32)
    lora[0:32, 0], lora[32:64, 0], lora[0:96, 1] = w["rwkv_w_up"][0], w["rwkv_a_up"][0], w["rwkv_g_up"][0]
    return {"stream": _stream(i), "xin": np.ascontiguousarray(xin), "params": _params(i), "consts": _consts(), "lora": lora,
            "bada": np.ascontiguousarray(np.repeat(_columns(i["b_ada_2"][0], 72)[:, :, None], 2, axis=2)),
            "rope": _rope_table(), "dft": _dft_table(),
            "iota": np.ascontiguousarray(np.broadcast_to(np.arange(ROWS, dtype=np.float32)[None], (P, ROWS)))}


def kernel(**inputs):
    import concourse.bacc as bacc
    from concourse.bass_utils import run_bass_kernel_spmd

    nc = bacc.Bacc("TRN2", target_bir_lowering=False, num_devices=1)
    arrays = _arrays(inputs)
    aps = {n: nc.dram_tensor(n, a.shape, F32, kind="ExternalInput").ap() for n, a in arrays.items()}
    out = nc.dram_tensor("out", (P, KT, ROWS), F32, kind="ExternalOutput").ap()
    build(nc, out=out, **aps)
    got = run_bass_kernel_spmd(nc, [arrays], core_ids=[0]).results[0]["out"]
    return np.ascontiguousarray(got.transpose(1, 0, 2).reshape(DM, ROWS).T)[None]
```

```python
from contextlib import ExitStack

import numpy as np
import concourse.bass as bass
from concourse import mybir

F32 = mybir.dt.float32
F32R = mybir.dt.float32r
ALU = mybir.AluOpType
ACT = mybir.ActivationFunctionType
AX_X = mybir.AxisListType.X

P = 128
ROWS = 256
DM = 1024
KT = DM // P
FF = 2816
FT = FF // P
DA = 512
IT = DA // P
NH = 8
CH = 64
NC = ROWS // CH
RH, RDV = 4, 512
UNIT = 2048
RING = 3
DECAY = float(np.exp(-0.5))

FFN_MARKS = [2, 2] + [2, 8, 2] * 10 + [8]
MARKS = []
PHASE = {}


def _phase(name, marks):
    PHASE[name] = len(MARKS)
    MARKS.extend(marks)


_phase("ffn1", FFN_MARKS)
_phase("rwkv_in", [2] * 7)
_phase("fox_qk", [2] * 4)
_phase("fox_v", [1, 2])
_phase("rwkv_proj", [4] * 2)
_phase("fox_proj", [4] * 2)
_phase("gates", [2] * 8)
_phase("out", [2] * 4)
_phase("ffn2", FFN_MARKS)
_phase("ffn3", FFN_MARKS)
_phase("ret_q", [2] * 4)
_phase("ret_k", [2] * 4)
_phase("ret_v", [1, 4] * 4)
_phase("four_in", [1, 2] * 2)
_phase("ret_g", [2] * 8)
_phase("ret_proj", [1] * 8)
_phase("four_proj", [2] * 4)
_phase("gates2", [2] * 8)
_phase("out2", [2] * 4)
_phase("ffn4", FFN_MARKS)
NW = len(MARKS)
MARK0 = [0]
for _m in MARKS:
    MARK0.append(MARK0[-1] + _m)

ADA = 36
MODR = 36
ADA_NB = 3
ADA_AFTER = {PHASE["rwkv_in"] - 1: ADA_NB, PHASE["rwkv_proj"] - 1: ADA - ADA_NB}
ORDER = []
for _s in range(NW):
    ORDER.append(("w", _s))
    if _s - 2 in ADA_AFTER:
        _d = sum(1 for o in ORDER if o[0] == "a")
        ORDER.extend(("a", _d + n) for n in range(ADA_AFTER[_s - 2]))
RAW_OF = {o: n for n, o in enumerate(ORDER)}
NU = len(ORDER)

NORM = {n: k for k, n in enumerate(("na", "nb", "nf", "nc", "nd", "ne", "ng", "nh", "ni", "nj"))}
NORM_H = {n: k for k, n in enumerate(("na", "nb", "nf", "nc", "ne", "ng", "nh", "ni"))}
NORM_ACC = {n: k for k, n in enumerate(("na", "nb", "nc", "nd", "ng", "ni", "nj"))}
STAT = {n: k for k, n in enumerate(("kk", "bon", "fq", "fk", "mu", "var"))}

PCOLS = {}
_n = 0
for _name, _w in [("n1", 8), ("nm", 8), ("mu", 14), ("w0", 4), ("a0", 4), ("kk", 4), ("ka", 4), ("rk", 4),
                  ("lnxg", 4), ("lnxb", 4), ("fb", 1), ("qn", 1), ("kn", 1), ("n2", 8), ("nf", 8),
                  ("c", 16), ("m1", 8), ("m2", 8), ("gn", 16), ("m3", 8), ("mf", 8),
                  ("dec", 8), ("epsr", 1), ("epsl", 1), ("epsq", 1), ("one", 1), ("jcol", 6)]:
    PCOLS[_name] = (_n, _n + _w)
    _n += _w
NPAR = _n
CCOLS = {}
_n = 0
for _name, _w in [("ident", 128), ("ones", 128), ("sel", 32), ("bc", 512), ("tmask", 128), ("lmask", 384),
                  ("l0t", 64), ("causal", 128)]:
    CCOLS[_name] = (_n, _n + _w)
    _n += _w
NCON = _n


def build(nc, stream, xin, params, consts, lora, bada, rope, dft, iota, out):
    with ExitStack() as ctx:
        sems = {}

        def S(name):
            if name not in sems:
                sems[name] = ctx.enter_context(nc.semaphore(name))
            return sems[name]

        def sb(name, shape, off, dt=F32):
            return nc.alloc_sbuf_tensor_at(name, shape, dt, offset=off)

        RAW0 = 16512
        HI0 = RAW0 + RING * UNIT * 4
        LO0 = HI0 + RING * UNIT * 4
        HHI0 = LO0 + RING * UNIT * 4
        HLO0 = HHI0 + 16384
        XC0 = HLO0 + 16384
        D0 = XC0 + 16384
        CON0 = D0 + 16384
        A0 = CON0 + 9216
        B1, B2, C0 = HHI0 + 8192, HLO0 + 8192, XC0 + 8192

        RAW = [sb(f"RAW{i}", [P, UNIT], RAW0 + i * UNIT * 4) for i in range(RING)]
        W_HI = [sb(f"W_HI{i}", [P, UNIT], HI0 + i * UNIT * 4, F32R) for i in range(RING)]
        W_LO = [sb(f"W_LO{i}", [P, UNIT], LO0 + i * UNIT * 4, F32R) for i in range(RING)]
        H_HI = sb("H_HI", [P, 2, KT, ROWS], HHI0, F32R)
        H_LO = sb("H_LO", [P, 2, KT, ROWS], HLO0, F32R)
        XC = sb("XC", [P, 2, KT, ROWS], XC0)
        HID_HI = sb("HID_HI", [P, 2, 512], D0, F32R)
        HID_LO = sb("HID_LO", [P, 2, 512], D0 + 4096, F32R)
        SILU = sb("SILU", [P, 2, 512], D0 + 8192)
        PROD = sb("PROD", [P, 2, 512], D0 + 12288)
        NT = sb("NT", [P, KT, ROWS], D0 + 8192)
        NT2 = sb("NT2", [P, KT, ROWS], A0 + 47104)
        NT3 = sb("NT3", [P, KT, ROWS], A0 + 16384)
        CON = sb("CON", [P, NCON], CON0)
        PAR = sb("PAR", [P, NPAR], CON0 + NCON * 4)
        off = (CON0 + (NCON + NPAR) * 4 + 31) // 32 * 32
        MOD = sb("MOD", [P, 72, 2], off)
        off += 576
        SCZ = sb("SCZ", [P, MODR * (KT + 1) - 2], off)
        off += (MODR * (KT + 1) - 2) * 4
        off = (off + 31) // 32 * 32
        DUM = sb("DUM", [P, 1], off)
        off += 32
        GAIN = sb("GAIN", [P, 5, 8], off)
        off += 160
        GATE = sb("GATE", [P, 4, 8], off)
        off += 128
        LG = sb("LG", [P, 5, 8], off)
        off += 160
        LB = sb("LB", [P, RH, 4], off)
        off += 64
        assert off <= A0

        def con(name, rows=P):
            a, b = CCOLS[name]
            return CON[0:rows, a:b]

        def par(name, i=0, n=1, rows=P):
            a = PCOLS[name][0]
            return PAR[0:rows, a + i:a + i + n]

        STD = sb("STD", [P, ROWS], A0 + 61440)
        RSTD = sb("RSTD", [P, ROWS], A0 + 62464)

        PRE = sb("PRE", [P, 14, ROWS + 1], A0)
        RKV = sb("RKV", [P, 3, IT, ROWS], A0 + 14400)
        LOR = sb("LOR", [P, 2, ROWS], A0 + 26688)
        FQ = sb("FQ", [P, IT, ROWS], A0 + 28736)
        FK = sb("FK", [P, IT, ROWS], A0 + 32832)
        FV = sb("FV", [P, 2, DA], A0 + 36928)
        LW = sb("LW", [P, 2, DA], A0 + 41024)
        SG = sb("SG", [P, IT, ROWS], A0 + 45120)
        AA = sb("AA", [P, IT, ROWS], A0 + 49216)
        KK = sb("KK", [P, IT, ROWS], A0 + 53312)
        TMP = sb("TMP", [P, IT, ROWS], A0 + 57408)
        STA = sb("STA", [NH, ROWS], A0 + 61504)
        STB = sb("STB", [NH, ROWS], A0 + 62528)
        GG = sb("GG", [P, IT, ROWS], B1)
        BO = sb("BO", [P, IT, ROWS], B1 + 4096)
        AR = sb("AR", [P, IT, NC, 2, CH], B2)
        BK = sb("BK", [P, IT, NC, 2, CH], C0)
        AV = sb("AV", [P, IT, NC, 2, CH], D0)
        LS = sb("LS", [P, IT, ROWS], D0 + 8192)
        PC = sb("PC", [P, IT, ROWS], D0 + 12288)
        F1 = sb("F1", [NH, ROWS], A0 + 41024)
        F2 = sb("F2", [NH, ROWS], A0 + 42048)
        F3 = sb("F3", [NH, ROWS], A0 + 43072)
        F4 = sb("F4", [NH, ROWS], A0 + 44096)
        NCB = sb("NCB", [P, NH, ROWS], A0)
        SCO = sb("SCO", [P, 2, 384], A0 + 8192)
        PRT = sb("PRT", [P, 2, 384], A0 + 11264)
        YB = sb("YB", [P, IT, ROWS], D0 + 8192)
        FST = sb("FST", [P, 2, 6], A0 + 14336)
        TT = sb("TT", [P, NC, NH, 2 * CH], A0)
        XM = sb("XM", [CH, NC, NH, CH], A0 + 16384)
        XT = sb("XT", [CH, NC, NH, CH], A0 + 24576)
        ZM = sb("ZM", [CH, NC, NH, CH], A0 + 32768)
        BKR = sb("BKR", [P, NC, DA], A0 + 40960)
        AVR = sb("AVR", [P, NC, DA], A0 + 49152)
        GT = sb("GT", [P, NC, IT, CH], A0 + 57344)
        WM = sb("WM", [CH, NC * NH, CH], C0)
        UM = sb("UM", [CH, NC, NH, CH], D0)
        ST = sb("ST", [P, NC + 1, IT, CH], A0 + 32768)
        YY = sb("YY", [P, IT, ROWS], A0 + 16384)
        YS = sb("YS", [P, IT, ROWS], A0 + 20480)
        YA_HI = sb("YA_HI", [P, IT, ROWS], C0, F32R)
        YA_LO = sb("YA_LO", [P, IT, ROWS], C0 + 4096, F32R)
        YB_HI = sb("YB_HI", [P, IT, ROWS], D0, F32R)
        YB_LO = sb("YB_LO", [P, IT, ROWS], D0 + 4096, F32R)
        MROW = sb("MROW", [MODR, 512], A0 + 45056)
        OA = sb("OA", [P, KT, ROWS], A0)
        OB = sb("OB", [P, KT, ROWS], A0 + 8192)
        M_HI = sb("M_HI", [P, KT, ROWS], A0 + 16384, F32R)
        M_LO = sb("M_LO", [P, KT, ROWS], A0 + 24576, F32R)
        SGA = sb("SGA", [P, 4, ROWS], A0 + 32768)
        MT = sb("MT", [P, 2, 3, ROWS], A0 + 36864)

        RK = sb("RK", [P, 2, KT, ROWS], A0)
        RV = sb("RV", [P, 4, RH * RDV], A0 + 16384)
        RQ = sb("RQ", [P, KT, ROWS], A0 + 49152)
        ROPE = sb("ROPE", [P, 2, ROWS], A0 + 57344)
        RT = sb("RT", [P, 4, ROWS], D0)
        RO = sb("RO", [P, 16, ROWS], D0)
        PT = sb("PT", [P, 4, ROWS], C0)
        DD = sb("DD", [P, 4, ROWS], C0 + 4096)
        T1 = sb("T1", [P, 2, ROWS], B1)
        T2 = sb("T2", [P, 2, ROWS], B1 + 2048)
        EB = sb("EB", [P, 2, ROWS], B1 + 4096)
        IOTA = sb("IOTA", [P, ROWS], B1 + 6144)
        SQ = sb("SQ", [P, 4, ROWS], B2)
        RST = sb("RST", [P, 2, ROWS], B2 + 4096)
        SGG = sb("SGG", [P, 2, ROWS], B2 + 6144)
        R_HI = sb("R_HI", [P, 16, ROWS], A0 + 16384, F32R)
        R_LO = sb("R_LO", [P, 16, ROWS], A0 + 32768, F32R)
        FX = [[sb(f"FX{q}{r}", [P, 512], o) for r, o in enumerate(oo)]
              for q, oo in enumerate(((A0 + 57344, A0 + 59392), (A0 + 61440, CON0 + CCOLS["lmask"][0] * 4)))]
        DFT = sb("DFT", [P, 2, 512], B1)
        ZZ = sb("ZZ", [P, 2, 2, 512], A0 + 49152)
        X_HI = sb("X_HI", [P, KT, ROWS], A0, F32R)
        X_LO = sb("X_LO", [P, KT, ROWS], A0 + 8192, F32R)
        OR = sb("OR", [P, KT, ROWS], C0)
        OF = sb("OF", [P, KT, ROWS], B1)
        M2_HI = sb("M2_HI", [P, KT, ROWS], A0, F32R)
        M2_LO = sb("M2_LO", [P, KT, ROWS], A0 + 8192, F32R)
        SG2 = sb("SG2", [P, 4, ROWS], A0 + 49152)
        MT2 = sb("MT2", [P, 2, 3, ROWS], A0 + 53248)

        PS = ctx.enter_context(nc.psum_tensor("PS", [P, 8, 512], F32))
        BK8 = [PS[:, i] for i in range(8)]
        ADAP = BK8[7]

        def pair(b):
            return PS[:, b:b + 2].rearrange("p b (i n) -> p (b i) n", n=ROWS)

        NORM_BANK = {n: BK8[b][:, 0:ROWS] for n, b in (("na", 4), ("nb", 3), ("nf", 7), ("nc", 2), ("nd", 3), ("ne", 2),
                                                       ("ng", 3), ("nh", 2), ("ni", 2), ("nj", 3))}
        psum_ready = S("psum_ready")
        landed = [S(f"landed{i}") for i in range(RING)]
        hi_done, lo_done = S("hi_done"), S("lo_done")
        ada_used = S("ada_used")

        def raw(s):
            return RAW_OF[("w", s)]

        def split_hi(act, s, j=None, j0=0):
            if s >= NW:
                return
            u = raw(s)
            if j is None:
                act.wait_ge(landed[u % RING], 16 * (u // RING + 1))
                if s >= RING:
                    act.wait_ge(psum_ready, MARK0[s - RING + 1])
            else:
                act.wait_ge(landed[u % RING], (j - j0) * 16 + 16 * (u // RING + 1))
                act.wait_ge(psum_ready, (j - j0) * 12 + MARK0[s - RING + 1])
            nc.scalar.activation(W_HI[s % RING][:], RAW[u % RING][:], ACT.Copy).then_inc(hi_done, 1)

        def split_lo(dve, s, j=None, j0=0):
            if s >= NW:
                return
            u = raw(s)
            dve.wait_ge(hi_done, s + 1 if j is None else (j - j0) * 3 + s + 1)
            nc.vector.tensor_tensor(W_LO[s % RING][:], RAW[u % RING][:], W_HI[s % RING][:].bitcast(F32),
                                    ALU.subtract).then_inc(lo_done, 1)

        def three(acc, w_hi, w_lo, x_hi, x_lo, first, last):
            nc.tensor.matmul(acc, w_hi, x_hi, start=first, stop=False)
            nc.tensor.matmul(acc, w_hi, x_lo, start=False, stop=False)
            return nc.tensor.matmul(acc, w_lo, x_hi, start=False, stop=last)

        block = ctx.enter_context(nc.Block())

        @block.sync
        def _(sp):
            sp.dma_start(PAR[:], params).then_inc(S("par_in"), 16)
            sp.dma_start(XC[:, 0, 0:4], xin[0, :, 0:4]).then_inc(S("x_in0"), 16)
            sp.dma_start(XC[:, 0, 4:8], xin[0, :, 4:8]).then_inc(S("x_in1"), 16)
            sp.dma_start(CON[:, 0:256], consts[:, 0:256]).then_inc(S("con_in"), 16)

            def free_raw(u, j=None, j0=0):
                if u < RING:
                    return
                kind, n = ORDER[u - RING]
                if kind == "w":
                    sp.wait_ge(lo_done, n + 1 if j is None else (j - j0) * 3 + n + 1)
                else:
                    sp.wait_ge(ada_used, n + 1)

            def load(u, j=None, j0=0):
                free_raw(u, j, j0)
                src = stream[u] if j is None else \
                    stream[bass.ds((j - j0) * 3 + u, 1)].rearrange("a p n -> (a p) n")
                sp.dma_start(RAW[u % RING][:], src).then_inc(landed[u % RING], 16)

            u = 0
            while u < NU:
                n = 0
                while u >= RING and u + n < NU and ORDER[u + n][0] == "w" and ORDER[u + n - RING][0] == "w":
                    n += 1
                if n >= 6:
                    with sp.Fori(0, n // 3) as j:
                        for i in range(3):
                            load(u + i, j, 0)
                    u += n // 3 * 3
                else:
                    load(u)
                    u += 1

        @block.gpsimd
        def _(pool):
            pool.wait_ge(landed[0], 16)
            pool.dma_start(CON[:, 256:], consts[:, 256:]).then_inc(S("masks_in"), 16)
            pool.dma_start(LW[:], lora).then_inc(S("lw_in"), 16)
            pool.dma_start(MOD[:], bada).then_inc(S("bada_in"), 16)
            pool.wait_ge(psum_ready, MARK0[PHASE["fox_proj"]])
            pool.dma_start(XC[:, 1], xin[1]).then_inc(S("ctx_in"), 16)
            pool.wait_ge(S("x_out1"), 8)
            pool.dma_start(ROPE[:], rope).then_inc(S("rope_in"), 16)
            pool.wait_ge(psum_ready, MARK0[PHASE["four_in"]])
            pool.dma_start(IOTA[:], iota).then_inc(S("iota_in"), 16)
            pool.wait_ge(S("d_arg"), RH)
            pool.dma_start(DFT[:], dft).then_inc(S("dft_in"), 16)
            for k in range(0, KT, 4):
                pool.wait_ge(S("final"), k + 4)
                pool.dma_start(out[:, k:k + 4], NT[:, k:k + 4]).then_inc(S("stored"), 16)
            pool.wait_ge(S("stored"), 32)

        @block.tensor
        def _(pe):
            def wait_unit(s, j=None, j0=0):
                pe.wait_ge(lo_done, s + 1 if j is None else (j - j0) * 3 + s + 1)

            def norm_sum(name, k, tmp=NT):
                if name in NORM_ACC and 0 < k < 6:
                    return
                if name in NORM_ACC and k == 0:
                    pe.wait_ge(S("norm_acc"), 5 * NORM_ACC[name] + 5)
                pe.wait_ge(S("norm_sq"), KT * NORM[name] + k + 1)
                last = nc.tensor.matmul(NORM_BANK[name], con("ones"), tmp[:, k], start=(k == 0), stop=(k == 7))
                if k == 7:
                    last.then_inc(S("norm_ssq"), 1)

            def norm(name, tmp=NT):
                for k in range(KT):
                    norm_sum(name, k, tmp)

            def ffn(f, name, halves, h_name, then):
                n = halves * ROWS
                s0 = PHASE[name]
                rh = (lambda k: H_HI[:, 0:halves, k])
                rl = (lambda k: H_LO[:, 0:halves, k])

                def up(t, s, j=None, j0=0):
                    wait_unit(s, j, j0)
                    tt = f * FT + t
                    if tt >= 2:
                        pe.wait_ge(S("hid_prod"), tt - 1 if j is None else (j - j0) * 2 + tt - 1)
                    sl = s % RING
                    for w, k in ([(w, k) for k in range(KT) for w in range(2)] if t == 0 else
                                 [(w, k) for w in range(2) for k in range(KT)]):
                        if t == 0 and w == 0:
                            pe.wait_ge(S("norm_h"), KT * NORM_H[h_name] + k + 1)
                        c = (w * KT + k) * P
                        last = three(BK8[2 * (t % 2) + w][:, 0:n], W_HI[sl][:, c:c + P], W_LO[sl][:, c:c + P],
                                     rh(k), rl(k), k == 0, k == KT - 1)
                        if k == KT - 1:
                            last.then_inc(psum_ready, 1)

                def down(i, s, j=None, j0=0):
                    wait_unit(s, j, j0)
                    sl = s % RING
                    early = 4 if i == 10 else 0
                    for m, t in ([(m, 0) for m in range(early)] + [(m, 1) for m in range(early)] +
                                 [(m, t) for m in range(early, KT) for t in range(2)]):
                        if m == 0 and (t == 0 or early):
                            a = f * FT + 2 * i + 1 + (t if early else 1)
                            pe.wait_ge(S("hid_lo"), a if j is None else (j - j0) * 2 + a)
                        d = f * 88 + i * 8 + m
                        if t == 0 and d >= 4:
                            pe.wait_ge(S("down_added"), d - 3 if j is None else (j - j0) * 8 + d - 3)
                        c = (t * KT + m) * P
                        last = three(BK8[4 + m % 4][:, 0:n], W_HI[sl][:, c:c + P], W_LO[sl][:, c:c + P],
                                     HID_HI[:, t, 0:n], HID_LO[:, t, 0:n], t == 0, t == 1)
                        if t == 1:
                            last.then_inc(psum_ready, 1)
                    if i == 10:
                        norm(then)

                up(0, s0)
                up(1, s0 + 1)
                with pe.Fori(1, 11) as j:
                    up(2, s0 + 2, j, 1)
                    down(0, s0 + 3, j, 1)
                    up(3, s0 + 4, j, 1)
                down(10, s0 + 32)

            def cols(name, banks, rhs_hi, rhs_lo, n, out_sem, kt=KT, tiles=2, first=None, behind=None, only=None):
                s0 = PHASE[name]
                units = [s for s in range(s0, NW) if s < s0 + {"rwkv_in": 7, "fox_qk": 4, "rwkv_proj": 2, "fox_proj": 2,
                         "gates": 8, "out": 4, "ret_k": 4, "ret_q": 4, "ret_g": 8, "ret_proj": 8, "four_proj": 4,
                         "gates2": 8, "out2": 4}[name]]
                for s in units if only is None else [s0 + only]:
                    wait_unit(s)
                    turns = s == s0 and first is not None
                    for w, k in ([(w, k) for k in range(kt) for w in range(tiles)] if turns else
                                 [(w, k) for w in range(tiles) for k in range(kt)]):
                        tile = (s - s0) * tiles + w
                        if k == 0 and tile >= len(banks):
                            pe.wait_ge(S(out_sem), tile - len(banks) + 1)
                        if turns and w == 0:
                            pe.wait_ge(S(first[0]), first[1] + k + 1 if kt == KT else first[1] + k // 4 + 1)
                        c = (w * kt + k) * P
                        sl = s % RING
                        last = three(BK8[banks[tile % len(banks)]][:, 0:n], W_HI[sl][:, c:c + P], W_LO[sl][:, c:c + P],
                                     rhs_hi(k), rhs_lo(k), k == 0, k == kt - 1)
                        if k == kt - 1:
                            last.then_inc(psum_ready, 1)
                    if behind is not None and s - s0 in behind:
                        behind[s - s0]()

            def rows(name, n_chunks, rts, banks, out_sem, only=None):
                for q in range(n_chunks):
                    s = PHASE[name] + 2 * q
                    for half in range(2):
                        if only is not None and 2 * q + half != only:
                            continue
                        wait_unit(s + half)
                        for r, (h, r0) in enumerate(rts):
                            if half == 0 and (q * len(rts) + r) >= len(banks):
                                pe.wait_ge(S(out_sem), q * len(rts) + r - len(banks) + 1)
                            bank = BK8[banks[(q * len(rts) + r) % len(banks)]]
                            for k4 in range(4):
                                k = half * 4 + k4
                                sl = (s + half) % RING
                                c = k4 * 512
                                st, sp_ = (k == 0), (k == 7)
                                xh, xl = H_HI[:, h, k, r0:r0 + P], H_LO[:, h, k, r0:r0 + P]
                                wh, wl = W_HI[sl][:, c:c + 512], W_LO[sl][:, c:c + 512]
                                nc.tensor.matmul(bank[:], xh, wh, start=st, stop=False)
                                nc.tensor.matmul(bank[:], xh, wl, start=False, stop=False)
                                last = nc.tensor.matmul(bank[:], xl, wh, start=False, stop=sp_)
                            if half == 1 or r == len(rts) - 1:
                                last.then_inc(psum_ready, 1)

            ada_at = [0]

            def ada(n):
                for m in range(ada_at[0], min(ada_at[0] + n, ADA * 4)):
                    d, k, q = m // 4, m % 8, m // 8
                    u = RAW_OF[("a", d)]
                    if m == 0:
                        pe.wait_ge(S("sc_done"), 1)
                    if m % 4 == 0:
                        pe.wait_ge(landed[u % RING], 16 * (u // RING + 1))
                    z = MODR - 2 + MODR * k - 2 * q
                    last = nc.tensor.matmul(ADAP[0:MODR], SCZ[:, z:z + MODR], RAW[u % RING][:, (m % 4) * 512:(m % 4 + 1) * 512],
                                            start=(m == 0), stop=(m == ADA * 4 - 1))
                    if m % 4 == 3:
                        last.then_inc(ada_used, 1)
                ada_at[0] = min(ada_at[0] + n, ADA * 4)

            pe.wait_ge(S("con_in"), 16)
            norm("na")
            ffn(0, "ffn1", 1, "na", "nb")
            ada(4 * ADA_NB)
            xh, xl = (lambda k: H_HI[:, 0, k]), (lambda k: H_LO[:, 0, k])
            cols("rwkv_in", [4, 5, 6, 0], xh, xl, ROWS, "pre_out", first=("norm_h", KT * NORM_H["nb"]))
            pe.wait_ge(S("pre_out"), 14)
            cols("fox_qk", [4, 5, 6, 0], xh, xl, ROWS, "fqk_out")
            rows("fox_v", 1, [(0, 0), (0, P)], [1, 2], "fv_out")
            pe.wait_ge(S("fqk_out"), 8)
            pe.wait_ge(S("lw_in"), 16)
            pe.wait_ge(S("masks_in"), 16)
            pe.wait_ge(S("lora_act"), 1)
            for i in range(IT):
                last = nc.tensor.matmul(BK8[3 + i // 2][:, (i % 2) * ROWS:(i % 2 + 1) * ROWS], LW[0:32, 0, i * P:(i + 1) * P],
                                        LOR[0:32, 0], start=True, stop=True)
            last.then_inc(S("lora_z"), 1)
            for i in range(IT):
                last = nc.tensor.matmul(BK8[5 + i // 2][:, (i % 2) * ROWS:(i % 2 + 1) * ROWS], LW[32:64, 0, i * P:(i + 1) * P],
                                        LOR[32:64, 0], start=True, stop=True)
            last.then_inc(S("lora_a"), 1)
            pe.wait_ge(S("lora_act"), 2)
            pe.wait_ge(S("fv_out"), 2)
            for i in range(IT):
                last = nc.tensor.matmul(BK8[[0, 1][i // 2]][:, (i % 2) * ROWS:(i % 2 + 1) * ROWS], LW[0:96, 1, i * P:(i + 1) * P],
                                        LOR[0:96, 1], start=True, stop=True)
            last.then_inc(S("lora_g"), 1)

            def stat(src, banks, name):
                ada(5)
                pe.wait_ge(S("stat_in"), STAT[name] + 1)
                for i in range(IT):
                    last = nc.tensor.matmul(BK8[banks][0:NH, 0:ROWS], con("sel")[:, 8 * i:8 * i + 8], src[:, i],
                                            start=(i == 0), stop=(i == IT - 1))
                last.then_inc(S("stat_sum"), 1)

            def spread(src, b0, name):
                ada(5)
                pe.wait_ge(S("stat_st"), STAT[name] + 1)
                for i in range(IT):
                    last = nc.tensor.matmul(BK8[b0 + i // 2][:, (i % 2) * ROWS:(i % 2 + 1) * ROWS],
                                            con("bc", NH)[:, i * P:(i + 1) * P], src, start=True, stop=True)
                last.then_inc(S("stat_bc"), 1)

            stat(TMP, 2, "kk")
            pe.wait_ge(S("sg_done"), 1)
            spread(STA[:], 3, "kk")
            stat(TMP, 2, "bon")
            pe.wait_ge(S("aa_done"), 1)
            spread(STA[:], 5, "bon")
            stat(TMP, 2, "fq")
            spread(STA[:], 3, "fq")
            stat(TMP, 2, "fk")
            spread(STA[:], 5, "fk")
            ada(14)
            pe.wait_ge(S("lf_cum"), 1)
            pe.wait_ge(S("fq_norm"), 1)
            pe.wait_ge(S("fk_norm"), 1)
            pe.wait_ge(S("gg_done"), 1)
            for h in range(NH):
                if h >= 4 and h % 2 == 0:
                    pe.wait_ge(S("ncb_out"), h // 2 - 1)
                last = nc.tensor.matmul(BK8[[0, 1][(h // 2) % 2]][:, (h % 2) * ROWS:(h % 2 + 1) * ROWS],
                                        con("ident", NH)[:, h:h + 1].to_broadcast([NH, P]), STB[:],
                                        start=True, stop=True)
                if h % 2:
                    last.then_inc(S("ncb"), 1)
            for h in range(NH + 1):
                if h < NH:
                    i, p0 = h // 2, 64 * (h % 2)
                    if h >= 2:
                        pe.wait_ge(S("sco_out"), h - 1)
                    b = BK8[3 + h % 2]
                    nc.tensor.matmul(b[:, 0:P], FQ[p0:p0 + 64, i, 0:P], FK[p0:p0 + 64, i, 0:P], start=True, stop=True)
                    last = nc.tensor.matmul(b[:, P:384], FQ[p0:p0 + 64, i, P:ROWS], FK[p0:p0 + 64, i, :], start=True, stop=True)
                    last.then_inc(S("scores"), 1)
                if h >= 1:
                    g = h - 1
                    i, p0 = g // 2, 64 * (g % 2)
                    ada(3)
                    pe.wait_ge(S("probs"), g + 1)
                    if g >= 2:
                        pe.wait_ge(S("fo_out"), g - 1)
                    for q in range(3):
                        last = nc.tensor.transpose(BK8[5 + g % 2][:, q * P:(q + 1) * P], SCO[:, g % 2, q * P:(q + 1) * P],
                                                   con("ident"))
                    last.then_inc(S("prt"), 1)
                    pe.wait_ge(S("prt_out"), g + 1)
                    o = BK8[1 + g % 2][p0:p0 + 64, 0:ROWS]
                    v = (lambda kt: FV[:, kt, 64 * g:64 * g + 64])
                    nc.tensor.matmul(o[:, 0:P], v(0), PRT[:, g % 2, 0:P], start=True, stop=True)
                    nc.tensor.matmul(o[:, P:ROWS], v(0), PRT[:, g % 2, P:2 * P], start=True, stop=False)
                    last = nc.tensor.matmul(o[:, P:ROWS], v(1), PRT[:, g % 2, 2 * P:3 * P], start=False, stop=True)
                    last.then_inc(S("fox_o"), 1)
            ada(4)
            pe.wait_ge(S("bk_ready"), 1)
            pe.wait_ge(S("av_ready"), 1)
            pe.wait_ge(S("fo_out"), NH)
            for c in range(NC):
                for n, src in enumerate((BK, AV)):
                    q = 2 * c + n
                    if q >= 2:
                        pe.wait_ge(S("tr_out"), q - 1)
                    for i in range(IT):
                        last = nc.tensor.transpose(BK8[q % 2][:, i * P:(i + 1) * P],
                                                   src[:, i, c].rearrange("p a b -> p (a b)"), con("ident"))
                    last.then_inc(S("tr"), 1)
            for c in range(NC):
                for p in range(2):
                    q = 2 * c + p
                    if q >= 4:
                        pe.wait_ge(S("tt_out"), q - 3)
                    for i in range(IT):
                        last = nc.tensor.matmul(BK8[2 + q % 4][:, i * P:(i + 1) * P],
                                                BK[64 * p:64 * p + 64, i, c].rearrange("p a b -> p (a b)"),
                                                AR[64 * p:64 * p + 64, i, c].rearrange("p a b -> p (a b)"),
                                                start=True, stop=True)
                    last.then_inc(S("tt"), 1)
            pe.wait_ge(S("tr_out"), 8)
            for c in range(NC):
                pe.wait_ge(S("tt_out"), 2 * c + 2)
                if c >= 2:
                    pe.wait_ge(S("w_out"), c - 1)
                for h in range(NH):
                    last = nc.tensor.matmul(BK8[c % 2][0:CH, h * CH:(h + 1) * CH], TT[CH:P, c, h, 0:CH],
                                            AVR[CH:P, c, h * CH:(h + 1) * CH], start=True, stop=True)
                last.then_inc(S("w"), 1)
            pe.wait_ge(S("w_out"), 4)

            def x_done(n):
                return 2 * n + 2 if n < 5 * NC else 5 * NC + n + 1

            def z_step(n):
                lev, c = n // NC, n % NC
                if n >= 2:
                    pe.wait_ge(S("z_out"), n - 1)
                if lev > 0:
                    pe.wait_ge(S("x_out"), x_done(n - NC))
                for h in range(NH):
                    rhs = con("ident", CH)[:, 0:CH] if lev == 0 else XM[:, c, h]
                    last = nc.tensor.matmul(BK8[n % 2][0:CH, h * CH:(h + 1) * CH], TT[0:CH, c, h, 0:CH], rhs,
                                            start=True, stop=True)
                last.then_inc(S("z"), 1)

            for n in range(NC + 2):
                z_step(n)
                ada(1)
            for n in range(NC, 6 * NC):
                lev, c = n // NC, n % NC
                pe.wait_ge(S("z_out"), n + 1)
                pe.wait_ge(S("x_out"), x_done(n - 2))
                if lev < 5:
                    for h in range(NH):
                        last = nc.tensor.matmul(BK8[2 + n % 2][0:CH, h * CH:(h + 1) * CH], XT[:, c, h], ZM[:, c, h],
                                                start=True, stop=True)
                    last.then_inc(S("xz"), 1)
                for h in range(NH):
                    last = nc.tensor.matmul(BK8[4 + n % 2][0:CH, h * CH:(h + 1) * CH], ZM[:, c, h], XT[:, c, h],
                                            start=True, stop=True)
                last.then_inc(S("zx"), 1)
                if n + 2 < 6 * NC:
                    z_step(n + 2)
            for c in range(NC):
                pe.wait_ge(S("x_out"), x_done(5 * NC + c))
                if c >= 2:
                    pe.wait_ge(S("u_out"), c - 1)
                for h in range(NH):
                    last = nc.tensor.matmul(BK8[2 + c % 2][0:CH, h * CH:(h + 1) * CH], XT[:, c, h],
                                            WM[:, c * NH + h], start=True, stop=True)
                last.then_inc(S("u"), 1)
                if c >= 2:
                    pe.wait_ge(S("gt_out"), c - 1)
                elif c == 0:
                    pe.wait_ge(S("x_out"), x_done(6 * NC - 1))
                for h in range(NH):
                    i, p0 = h // 2, 64 * (h % 2)
                    last = nc.tensor.matmul(BK8[4 + c % 2][p0:p0 + CH, i * CH:(i + 1) * CH], AVR[0:CH, c, h * CH:(h + 1) * CH],
                                            XT[:, c, h], start=True, stop=True)
                last.then_inc(S("gt"), 1)
                ada(1)
            pe.wait_ge(S("gt_out"), 4)
            pe.wait_ge(S("u_out"), 4)
            for c in range(NC):
                pe.wait_ge(S("state"), c + 1)
                for p in range(2):
                    for i in range(IT):
                        last = nc.tensor.matmul(BK8[p][0:CH, i * CH:(i + 1) * CH], GT[64 * p:64 * p + 64, c, i],
                                                ST[64 * p:64 * p + 64, c, i], start=True, stop=True)
                last.then_inc(S("sa"), 1)
                ada(1)
                pe.wait_ge(S("sa_out"), 2 * c + 2)
                if c < NC - 1:
                    for h in range(NH):
                        i, p0 = h // 2, 64 * (h % 2)
                        last = nc.tensor.matmul(BK8[2][p0:p0 + CH, i * CH:(i + 1) * CH], BKR[:, c, h * CH:(h + 1) * CH],
                                                AVR[:, c, h * CH:(h + 1) * CH], start=True, stop=True)
                    last.then_inc(S("st"), 1)
                for p in range(2):
                    for i in range(IT):
                        h = 2 * i + p
                        y = BK8[(3 if p == 0 else 5) + i // 2][64 * p:64 * p + 64, (i % 2) * ROWS + c * CH:(i % 2) * ROWS + (c + 1) * CH]
                        nc.tensor.matmul(y, ST[64 * p:64 * p + 64, c, i], AR[64 * p:64 * p + 64, i, c, 1], start=True, stop=False)
                        last = nc.tensor.matmul(y, AVR[:, c, h * CH:(h + 1) * CH], TT[:, c, h, CH:2 * CH], start=False, stop=True)
            last.then_inc(S("y"), 1)
            ada(8)
            pe.wait_ge(S("yy_even"), 1)
            stat(YY, 2, "mu")
            spread(STA[:], 3, "mu")
            stat(YS, 2, "var")
            spread(STA[:], 5, "var")
            ada(ADA * 4)
            pe.wait_ge(S("mod_rows"), 1)
            for j in range(4):
                last = nc.tensor.transpose(ADAP[:, j * MODR:(j + 1) * MODR], MROW[:, j * P:(j + 1) * P], con("ident", MODR)[:, 0:MODR])
            last.then_inc(S("mod_tr"), 1)
            pe.wait_ge(S("ya_split"), 1)
            cols("rwkv_proj", [0, 1, 2, 3], lambda k: YA_HI[:, k], lambda k: YA_LO[:, k], ROWS, "oa_out", kt=4, tiles=4)
            pe.wait_ge(S("yb_split"), 1)
            pe.wait_ge(S("oa_out"), 8)
            cols("fox_proj", [4, 5, 6, 0], lambda k: YB_HI[:, k], lambda k: YB_LO[:, k], ROWS, "ob_out", kt=4, tiles=4)
            pe.wait_ge(S("ob_out"), 8)
            pe.wait_ge(S("mod_out"), 1)
            cols("gates", [0, 1, 2, 3], xh, xl, ROWS, "gate_out", behind={0: lambda: norm("nf", NT2)})
            cols("out", [4, 5, 6, 3], lambda k: M_HI[:, k], lambda k: M_LO[:, k], ROWS, "x_out1", first=("m_split", 0),
                 behind={3: lambda: norm("nc")})
            ffn(1, "ffn2", 1, "nc", "nd")
            norm("ne")
            ffn(2, "ffn3", 2, "ne", "ng")
            cols("ret_q", [4, 5, 6, 7], xh, xl, ROWS, "rq_out", first=("norm_h", KT * NORM_H["ng"]),
                 behind={0: lambda: norm("nh", NT3)})
            cols("ret_k", [0, 1, 2, 3], lambda k: H_HI[:, :, k], lambda k: H_LO[:, :, k], 512, "rk_out", first=("norm_h", KT * NORM_H["nh"]))
            pe.wait_ge(S("rq_out"), 8)
            for n in range(8):
                if n == 2:
                    pe.wait_ge(S("rk_out"), 8)
                rows("ret_v", 4, [(0, 0), (0, P), (1, 0), (1, P)], [4, 5, 6, 7, 0, 1, 2, 3], "rv_out", only=n)
            pe.wait_ge(S("rv_out"), 16)

            def beside(n):
                if n < 4:
                    rows("four_in", 2, [(0, 0), (0, P)], [4, 5], "fx_out", only=n)
                else:
                    if n == 4:
                        pe.wait_ge(S("fx_out"), 4)
                    cols("ret_g", [4, 5], xh, xl, ROWS, "rg_out", only=n - 4)

            for h in range(RH + 1):
                if h < RH:
                    if h >= 1:
                        pe.wait_ge(S("pt_out"), h)
                    for kt in range(4):
                        half, k0 = kt // 2, (kt % 2) * P
                        for d in range(2):
                            last = nc.tensor.matmul(BK8[kt // 2][:, (kt % 2) * ROWS:(kt % 2 + 1) * ROWS],
                                                    RK[:, half, 2 * h + d, k0:k0 + P], RQ[:, 2 * h + d],
                                                    start=(d == 0), stop=(d == 1))
                    last.then_inc(S("rscores"), 1)
                beside(2 * h)
                if h >= 1:
                    pe.wait_ge(S("tile_sum"), 2 * h - 1)
                    nc.tensor.matmul(BK8[6][:, 0:ROWS], con("ones"), SQ[:, 0], start=True, stop=True).then_inc(S("mean_sum"), 1)
                if h < RH:
                    pe.wait_ge(S("pt_out"), h + 1)
                    for i in range(4):
                        for kt in range(4):
                            last = nc.tensor.matmul(BK8[2 + i // 2][:, (i % 2) * ROWS:(i % 2 + 1) * ROWS],
                                                    RV[:, kt, h * RDV + i * P:h * RDV + (i + 1) * P], PT[:, kt],
                                                    start=(kt == 0), stop=(kt == 3))
                    last.then_inc(S("pv_done"), 1)
                if h == RH:
                    beside(2 * h + 1)
                if h >= 1:
                    pe.wait_ge(S("tile_sum"), 2 * h)
                    nc.tensor.matmul(BK8[7][:, 0:ROWS], con("ones"), SQ[:, 0], start=True, stop=True).then_inc(S("rvar_sum"), 1)
                if h < RH:
                    beside(2 * h + 1)
            pe.wait_ge(S("dft_in"), 16)
            pe.wait_ge(S("rvar_rt"), RH)
            for g in range(4):
                for t in range(2):
                    q = 2 * g + t
                    if q >= 2:
                        pe.wait_ge(S("zz_out"), q - 1)
                    for k in range(2):
                        last = nc.tensor.matmul(BK8[6 + q % 2][:], FX[q // 4][k][:, q % 4 * P:(q % 4 + 1) * P], DFT[:, k],
                                                start=(k == 0), stop=(k == 1))
                    last.then_inc(S("zz"), 1)
                if g < 2:
                    beside(10 + g)
                pe.wait_ge(S("zz_out"), 2 * g + 2)
                for t in range(2):
                    q = 2 * g + t
                    if q >= 2:
                        pe.wait_ge(S("xm_out"), q - 1)
                    n = 0
                    for part in range(2):
                        for k in range(2):
                            last = nc.tensor.matmul(BK8[q % 2][:, 0:ROWS], DFT[:, k, part * 256 + t * P:part * 256 + (t + 1) * P],
                                                    ZZ[:, g % 2, k, part * ROWS:(part + 1) * ROWS], start=(n == 0), stop=(n == 3))
                            n += 1
                    last.then_inc(S("xm"), 1)
            cols("ret_proj", [2, 3, 6, 7], lambda k: R_HI[:, k], lambda k: R_LO[:, k], ROWS, "or_out", kt=16, tiles=1,
                 first=("r_split", 0))
            pe.wait_ge(S("xm_out"), 8)
            pe.wait_ge(S("or_out"), 8)
            cols("four_proj", [4, 5, 0, 1], lambda k: X_HI[:, k], lambda k: X_LO[:, k], ROWS, "of_out")
            cols("gates2", [2, 3, 6, 7], xh, xl, ROWS, "gate2_out")
            pe.wait_ge(S("of_out"), 8)
            cols("out2", [4, 5, 0, 1], lambda k: M2_HI[:, k], lambda k: M2_LO[:, k], ROWS, "x_out2", first=("m2_split", 0),
                 behind={3: lambda: norm("ni")})
            ffn(3, "ffn4", 1, "ni", "nj")

        @block.scalar
        def _(act):
            A = nc.scalar.activation

            def load_sqrt():
                A(DUM[:], par("one"), ACT.Sqrt)

            def square(name, half, k, sem, v, tmp=NT):
                act.wait_ge(S(sem), v)
                A(tmp[:, k], XC[:, half, k], ACT.Square).then_inc(S("norm_sq"), 1)

            def root(name):
                act.wait_ge(S("norm_ssq"), NORM[name] + 1)
                A(STD[:], NORM_BANK[name], ACT.Sqrt, scale=1.0 / DM, bias=par("epsr")).then_inc(S("norm_std"), 1)

            def round_rows(name, half, k, shift=None, tmp=NT):
                act.wait_ge(S("norm_t"), KT * NORM_H[name] + k + 1)
                if shift is None:
                    ins = A(H_HI[:, half, k], tmp[:, k], ACT.Copy)
                else:
                    ins = A(H_HI[:, half, k], tmp[:, k], ACT.Identity, bias=MOD[:, shift[0] + k, shift[1]:shift[1] + 1])
                ins.then_inc(S("norm_hi"), 1)

            def ffn(f, name, halves):
                n = halves * ROWS
                s0 = PHASE[name]

                def silu(t, mark, j=None, j0=0):
                    tt = f * FT + t
                    if tt >= 2:
                        act.wait_ge(S("hid_prod"), tt - 1 if j is None else (j - j0) * 2 + tt - 1)
                    act.wait_ge(psum_ready, mark if j is None else (j - j0) * 12 + mark)
                    A(SILU[:, t % 2, 0:n], BK8[2 * (t % 2)][:, 0:n], ACT.Silu).then_inc(S("silu"), 1)

                m0 = MARK0[s0]
                split_hi(act, s0 + 2)
                silu(0, m0 + 1)
                split_hi(act, s0 + 3)
                silu(1, m0 + 3)

                def body(j, j0, i):
                    s, m = s0 + 2 + 3 * (i - 1), m0 + 4 + 12 * (i - 1)
                    split_hi(act, s + 2, j, j0)
                    split_hi(act, s + 3, j, j0)
                    silu(2 * i, m + 1, j, j0)
                    split_hi(act, s + 4, j, j0)
                    silu(2 * i + 1, m + 11, j, j0)

                with act.Fori(1, 10) as j:
                    body(j, 1, 1)
                body(None, 0, 10)
                split_hi(act, s0 + 34)

            act.wait_ge(S("par_in"), 16)
            load_sqrt()
            for k in range(KT):
                square("na", 0, k, f"x_in{k // 4}", 16)
            root("na")
            split_hi(act, 0)
            for k in range(KT):
                round_rows("na", 0, k)
            split_hi(act, 1)
            act.wait_ge(S("scz_zero"), 1)
            A(SCZ[:, MODR - 2:].rearrange("p (k n) -> p k n", n=MODR)[:, :, 0:2],
              par("c", 0, 16).rearrange("p (k n) -> p k n", n=2), ACT.Silu).then_inc(S("sc_done"), 1)
            ffn(0, "ffn1", 1)
            load_sqrt()
            for k in range(KT):
                square("nb", 0, k, "down_added", 80 + k + 1)
            root("nb")
            for k in range(KT):
                round_rows("nb", 0, k)
            s0 = PHASE["rwkv_in"]
            m0 = MARK0[s0]
            for t in range(14):
                if t % 2 == 0:
                    split_hi(act, s0 + t // 2 + 2)
                act.wait_ge(psum_ready, m0 + t + 1)
                A(PRE[:, t, 1:ROWS + 1], BK8[[4, 5, 6, 0][t % 4]][:, 0:ROWS], ACT.Copy).then_inc(S("pre_out"), 1)
            s0 = PHASE["fox_qk"]
            m0 = MARK0[s0]
            for t in range(8):
                if t % 2 == 0:
                    split_hi(act, s0 + t // 2 + 2)
                act.wait_ge(psum_ready, m0 + t + 1)
                A((FQ, FK)[t // 4][:, t % 4], BK8[[4, 5, 6, 0][t % 4]][:, 0:ROWS], ACT.Copy).then_inc(S("fqk_out"), 1)
            s0 = PHASE["fox_v"]
            m0 = MARK0[s0]
            split_hi(act, s0 + 2)
            split_hi(act, s0 + 3)
            for r in range(2):
                act.wait_ge(psum_ready, m0 + 2 + r)
                A(FV[:, r], BK8[1 + r], ACT.Copy).then_inc(S("fv_out"), 1)
            act.wait_ge(S("lor"), 1)
            A(LOR[0:32, 0], LOR[0:32, 0], ACT.Tanh).then_inc(S("lora_act"), 1)
            A(LOR[0:96, 1], LOR[0:96, 1], ACT.Sigmoid).then_inc(S("lora_act"), 1)
            act.wait_ge(S("lora_z"), 1)
            for i in range(IT):
                last = A(SG[:, i], pair(3)[:, i], ACT.Sigmoid, bias=par("w0", i))
            last.then_inc(S("sg_done"), 1)
            act.wait_ge(S("lora_a"), 1)
            for i in range(IT):
                last = A(AA[:, i], pair(5)[:, i], ACT.Sigmoid, bias=par("a0", i))
            last.then_inc(S("aa_done"), 1)
            act.wait_ge(S("lora_g"), 1)
            A(GG[:], pair(0), ACT.Copy).then_inc(S("gg_done"), 1)
            act.wait_ge(S("kk_max"), 1)
            A(STA[:], STA[:], ACT.Sqrt).then_inc(S("kk_rt"), 1)
            act.wait_ge(S("stat_sum"), STAT["fq"] + 1)
            act.wait_ge(S("stat_bc"), STAT["bon"] + 1)
            A(STA[:], BK8[2][0:NH, 0:ROWS], ACT.Sqrt, scale=1.0, bias=par("epsq", 0, 1, NH)).then_inc(S("fq_rt"), 1)
            act.wait_ge(S("stat_sum"), STAT["fk"] + 1)
            act.wait_ge(S("stat_bc"), STAT["fq"] + 1)
            A(STA[:], BK8[2][0:NH, 0:ROWS], ACT.Sqrt, scale=1.0 / 64, bias=par("epsr", 0, 1, NH)).then_inc(S("fk_rt"), 1)
            act.wait_ge(S("f_x"), 1)
            A(F3[:], F1[:], ACT.Abs).then_inc(S("f_act"), 1)
            act.wait_ge(S("f_act"), 1)
            A(F3[:], F3[:], ACT.Exp, scale=-1.0).then_inc(S("f_act"), 1)
            act.wait_ge(S("f_act"), 2)
            A(F3[:], F3[:], ACT.Ln, bias=par("one", 0, 1, NH)).then_inc(S("f_act"), 1)
            act.wait_ge(S("ls_done"), 2)
            A(PC[:], LS[:], ACT.Exp, scale=-DECAY).then_inc(S("ex"), 1)
            act.wait_ge(S("ex"), 1)
            A(LS[:], LS[:], ACT.Exp, scale=DECAY).then_inc(S("ex"), 1)
            A(TMP[:], TMP[:], ACT.Exp, scale=-DECAY).then_inc(S("ex"), 1)
            act.wait_ge(S("ar_a"), 1)
            A(AV[:, :, :, 0], AR[:, :, :, 0], ACT.Copy)
            A(AV[:, :, :, 1], RKV[:, 2].rearrange("p i (c t) -> p i c t", c=NC), ACT.Copy).then_inc(S("av_ready"), 1)
            for q in range(4):
                act.wait_ge(S("ncb"), q + 1)
                A(NCB[:, 2 * q:2 * q + 2], BK8[q % 2].rearrange("p (h n) -> p h n", h=2), ACT.Copy).then_inc(S("ncb_out"), 1)
            for h in range(NH + 2):
                if h < NH:
                    act.wait_ge(S("fmax"), h + 1)
                    for r, (a, b) in enumerate(((0, P), (P, 384))):
                        last = A(SCO[:, h % 2, a:b], SCO[:, h % 2, a:b], ACT.Exp, bias=FST[:, h % 2, r:r + 1],
                                 accum_out=FST[:, h % 2, 2 + r:3 + r])
                    last.then_inc(S("fexp"), 1)
                if 1 <= h <= NH:
                    act.wait_ge(S("prt"), h)
                    if h >= 3:
                        act.wait_ge(S("fox_o"), h - 2)
                    A(PRT[:, (h - 1) % 2], BK8[5 + (h - 1) % 2][:, 0:384], ACT.Copy).then_inc(S("prt_out"), 1)
                if h >= 2:
                    g = h - 2
                    p0 = 64 * (g % 2)
                    act.wait_ge(S("fox_o"), g + 1)
                    if g == 0:
                        act.wait_ge(S("bk_ready"), 1)
                    A(YB[p0:p0 + 64, g // 2], BK8[1 + g % 2][p0:p0 + 64, 0:ROWS], ACT.Copy).then_inc(S("fo_out"), 1)
            for q in range(8):
                act.wait_ge(S("tr"), q + 1)
                A((BKR, AVR)[q % 2][:, q // 2], BK8[q % 2], ACT.Copy).then_inc(S("tr_out"), 1)
            for c in range(NC):
                act.wait_ge(S("w"), c + 1)
                A(WM[:, c * NH:(c + 1) * NH], BK8[c % 2][0:CH].rearrange("p (h n) -> p h n", h=NH), ACT.Copy).then_inc(S("w_out"), 1)
            for c in range(NC):
                act.wait_ge(S("u"), c + 1)
                A(UM[:, c], BK8[2 + c % 2][0:CH].rearrange("p (h n) -> p h n", h=NH), ACT.Copy).then_inc(S("u_out"), 1)
            act.wait_ge(S("y"), 1)
            A(YY[0:CH], pair(3)[0:CH], ACT.Copy).then_inc(S("yy_even"), 1)
            act.wait_ge(S("stat_sum"), STAT["var"] + 1)
            act.wait_ge(S("stat_bc"), STAT["mu"] + 1)
            A(STA[:], BK8[2][0:NH, 0:ROWS], ACT.Sqrt, scale=1.0 / 64, bias=par("epsl", 0, 1, NH)).then_inc(S("var_rt"), 1)
            act.wait_ge(ada_used, ADA)
            A(MROW[:], ADAP[0:MODR], ACT.Copy).then_inc(S("mod_rows"), 1)
            for name, dst, banks, sem in (("rwkv_proj", OA, [0, 1, 2, 3], "oa_out"), ("fox_proj", OB, [4, 5, 6, 0], "ob_out")):
                s0 = PHASE[name]
                m0 = MARK0[s0]
                for t in range(8):
                    if t % 4 == 0:
                        split_hi(act, s0 + t // 4 + 2)
                    act.wait_ge(psum_ready, m0 + t + 1)
                    A(dst[:, t], BK8[banks[t % 4]][:, 0:ROWS], ACT.Copy).then_inc(S(sem), 1)
                    if name == "fox_proj" and t == 5:
                        for k in range(KT):
                            square("nf", 1, k, "ctx_in", 16, NT2)

            def gates(name, dst, banks, out_sem, used_sem, before={}):
                s0 = PHASE[name]
                m0 = MARK0[s0]
                for t in range(16):
                    if t in before:
                        before[t]()
                    if t % 2 == 0:
                        split_hi(act, s0 + t // 2 + 2)
                    if t >= 4:
                        act.wait_ge(S(used_sem), (t - 4) // 2 + 1)
                    act.wait_ge(psum_ready, m0 + t + 1)
                    A(dst[:, t % 4], BK8[banks[t % 4]][:, 0:ROWS], ACT.Sigmoid).then_inc(S(out_sem), 1)

            gates("gates", SGA, [0, 1, 2, 3], "gate_out", "gate_used",
                  before={3: lambda: root("nf"),
                          6: lambda: [round_rows("nf", 1, k, (0, 1), NT2) for k in range(4)],
                          8: lambda: [round_rows("nf", 1, k, (0, 1), NT2) for k in range(4, KT)]})
            def out_square(phase, name, sem):
                split_hi(act, PHASE[phase] + 2)
                split_hi(act, PHASE[phase] + 3)
                load_sqrt()
                split_hi(act, PHASE[phase] + 4)
                for k in range(4):
                    square(name, 0, k, sem, k + 1)
                split_hi(act, PHASE[phase] + 5)
                for k in range(4, KT):
                    square(name, 0, k, sem, k + 1)

            out_square("out", "nc", "x_out1")
            root("nc")
            for k in range(KT):
                round_rows("nc", 0, k)
            ffn(1, "ffn2", 1)
            load_sqrt()
            for k in range(KT):
                square("nd", 0, k, "down_added", 168 + k + 1)
            root("nd")
            for k in range(KT):
                square("ne", 0, k, "nd_x", k + 1)
            root("ne")
            for k in range(KT):
                round_rows("ne", 0, k, (0, 0))
            ffn(2, "ffn3", 2)
            load_sqrt()
            for k in range(KT):
                square("ng", 0, k, "down_added", 256 + k + 1)
            root("ng")
            for k in range(2):
                square("nh", 1, k, "down_added", 256 + k + 1, NT3)
            for k in range(KT):
                round_rows("ng", 0, k, (24, 0))
                if k < 6:
                    square("nh", 1, k + 2, "down_added", 256 + k + 3, NT3)
            s0 = PHASE["ret_q"]
            split_hi(act, s0 + 2)
            root("nh")
            split_hi(act, s0 + 3)
            for u in (4, 5):
                for k in range(4 * u - 16, 4 * u - 12):
                    round_rows("nh", 1, k, (24, 1), NT3)
                split_hi(act, s0 + u)
            s0 = PHASE["ret_k"]
            for h in range(RH):
                split_hi(act, s0 + h + 2)
                for w in range(2):
                    act.wait_ge(S("rk_x"), 2 * h + w + 1)
                    A(RK[:, 1, 2 * h + w], BK8[(2 * h + w) % 4][:, ROWS:512], ACT.Copy).then_inc(S("rk_out"), 1)
            A(LG[:, 0], par("dec", 0, 8), ACT.Abs).then_inc(S("dec_a"), 1)
            act.wait_ge(S("dec_a"), 1)
            A(LG[:, 0], LG[:, 0], ACT.Exp, scale=-1.0).then_inc(S("dec_a"), 1)
            s0 = PHASE["ret_v"]
            for q in range(4):
                split_hi(act, s0 + 2 * q + 2)
                split_hi(act, s0 + 2 * q + 3)
                for r in range(4):
                    act.wait_ge(psum_ready, MARK0[s0 + 2 * q + 1] + r + 1)
                    A(RV[:, r, 512 * q:512 * (q + 1)], BK8[[4, 5, 6, 7, 0, 1, 2, 3][(4 * q + r) % 8]], ACT.Copy).then_inc(S("rv_out"), 1)
            def beside(n):
                split_hi(act, PHASE["four_in"] + n + 2)
                beside_out(n)

            def beside_out(n):
                if n < 4:
                    for r in range(2 if n % 2 else 0):
                        act.wait_ge(psum_ready, MARK0[PHASE["four_in"] + n] + r + 1)
                        A(FX[n // 2][r][:], BK8[4 + r], ACT.Copy).then_inc(S("fx_out"), 1)
                    return
                for t in (2 * n - 8, 2 * n - 7):
                    if t >= 2:
                        act.wait_ge(S("rg_used"), t - 1)
                    act.wait_ge(psum_ready, MARK0[PHASE["ret_g"]] + t + 1)
                    A(SGG[:, t % 2], BK8[4 + t % 2][:, 0:ROWS], ACT.Silu).then_inc(S("rg_out"), 1)

            for h in range(RH + 1):
                if h < RH:
                    act.wait_ge(S("d_arg"), h + 1)
                    A(DD[:, 0:2], DD[:, 0:2], ACT.Exp)
                    for kt in range(2):
                        A(DD[:, 2 + kt], IOTA[:], ACT.Exp, scale=LG[:, 4, h:h + 1], bias=LB[:, h, kt:kt + 1])
                        last = A(EB[:, kt], IOTA[:], ACT.Exp, scale=LG[:, 3, 4 + h:5 + h], bias=LB[:, h, 2 + kt:3 + kt])
                    last.then_inc(S("d_exp"), 1)
                split_hi(act, PHASE["four_in"] + 2 * h + 2)
                if h == RH:
                    beside_out(2 * h)
                if h >= 1:
                    act.wait_ge(S("ro_c"), h)
                    A(SQ[:], RO[:, 4 * (h - 1):4 * h], ACT.Square).then_inc(S("rvar_in"), 1)
                if h < RH:
                    beside_out(2 * h)
                    act.wait_ge(S("pv_done"), h + 1)
                    A(RO[:, 4 * h:4 * h + 4], pair(2), ACT.Copy).then_inc(S("ro_out"), 1)
                if h >= 1:
                    act.wait_ge(S("rvar_sum"), h)
                    if h >= 2:
                        act.wait_ge(S("rn_rec"), h - 1)
                    A(RST[:, 0], BK8[7][:, 0:ROWS], ACT.Sqrt, scale=1.0 / RDV, bias=par("epsr")).then_inc(S("rvar_rt"), 1)
                beside(2 * h + 1)
            for q in range(8):
                act.wait_ge(S("zz"), q + 1)
                if q >= 4:
                    act.wait_ge(S("xm"), 2 * (q // 2) - 2)
                A(ZZ[:, (q // 2) % 2, q % 2, 0:ROWS], BK8[6 + q % 2][:, 0:ROWS], ACT.Copy)
                A(ZZ[:, (q // 2) % 2, q % 2, ROWS:512], BK8[6 + q % 2][:, ROWS:512], ACT.Copy, scale=-1.0).then_inc(S("zz_out"), 1)
                if q in (1, 3):
                    beside(10 + q // 2)
            s0 = PHASE["ret_proj"]
            for t in range(8):
                split_hi(act, s0 + t + 2)
                act.wait_ge(psum_ready, MARK0[s0] + t + 1)
                A(OR[:, t], BK8[[2, 3, 6, 7][t % 4]][:, 0:ROWS], ACT.Copy).then_inc(S("or_out"), 1)
            s0 = PHASE["four_proj"]
            for t in range(8):
                if t % 2 == 0:
                    split_hi(act, s0 + t // 2 + 2)
                act.wait_ge(psum_ready, MARK0[s0] + t + 1)
                A(OF[:, t], BK8[[4, 5, 0, 1][t % 4]][:, 0:ROWS], ACT.Copy).then_inc(S("of_out"), 1)
            gates("gates2", SG2, [2, 3, 6, 7], "gate2_out", "gate2_used")
            out_square("out2", "ni", "x_out2")
            root("ni")
            for k in range(KT):
                round_rows("ni", 0, k, (48, 0))
            ffn(3, "ffn4", 1)
            load_sqrt()
            for k in range(KT):
                square("nj", 0, k, "down_added", 344 + k + 1)
            root("nj")

        @block.vector
        def _(dve):
            V = nc.vector
            count = [0]

            def link(ins):
                count[0] += 1
                ins.then_inc(S("dve_link"), 1)
                dve.wait_ge(S("dve_link"), count[0])

            def add_squares(name, k):
                dve.wait_ge(S("norm_sq"), KT * NORM[name] + k + 1)
                if k > 1:
                    dve.wait_ge(S("norm_acc"), 5 * NORM_ACC[name] + k - 1)
                V.tensor_tensor(NT[:, 0], NT[:, 0], NT[:, k], ALU.add).then_inc(S("norm_acc"), 1)

            def scale(name, half, k, gain, dst, sem="norm_t"):
                V.scalar_tensor_tensor(out=dst[:, k], in0=XC[:, half, k], scalar=gain(k), in1=RSTD[:],
                                       op0=ALU.mult, op1=ALU.mult).then_inc(S(sem), 1)

            def rest(name, half, k, shift=None, tmp=NT):
                dve.wait_ge(S("norm_hi"), KT * NORM_H[name] + k + 1)
                hi = H_HI[:, half, k].bitcast(F32)
                if shift is None:
                    ins = V.tensor_tensor(H_LO[:, half, k], tmp[:, k], hi, ALU.subtract)
                else:
                    ins = V.scalar_tensor_tensor(out=H_LO[:, half, k], in0=tmp[:, k], scalar=MOD[:, shift[0] + k, shift[1]:shift[1] + 1],
                                                 in1=hi, op0=ALU.add, op1=ALU.subtract)
                ins.then_inc(S("norm_h"), 1)

            def reciprocal(name):
                dve.wait_ge(S("norm_std"), NORM[name] + 1)
                link(V.reciprocal(RSTD[:], STD[:]))

            def norm(name, half, gain, shift=None, tmp=NT):
                reciprocal(name)
                norm_rows(name, half, gain, shift, tmp)

            def norm_rows(name, half, gain, shift=None, tmp=NT):
                for k in range(KT + 2):
                    if k < KT:
                        scale(name, half, k, gain, tmp)
                    if k >= 2:
                        rest(name, half, k - 2, shift, tmp)

            def ffn(f, name, halves, gate, then):
                n = halves * ROWS
                s0 = PHASE[name]
                m0 = MARK0[s0]

                def hidden(t, mark, dmark, j=None, j0=0):
                    tt = f * FT + t
                    x = (lambda a, m: a if j is None else (j - j0) * m + a)
                    dve.wait_ge(S("silu"), x(tt + 1, 2))
                    dve.wait_ge(psum_ready, x(mark, 12))
                    V.tensor_tensor(PROD[:, t % 2, 0:n], SILU[:, t % 2, 0:n], BK8[2 * (t % 2) + 1][:, 0:n],
                                    ALU.mult).then_inc(S("hid_prod"), 1)
                    dve.wait_ge(S("hid_prod"), x(tt + 1, 2))
                    if dmark is not None:
                        dve.wait_ge(psum_ready, x(dmark, 12))
                    V.tensor_copy(HID_HI[:, t % 2, 0:n], PROD[:, t % 2, 0:n]).then_inc(S("hid_hi"), 1)
                    dve.wait_ge(S("hid_hi"), x(tt + 1, 2))
                    V.tensor_tensor(HID_LO[:, t % 2, 0:n], PROD[:, t % 2, 0:n], HID_HI[:, t % 2, 0:n].bitcast(F32),
                                    ALU.subtract).then_inc(S("hid_lo"), 1)

                def add(i, ms, mark, j=None, j0=0):
                    for m in ms:
                        d = f * 88 + 8 * i + m
                        if m == 0 and d > 0:
                            dve.wait_ge(S("down_added"), d if j is None else (j - j0) * 8 + d)
                        dve.wait_ge(psum_ready, mark + m + 1 if j is None else (j - j0) * 12 + mark + m + 1)
                        for h in range(halves):
                            last = V.scalar_tensor_tensor(out=XC[:, h, m], in0=BK8[4 + m % 4][:, h * ROWS:(h + 1) * ROWS],
                                                          scalar=gate(h, m), in1=XC[:, h, m], op0=ALU.mult, op1=ALU.add)
                        last.then_inc(S("down_added"), 1)
                        if i == 10 and 2 <= m <= 6:
                            add_squares(then, m - 1)

                split_lo(dve, s0 + 2)
                hidden(0, m0 + 2, m0 if f else None)
                split_lo(dve, s0 + 3)

                def body(j, j0, i):
                    s, m = s0 + 2 + 3 * (i - 1), m0 + 4 + 12 * (i - 1)
                    hidden(2 * i - 1, m, m - 2, j, j0)
                    split_lo(dve, s + 2, j, j0)
                    add(i - 1, range(0, 4), m + 2, j, j0)
                    split_lo(dve, s + 3, j, j0)
                    add(i - 1, range(4, 8), m + 2, j, j0)
                    hidden(2 * i, m + 2, m + 10, j, j0)
                    split_lo(dve, s + 4, j, j0)

                with dve.Fori(1, 10) as j:
                    body(j, 1, 1)
                body(None, 0, 10)
                hidden(21, m0 + 124, m0 + 122)
                split_lo(dve, s0 + 34)
                add(10, range(8), m0 + 124)

            half_ = (lambda h, m: 0.5)
            V.memset(SCZ[:], 0.0).then_inc(S("scz_zero"), 1)
            V.memset(PRE[:, :, 0:1], 0.0)
            for k in range(1, 6):
                add_squares("na", k)
            dve.wait_ge(S("par_in"), 16)
            dve.wait_ge(S("con_in"), 16)
            reciprocal("na")
            split_lo(dve, 0)
            norm_rows("na", 0, lambda k: par("n1", k))
            split_lo(dve, 1)
            ffn(0, "ffn1", 1, half_, "nb")
            norm("nb", 0, lambda k: par("nm", k))

            def shift(dst, t0, nt):
                cur, prev = PRE[:, t0:t0 + nt, 1:ROWS + 1], PRE[:, t0:t0 + nt, 0:ROWS]
                link(V.tensor_tensor(TMP[:, 0:nt], prev, cur, ALU.subtract))
                for t in range(nt):
                    last = V.scalar_tensor_tensor(out=dst[:, t], in0=TMP[:, t], scalar=par("mu", t0 + t), in1=cur[:, t],
                                                  op0=ALU.mult, op1=ALU.add)
                if dst is LOR:
                    last.then_inc(S("lor"), 1)
                    dve.wait_ge(S("lor"), 1)
                else:
                    link(last)

            s0 = PHASE["rwkv_in"]
            for u in range(7):
                split_lo(dve, s0 + u + 2)
                if u in (1, 3, 5, 6):
                    dve.wait_ge(S("pre_out"), 2 * u + 2)
                    if u < 6:
                        shift(RKV[:, u // 2], 2 * u - 2, 4)
                    else:
                        shift(LOR, 12, 2)
            R_, K_, V_ = RKV[:, 0], RKV[:, 1], RKV[:, 2]
            s0 = PHASE["fox_qk"]
            for u in range(4):
                split_lo(dve, s0 + u + 2)
                if u == 1:
                    for i in range(IT):
                        last = V.tensor_scalar(KK[:, i], K_[:, i], par("kk", i), None, ALU.mult)
                    link(last)
                    V.tensor_tensor(TMP[:], KK[:], KK[:], ALU.mult).then_inc(S("stat_in"), 1)
            s0 = PHASE["fox_v"]
            split_lo(dve, s0 + 2)
            split_lo(dve, s0 + 3)
            dve.wait_ge(S("stat_sum"), STAT["kk"] + 1)
            V.tensor_scalar(STA[:], BK8[2][0:NH, 0:ROWS], 1e-24, None, ALU.max).then_inc(S("kk_max"), 1)
            dve.wait_ge(S("aa_done"), 1)
            for i in range(IT):
                last = V.tensor_scalar(TMP[:, i], AA[:, i], 1.0, par("ka", i), ALU.subtract, ALU.mult)
            link(last)
            link(V.scalar_tensor_tensor(out=K_, in0=TMP[:], scalar=1.0, in1=K_, op0=ALU.add, op1=ALU.mult))
            for i in range(IT):
                last = V.scalar_tensor_tensor(out=TMP[:, i], in0=R_[:, i], scalar=par("rk", i), in1=K_[:, i],
                                              op0=ALU.mult, op1=ALU.mult)
            last.then_inc(S("stat_in"), 1)
            dve.wait_ge(S("kk_rt"), 1)
            V.reciprocal(STA[:], STA[:]).then_inc(S("stat_st"), 1)
            dve.wait_ge(S("stat_bc"), STAT["kk"] + 1)
            link(V.tensor_tensor(KK[:], KK[:], pair(3), ALU.mult))
            dve.wait_ge(S("stat_sum"), STAT["bon"] + 1)
            V.tensor_copy(STA[:], BK8[2][0:NH, 0:ROWS]).then_inc(S("stat_st"), 1)
            dve.wait_ge(S("gg_done"), 1)
            dve.wait_ge(S("stat_bc"), STAT["bon"] + 1)
            link(V.tensor_tensor(BO[:], V_, pair(5), ALU.mult))
            dve.wait_ge(S("masks_in"), 16)
            dve.wait_ge(S("fqk_out"), 8)
            for name, X, g in (("fq", FQ, "qn"), ("fk", FK, "kn")):
                V.tensor_tensor(TMP[:], X[:], X[:], ALU.mult).then_inc(S("stat_in"), 1)
                dve.wait_ge(S(f"{name}_rt"), 1)
                V.reciprocal(STA[:], STA[:]).then_inc(S("stat_st"), 1)
                dve.wait_ge(S("stat_bc"), STAT[name] + 1)
                V.scalar_tensor_tensor(out=X[:], in0=pair(3 if name == "fq" else 5), scalar=par(g), in1=X[:],
                                       op0=ALU.mult, op1=ALU.mult).then_inc(S(f"{name}_norm"), 1)
            dve.wait_ge(S("lora_g"), 1)
            link(V.tensor_scalar(F1[:], LOR[96:96 + NH, 1], par("fb")[96:96 + NH], None, ALU.add))
            V.tensor_scalar(F2[:], F1[:], 0.0, None, ALU.min).then_inc(S("f_x"), 1)
            link(V.memset(F4[:], 1.0))
            dve.wait_ge(S("sg_done"), 1)
            for i in range(IT):
                for c in range(0, ROWS, CH):
                    last = V.tensor_tensor_scan(LS[:, i, c:c + CH], con("ones")[:, 0:CH], SG[:, i, c:c + CH], 0.0, ALU.mult, ALU.add)
            last.then_inc(S("ls_done"), 1)
            dve.wait_ge(S("ls_done"), 1)
            V.tensor_tensor(TMP[:], LS[:], SG[:], ALU.subtract).then_inc(S("ls_done"), 1)
            dve.wait_ge(S("f_act"), 3)
            link(V.tensor_tensor(F3[:], F3[:], F2[:], ALU.subtract))
            V.tensor_tensor_scan(STB[:], F4[:], F3[:], 0.0, ALU.mult, ALU.add).then_inc(S("lf_cum"), 1)
            by_chunk = (lambda x: x.rearrange("p i (c t) -> p i c t", c=NC))
            dve.wait_ge(S("ex"), 3)
            V.scalar_tensor_tensor(out=AR[:, :, :, 0], in0=by_chunk(KK[:]), scalar=-1.0, in1=by_chunk(TMP[:]),
                                   op0=ALU.mult, op1=ALU.mult).then_inc(S("ar_a"), 1)
            V.tensor_tensor(AR[:, :, :, 1], by_chunk(R_), by_chunk(PC[:]), ALU.mult)
            V.tensor_tensor(BK[:, :, :, 1], by_chunk(K_), by_chunk(LS[:]), ALU.mult)
            link(V.tensor_tensor(KK[:], KK[:], AA[:], ALU.mult))
            V.tensor_tensor(BK[:, :, :, 0], by_chunk(KK[:]), by_chunk(LS[:]), ALU.mult).then_inc(S("bk_ready"), 1)
            diag = (lambda h: SCO[:, h % 2].rearrange("p (b n) -> p b n", n=P)[:, 0:3:2])
            for h in range(NH + 1):
                if h < NH:
                    dve.wait_ge(S("scores"), h + 1)
                    if h < 8 and h % 2 == 0:
                        dve.wait_ge(S("ncb_out"), h // 2 + 1)
                    if h >= 2:
                        dve.wait_ge(S("prt"), h - 1)
                    b = BK8[3 + h % 2]
                    V.tensor_tensor(SCO[:, h % 2, 0:P], b[:, 0:P], NCB[:, h, 0:P], ALU.add)
                    V.tensor_tensor(SCO[:, h % 2, P:384], b[:, P:384], NCB[:, h], ALU.add).then_inc(S("sco_out"), 1)
                    dve.wait_ge(S("sco_out"), h + 1)
                    link(V.tensor_tensor(diag(h), diag(h), con("causal").unsqueeze(1).to_broadcast([P, 2, P]), ALU.add))
                    V.tensor_reduce(FST[:, h % 2, 0:1], SCO[:, h % 2, 0:P], AX_X, ALU.max, negate=True)
                    V.tensor_reduce(FST[:, h % 2, 1:2], SCO[:, h % 2, P:384], AX_X, ALU.max, negate=True).then_inc(S("fmax"), 1)
                if h >= 1:
                    g = (h - 1) % 2
                    dve.wait_ge(S("fexp"), h)
                    link(V.reciprocal(FST[:, g, 4:6], FST[:, g, 2:4]))
                    V.tensor_scalar(SCO[:, g, 0:P], SCO[:, g, 0:P], FST[:, g, 4:5], None, ALU.mult)
                    V.tensor_scalar(SCO[:, g, P:384], SCO[:, g, P:384], FST[:, g, 5:6], None, ALU.mult).then_inc(S("probs"), 1)
            for q in range(8):
                c, p = q // 2, q % 2
                dve.wait_ge(S("tt"), q + 1)
                V.tensor_tensor(TT[:, c].rearrange("p (i q) n -> p i q n", q=2)[:, :, p],
                                BK8[2 + q % 4].rearrange("p (i n) -> p i n", n=P),
                                con("tmask").unsqueeze(1).to_broadcast([P, IT, P]), ALU.mult).then_inc(S("tt_out"), 1)
            dve.wait_ge(S("tt_out"), 8)
            eye = con("ident", CH)[:, 0:CH].unsqueeze(1).to_broadcast([CH, NH, CH])
            heads = (lambda b: BK8[b][0:CH].rearrange("p (h n) -> p h n", n=CH))
            lmask = (lambda lev: con("lmask", CH)[:, lev * CH:(lev + 1) * CH].unsqueeze(1).to_broadcast([CH, NH, CH]))
            link(V.tensor_tensor(XT[:].rearrange("p c h n -> p (c h) n"), TT[0:CH, :, :, 0:CH].rearrange("p c h n -> p (c h) n"),
                                 con("l0t", CH).unsqueeze(1).to_broadcast([CH, NC * NH, CH]), ALU.mult))
            for n in range(NC):
                dve.wait_ge(S("z"), n + 1)
                V.tensor_tensor(XM[:, n], heads(n % 2), lmask(0), ALU.mult).then_inc(S("z_out"), 1)
                V.tensor_tensor(XT[:, n], XT[:, n], eye, ALU.add).then_inc(S("x_out"), 1)
                dve.wait_ge(S("z_out"), n + 1)
                V.tensor_tensor(XM[:, n], XM[:, n], eye, ALU.add).then_inc(S("x_out"), 1)

            def z_mask(n):
                dve.wait_ge(S("z"), n + 1)
                V.tensor_tensor(ZM[:, n % NC], heads(n % 2), lmask(n // NC), ALU.mult).then_inc(S("z_out"), 1)

            z_mask(NC)
            z_mask(NC + 1)
            for n in range(NC, 6 * NC):
                c = n % NC
                if n < 5 * NC:
                    dve.wait_ge(S("xz"), n - NC + 1)
                    V.tensor_tensor(XM[:, c], XM[:, c], heads(2 + n % 2), ALU.add).then_inc(S("x_out"), 1)
                dve.wait_ge(S("zx"), n - NC + 1)
                V.tensor_tensor(XT[:, c], XT[:, c], heads(4 + n % 2), ALU.add).then_inc(S("x_out"), 1)
                if n + 2 < 6 * NC:
                    z_mask(n + 2)
            dve.wait_ge(S("x_out"), 11 * NC)
            V.memset(ST[:, 0], 0.0).then_inc(S("state"), 1)
            for c in range(NC):
                dve.wait_ge(S("gt"), c + 1)
                V.tensor_copy(GT[:, c], BK8[4 + c % 2][:, 0:256].rearrange("p (i n) -> p i n", n=CH)).then_inc(S("gt_out"), 1)
            dve.wait_ge(S("u_out"), 4)
            for c in range(NC):
                dve.wait_ge(S("sa"), c + 1)
                for p in range(2):
                    V.tensor_tensor(AVR[0:CH, c].rearrange("p (i q v) -> p i q v", q=2, v=CH)[:, :, p],
                                    BK8[p][0:CH, 0:256].rearrange("p (i v) -> p i v", v=CH),
                                    UM[:, c].rearrange("p (i q) v -> p i q v", q=2)[:, :, p], ALU.add).then_inc(S("sa_out"), 1)
                if c < NC - 1:
                    dve.wait_ge(S("st"), c + 1)
                    link(V.tensor_tensor(ST[:, c + 1], BK8[2][:, 0:256].rearrange("p (i v) -> p i v", v=CH), ST[:, c], ALU.add))
                    pc = PC[:].rearrange("p i (c t) -> p i c t", c=NC)[:, :, c, CH - 1:CH].to_broadcast([P, IT, CH])
                    V.tensor_tensor(ST[:, c + 1], ST[:, c + 1], pc, ALU.mult).then_inc(S("state"), 1)
            dve.wait_ge(S("y"), 1)
            V.tensor_copy(YY[CH:P], pair(5)[CH:P]).then_inc(S("stat_in"), 1)
            dve.wait_ge(S("stat_sum"), STAT["mu"] + 1)
            V.tensor_scalar(STA[:], BK8[2][0:NH, 0:ROWS], 1.0 / CH, None, ALU.mult).then_inc(S("stat_st"), 1)
            dve.wait_ge(S("stat_bc"), STAT["mu"] + 1)
            link(V.tensor_tensor(YY[:], YY[:], pair(3), ALU.subtract))
            V.tensor_tensor(YS[:], YY[:], YY[:], ALU.mult).then_inc(S("stat_in"), 1)
            dve.wait_ge(S("var_rt"), 1)
            V.reciprocal(STA[:], STA[:]).then_inc(S("stat_st"), 1)
            dve.wait_ge(S("stat_bc"), STAT["var"] + 1)
            link(V.tensor_tensor(YY[:], YY[:], pair(5), ALU.mult))
            for i in range(IT):
                last = V.tensor_scalar(YY[:, i], YY[:, i], par("lnxg", i), par("lnxb", i), ALU.mult, ALU.add)
            link(last)
            link(V.tensor_tensor(YY[:], YY[:], BO[:], ALU.add))
            link(V.tensor_tensor(YY[:], YY[:], GG[:], ALU.mult))
            link(V.tensor_copy(YA_HI[:], YY[:]))
            V.tensor_tensor(YA_LO[:], YY[:], YA_HI[:].bitcast(F32), ALU.subtract).then_inc(S("ya_split"), 1)
            link(V.tensor_copy(YB_HI[:], YB[:]))
            V.tensor_tensor(YB_LO[:], YB[:], YB_HI[:].bitcast(F32), ALU.subtract).then_inc(S("yb_split"), 1)
            for u in range(2):
                split_lo(dve, PHASE["rwkv_proj"] + u + 2)
            dve.wait_ge(S("mod_tr"), 1)
            dve.wait_ge(S("bada_in"), 16)
            link(V.tensor_tensor(MOD[:].rearrange("p (q j) n -> p j q n", j=4), MOD[:].rearrange("p (q j) n -> p j q n", j=4),
                                 ADAP[:, 0:4 * MODR].rearrange("p (j q n) -> p j q n", j=4, n=2), ALU.add))
            for g, (chunk, who, m) in enumerate(((1, 0, "m1"), (1, 1, "m1"), (4, 0, "m2"), (4, 1, "m2"), (7, 0, "m3"))):
                V.scalar_tensor_tensor(out=GAIN[:, g], in0=MOD[:, 8 * chunk:8 * chunk + 8, who], scalar=1.0, in1=par(m, 0, 8),
                                       op0=ALU.add, op1=ALU.mult)
            for g, (chunk, who, f) in enumerate(((2, 0, 0.5), (2, 1, 0.5), (5, 0, 1.0), (8, 0, 0.5))):
                last = V.tensor_scalar(GATE[:, g], MOD[:, 8 * chunk:8 * chunk + 8, who], f, None, ALU.mult)
            last.then_inc(S("mod_out"), 1)
            dve.wait_ge(S("mod_out"), 1)
            for u in range(2):
                split_lo(dve, PHASE["fox_proj"] + u + 2)

            def gates(name, sg, mt, oa, ob, hi, lo, out_sem, used_sem, split_sem, oa_sem, ob_sem, behind={}):
                s0 = PHASE[name]
                dve.wait_ge(S(oa_sem), 8)
                dve.wait_ge(S(ob_sem), 8)
                for m in range(KT):
                    split_lo(dve, s0 + m + 2)
                    dve.wait_ge(S(out_sem), 2 * m + 2)
                    w = mt[:, m % 2]
                    V.tensor_tensor(w[:, 0], sg[:, (2 * m) % 4], oa[:, m], ALU.mult)
                    V.tensor_tensor(w[:, 1], sg[:, (2 * m + 1) % 4], ob[:, m], ALU.mult).then_inc(S(used_sem), 1)
                    dve.wait_ge(S(used_sem), m + 1)
                    link(V.tensor_tensor(w[:, 2], w[:, 0], w[:, 1], ALU.add))
                    link(V.tensor_copy(hi[:, m], w[:, 2]))
                    last = V.tensor_tensor(lo[:, m], w[:, 2], hi[:, m].bitcast(F32), ALU.subtract)
                    last.then_inc(S(split_sem), 1)
                    if m in behind:
                        behind[m]()

            def out_add(name, banks, gate, sem, then):
                s0 = PHASE[name]
                for m in range(KT):
                    if m % 2 == 0:
                        split_lo(dve, s0 + m // 2 + 2)
                    dve.wait_ge(psum_ready, MARK0[s0] + m + 1)
                    V.scalar_tensor_tensor(out=XC[:, 0, m], in0=BK8[banks[m % 4]][:, 0:ROWS], scalar=gate(m), in1=XC[:, 0, m],
                                           op0=ALU.mult, op1=ALU.add).then_inc(S(sem), 1)
                    for k in {5: (1, 2, 3), 6: (4, 5)}.get(m, ()):
                        add_squares(then, k)

            def scale_nf(k0, k1):
                for k in range(k0, k1):
                    scale("nf", 1, k, lambda k: GAIN[:, 1, k:k + 1], NT2)

            def rest_nf(k0, k1):
                for k in range(k0, k1):
                    rest("nf", 1, k, (0, 1), NT2)

            gates("gates", SGA, MT, OA, OB, M_HI, M_LO, "gate_out", "gate_used", "m_split", "oa_out", "ob_out",
                  behind={1: lambda: [reciprocal("nf"), scale_nf(0, 2)], 2: lambda: scale_nf(2, 5),
                          3: lambda: [scale_nf(5, 8), rest_nf(0, 1)], 4: lambda: rest_nf(1, 4), 5: lambda: rest_nf(4, 7),
                          6: lambda: rest_nf(7, 8)})
            out_add("out", [4, 5, 6, 3], lambda m: 1.0, "x_out1", "nc")
            norm("nc", 0, lambda k: par("n2", k))
            ffn(1, "ffn2", 1, half_, "nd")
            reciprocal("nd")
            for k in range(KT):
                scale("nd", 0, k, lambda k: par("nf", k), XC[:, 0], "nd_x")
            norm("ne", 0, lambda k: GAIN[:, 0, k:k + 1], (0, 0))
            ffn(2, "ffn3", 2, lambda h, m: GATE[:, h, m:m + 1], "ng")
            norm("ng", 0, lambda k: GAIN[:, 2, k:k + 1], (24, 0))
            split_lo(dve, PHASE["ret_q"] + 2)
            reciprocal("nh")

            def rotate(ps_e, ps_o, dst, h, sem):
                link(V.tensor_tensor(RT[:, 0], ps_e, ROPE[:, 0], ALU.mult))
                V.tensor_tensor(RT[:, 2], ps_e, ROPE[:, 1], ALU.mult).then_inc(S(sem), 1)
                link(V.tensor_tensor(RT[:, 1], ps_o, ROPE[:, 1], ALU.mult))
                V.tensor_tensor(RT[:, 3], ps_o, ROPE[:, 0], ALU.mult).then_inc(S(sem), 1)
                dve.wait_ge(S(sem), 2 * h + 2)
                V.tensor_tensor(dst[:, 2 * h], RT[:, 0], RT[:, 1], ALU.subtract)
                link(V.tensor_tensor(dst[:, 2 * h + 1], RT[:, 2], RT[:, 3], ALU.add))

            dve.wait_ge(S("rope_in"), 16)
            s0 = PHASE["ret_q"]

            def rotate_q(h):
                dve.wait_ge(psum_ready, MARK0[s0] + 2 * h + 2)
                rotate(BK8[4 + (2 * h) % 4][:, 0:ROWS], BK8[4 + (2 * h + 1) % 4][:, 0:ROWS], RQ, h, "rq_out")

            def scale_nh(k0, k1):
                for k in range(k0, k1):
                    scale("nh", 1, k, lambda k: GAIN[:, 3, k:k + 1], NT3)

            def rest_nh(k0, k1):
                for k in range(k0, k1):
                    rest("nh", 1, k, (24, 1), NT3)

            rotate_q(0)
            split_lo(dve, s0 + 3)
            scale_nh(0, 4)
            rotate_q(1)
            scale_nh(4, KT)
            rest_nh(0, 4)
            split_lo(dve, s0 + 4)
            rest_nh(4, KT)
            rotate_q(2)
            split_lo(dve, s0 + 5)
            rotate_q(3)
            s0 = PHASE["ret_k"]
            for h in range(RH):
                split_lo(dve, s0 + h + 2)
                dve.wait_ge(psum_ready, MARK0[s0] + 2 * h + 2)
                rotate(BK8[(2 * h) % 4][:, 0:ROWS], BK8[(2 * h + 1) % 4][:, 0:ROWS], RK[:, 0], h, "rk_x")
            for s in range(PHASE["ret_v"], PHASE["ret_v"] + 8):
                split_lo(dve, s + 2)
            dve.wait_ge(S("dec_a"), 2)
            link(V.tensor_scalar(LG[:, 1], LG[:, 0], 2.0, None, ALU.add))
            link(V.reciprocal(LG[:, 1], LG[:, 1]))
            link(V.tensor_tensor(LG[:, 0], LG[:, 0], LG[:, 1], ALU.mult))
            link(V.tensor_tensor(LG[:, 1], LG[:, 0], LG[:, 0], ALU.mult))
            link(V.tensor_scalar(LG[:, 2], LG[:, 1], 1.0 / 17, None, ALU.mult))
            for n in (15, 13, 11, 9, 7, 5, 3):
                link(V.scalar_tensor_tensor(out=LG[:, 2], in0=LG[:, 2], scalar=1.0 / n, in1=LG[:, 1], op0=ALU.add, op1=ALU.mult))
            link(V.scalar_tensor_tensor(out=LG[:, 2], in0=LG[:, 2], scalar=1.0, in1=LG[:, 0], op0=ALU.add, op1=ALU.mult))
            link(V.tensor_scalar(LG[:, 1], par("dec", 0, 8), 0.0, None, ALU.min))
            link(V.scalar_tensor_tensor(out=LG[:, 4], in0=LG[:, 2], scalar=-2.0, in1=LG[:, 1], op0=ALU.mult, op1=ALU.add))
            link(V.tensor_scalar(LG[:, 3], LG[:, 4], -1.0, None, ALU.mult))
            for h in range(RH):
                V.tensor_scalar(LB[:, h, 0:2], par("jcol", 2, 2), LG[:, 4, h:h + 1], None, ALU.mult)
                last = V.tensor_scalar(LB[:, h, 2:4], par("jcol", 4, 2), LG[:, 4, 4 + h:5 + h], None, ALU.mult)
            link(last)
            dve.wait_ge(S("iota_in"), 16)
            for kt in range(2):
                V.tensor_scalar(T1[:, kt], IOTA[:], par("jcol", kt), 0.0, ALU.subtract, ALU.max)
                last = V.tensor_scalar(T2[:, kt], IOTA[:], par("jcol", kt), 0.0, ALU.subtract, ALU.min)
            link(last)

            def decay_arg(h):
                link(V.tensor_scalar(DD[:, 0:2], T1[:], LG[:, 4, h:h + 1], None, ALU.mult))
                V.scalar_tensor_tensor(out=DD[:, 0:2], in0=T2[:], scalar=LG[:, 3, 4 + h:5 + h], in1=DD[:, 0:2],
                                       op0=ALU.mult, op1=ALU.add).then_inc(S("d_arg"), 1)

            def tile_sum(x):
                link(V.tensor_tensor(SQ[:, 0:2], x[:, 0:2], x[:, 2:4], ALU.add))
                V.tensor_tensor(SQ[:, 0], SQ[:, 0], SQ[:, 1], ALU.add).then_inc(S("tile_sum"), 1)

            def r_split(h):
                t = slice(4 * h, 4 * h + 4)
                link(V.tensor_copy(R_HI[:, t], RO[:, t]))
                V.tensor_tensor(R_LO[:, t], RO[:, t], R_HI[:, t].bitcast(F32), ALU.subtract).then_inc(S("r_split"), 1)

            def beside(n):
                split_lo(dve, PHASE["four_in"] + n + 2)

            def gate_out(n):
                if n < 4:
                    return
                for t in (2 * n - 8, 2 * n - 7):
                    dve.wait_ge(S("rg_out"), t + 1)
                    V.scalar_tensor_tensor(out=RO[:, t], in0=SGG[:, t % 2], scalar=par("gn", t), in1=RO[:, t],
                                           op0=ALU.mult, op1=ALU.mult).then_inc(S("rg_used"), 1)

            decay_arg(0)
            for h in range(RH + 1):
                if h < RH:
                    dve.wait_ge(S("d_exp"), h + 1)
                    V.tensor_tensor(DD[:, 2:4], DD[:, 2:4], EB[:], ALU.add)
                    for kt in range(2):
                        blk = DD[:, kt, kt * P:(kt + 1) * P]
                        last = V.tensor_tensor(blk, blk, con("ident"), ALU.add)
                    link(last)
                    dve.wait_ge(S("rscores"), h + 1)
                    if h >= 1:
                        dve.wait_ge(S("pv_done"), h)
                    V.scalar_tensor_tensor(out=PT[:], in0=pair(0), scalar=1.0 / 16, in1=DD[:], op0=ALU.mult, op1=ALU.mult)\
                        .then_inc(S("pt_out"), 1)
                    dve.wait_ge(S("pt_out"), h + 1)
                if h >= 1:
                    g = h - 1
                    ro = RO[:, 4 * g:4 * g + 4]
                    dve.wait_ge(S("ro_out"), h)
                    tile_sum(ro)
                if h < RH - 1:
                    decay_arg(h + 1)
                if h < RH:
                    beside(2 * h)
                if h >= 1:
                    dve.wait_ge(S("mean_sum"), h)
                    V.scalar_tensor_tensor(out=ro, in0=BK8[6][:, 0:ROWS].unsqueeze(1).to_broadcast([P, 4, ROWS]), scalar=-1.0 / RDV,
                                           in1=ro, op0=ALU.mult, op1=ALU.add).then_inc(S("ro_c"), 1)
                    dve.wait_ge(S("ro_c"), h)
                if h >= 1:
                    dve.wait_ge(S("rvar_in"), h)
                    tile_sum(SQ)
                if h == RH:
                    beside(2 * h)
                gate_out(2 * h)
                if h == RH:
                    dve.wait_ge(S("pv_done"), RH)
                    dve.wait_ge(S("rg_used"), 8)
                    r_split(0)
                    r_split(1)
                if h >= 1:
                    dve.wait_ge(S("rvar_rt"), h)
                    V.reciprocal(RST[:, 1], RST[:, 0]).then_inc(S("rn_rec"), 1)
                    dve.wait_ge(S("rn_rec"), h)
                    V.tensor_tensor(ro, ro, RST[:, 1].unsqueeze(1).to_broadcast([P, 4, ROWS]), ALU.mult).then_inc(S("rn_done"), 1)
                    dve.wait_ge(S("rn_done"), h)
                beside(2 * h + 1)
                gate_out(2 * h + 1)
            dve.wait_ge(S("rg_used"), 12)
            r_split(2)
            beside(10)
            for q in range(8):
                if q in (0, 2):
                    gate_out(10 + q // 2)
                    if q == 0:
                        beside(11)
                    else:
                        dve.wait_ge(S("rg_used"), 16)
                        r_split(3)
                dve.wait_ge(S("xm"), q + 1)
                link(V.tensor_copy(X_HI[:, q], BK8[q % 2][:, 0:ROWS]))
                V.tensor_tensor(X_LO[:, q], BK8[q % 2][:, 0:ROWS], X_HI[:, q].bitcast(F32), ALU.subtract).then_inc(S("xm_out"), 1)
            for s in range(PHASE["ret_proj"], PHASE["ret_proj"] + 8):
                split_lo(dve, s + 2)
            for s in range(PHASE["four_proj"], PHASE["four_proj"] + 4):
                split_lo(dve, s + 2)
            gates("gates2", SG2, MT2, OR, OF, M2_HI, M2_LO, "gate2_out", "gate2_used", "m2_split", "or_out", "of_out")
            out_add("out2", [4, 5, 0, 1], lambda m: GATE[:, 2, m:m + 1], "x_out2", "ni")
            norm("ni", 0, lambda k: GAIN[:, 4, k:k + 1], (48, 0))
            ffn(3, "ffn4", 1, lambda h, m: GATE[:, 3, m:m + 1], "nj")
            reciprocal("nj")
            for k in range(KT):
                scale("nj", 0, k, lambda k: par("mf", k), NT, "final")



def _tiles(w, kt=KT):
    k, c = w.shape
    return w.reshape(kt, P, c // P, P).transpose(2, 1, 0, 3).reshape(c // P, P, kt * P)


def _units(tiles, per):
    n = tiles.shape[0] // per
    return tiles.reshape(n, per, P, -1).transpose(0, 2, 1, 3).reshape(n, P, UNIT)


def _ffn_units(w1, w3, w2):
    a = np.concatenate([_tiles(w1)[:, :, None], _tiles(w3)[:, :, None]], axis=2).reshape(FT, P, UNIT)
    d = w2.reshape(FT // 2, 2, P, DM).transpose(0, 2, 1, 3).reshape(FT // 2, P, UNIT)
    out = [a[0], a[1]]
    for j in range(1, 11):
        out += [a[2 * j], d[j - 1], a[2 * j + 1]]
    return out + [d[10]]


def _row_units(w):
    c = w.shape[1]
    t = w.reshape(2, 4, P, c // 512, 512).transpose(3, 0, 2, 1, 4)
    return list(t.reshape(c // 512 * 2, P, UNIT))


def _gate_units(w):
    a, b = _tiles(w[:, :DM]), _tiles(w[:, DM:])
    return list(np.concatenate([a[:, :, None], b[:, :, None]], axis=2).reshape(KT, P, UNIT))


def _columns(v, n):
    return np.asarray(v).reshape(n, P).T


def _stream(i):
    w = {n: np.asarray(a) for n, a in i.items()}
    win, win2 = w["w_in"][0], w["w_in_2"][0]
    z = np.zeros((DM, 64), np.float32)
    r0 = 3 * DA
    s0 = r0 + 32 + 32 + 96
    low = np.concatenate([win[:, r0:r0 + 64], z, win[:, r0 + 64:s0], win[:, s0 + 3 * DA:s0 + 3 * DA + NH],
                          z[:, :P - 96 - NH]], axis=1)
    out = _ffn_units(w["ffn1_w1"][0], w["ffn1_w3"][0], w["ffn1_w2"][0])
    out += list(_units(_tiles(np.concatenate([win[:, :r0], low], axis=1)), 2))
    out += list(_units(_tiles(win[:, s0:s0 + 2 * DA]), 2))
    out += _row_units(win[:, s0 + 2 * DA:s0 + 3 * DA])
    out += list(_units(_tiles(w["rwkv_proj"][0], 4), 4)) + list(_units(_tiles(w["fox_proj"][0], 4), 4))
    out += _gate_units(win[:, s0 + 3 * DA + NH:])
    out += list(_units(_tiles(w["w_out"][0]), 2))
    out += _ffn_units(w["ffn2_w1"][0], w["ffn2_w3"][0], w["ffn2_w2"][0])
    a, b = w["w13_ffn1_2"][0], w["w13_ffn2_2"][0]
    out += _ffn_units(a[:, :FF], a[:, FF:], w["w2_ffn1_2"][0])

    def even_odd(x):
        return x.reshape(DM, RH, P, 2).transpose(0, 1, 3, 2).reshape(DM, DM)

    out += list(_units(_tiles(even_odd(win2[:, :DM])), 2))
    out += list(_units(_tiles(even_odd(win2[:, DM:2 * DM])), 2))
    out += _row_units(win2[:, 2 * DM:4 * DM])
    out += _row_units(win2[:, 6 * DM:7 * DM])
    out += list(_units(_tiles(win2[:, 4 * DM:6 * DM]), 2))
    out += list(_tiles(w["p_ret_2"][0], 16))
    out += list(_units(_tiles(w["p_four_2"][0]), 2))
    out += _gate_units(win2[:, 7 * DM:])
    out += list(_units(_tiles(w["w_out_2"][0]), 2))
    out += _ffn_units(b[:, :FF], b[:, FF:], w["w2_ffn2_2"][0])
    ada = _row_units(w["w_ada_2"][0])
    assert len(out) == NW and len(ada) == ADA
    return np.ascontiguousarray(np.stack([out[n] if kind == "w" else ada[n] for kind, n in ORDER]))


def _params(i):
    w = {n: np.asarray(a) for n, a in i.items()}
    par = np.zeros((P, NPAR), np.float32)

    def put(name, cols):
        a, b = PCOLS[name]
        par[:, a:b] = cols

    for name, key, n in (("n1", "ffn1_norm", 8), ("nm", "mix_norm", 8), ("w0", "rwkv_w0", 4), ("a0", "rwkv_a0", 4),
                         ("kk", "rwkv_k_k", 4), ("ka", "rwkv_k_a", 4), ("rk", "rwkv_r_k", 4), ("lnxg", "rwkv_lnx_g", 4),
                         ("lnxb", "rwkv_lnx_b", 4), ("n2", "ffn2_norm", 8), ("nf", "final_norm", 8), 
                         ("m1", "norm_ffn1_2", 8), ("m2", "norm_mix_2", 8), ("gn", "ret_gn_w_2", 16),
                         ("m3", "norm_ffn2_2", 8), ("mf", "norm_final_2", 8)):
        put(name, _columns(w[key], n))
    mu = w["shift_mu"][0]
    z = np.zeros(64, np.float32)
    put("mu", _columns(np.concatenate([mu[:3 * DA + 64], z, mu[3 * DA + 64:], z[:32]]), 14))
    fb = np.zeros((P, 1), np.float32)
    fb[96:96 + NH, 0] = w["fox_f_bias"][0]
    put("fb", fb)
    for name, key in (("qn", "fox_q_norm"), ("kn", "fox_k_norm")):
        put(name, np.concatenate([w[key][0], w[key][0]])[:, None])
    c = np.stack([w["c_2"][0].reshape(KT, P).T, w["c_ctx_2"].reshape(KT, P).T], axis=2)
    put("c", c.reshape(P, 16))
    put("dec", np.broadcast_to(np.concatenate([w["decay_fwd_2"][0], w["decay_bwd_2"][0]])[None], (P, 8)))
    put("epsr", 1e-6)
    put("epsl", 64e-5)
    put("epsq", 64e-6)
    put("one", 1.0)
    j = np.arange(2)[None] * P + np.arange(P)[:, None]
    put("jcol", np.concatenate([j, ROWS - j, ROWS + j], axis=1))
    return par


def _consts():
    con = np.zeros((P, NCON), np.float32)

    def put(name, x):
        a, b = CCOLS[name]
        con[:x.shape[0], a:b] = x.reshape(x.shape[0], -1)

    r = np.arange(P)
    put("ident", np.eye(P))
    put("ones", np.ones((P, P)))
    head = np.arange(IT)[None] * 2 + r[:, None] // 64
    put("sel", (head[:, :, None] == np.arange(NH)).astype(np.float32))
    put("bc", (head.T[None] == np.arange(NH)[:, None, None]).astype(np.float32))
    s, t = (r % CH)[:, None], np.arange(CH)[None]
    put("tmask", np.concatenate([t > s, t >= s], axis=1).astype(np.float32))
    a, b = np.arange(CH)[:, None], np.arange(CH)[None]
    lev = [((a // m == b // m + 1) & (a // (2 * m) == b // (2 * m))) for m in (1, 2, 4, 8, 16, 32)]
    put("lmask", np.stack(lev, axis=1).astype(np.float32))
    put("l0t", lev[0].T.astype(np.float32))
    put("causal", np.where(r[None] <= r[:, None], 0.0, -3.0e38))
    return con


def _rope_table():
    inv = 10000.0 ** (-np.arange(64, dtype=np.float32) / 64)
    pos = np.arange(ROWS)
    ang = np.concatenate([(pos // 64)[None] * inv[:, None], (pos % 64)[None] * inv[:, None]], axis=0).astype(np.float32)
    return np.stack([np.cos(ang), np.sin(ang)], axis=1).astype(np.float32)


def _dft_table():
    n = np.arange(256)
    ang = 2 * np.pi * ((n[:, None] * n[None]) % 256) / 256
    t = np.concatenate([np.cos(ang), np.sin(ang)], axis=1) / 16
    return np.ascontiguousarray(t.reshape(2, P, 512).transpose(1, 0, 2)).astype(np.float32)


def _arrays(i):
    w = {n: np.asarray(i[n]) for n in ("x", "ctx_2", "rwkv_w_up", "rwkv_a_up", "rwkv_g_up")}
    xin = np.stack([w[n][0].T.reshape(KT, P, ROWS).transpose(1, 0, 2) for n in ("x", "ctx_2")])
    lora = np.zeros((P, 2, DA), np.float32)
    lora[0:32, 0], lora[32:64, 0], lora[0:96, 1] = w["rwkv_w_up"][0], w["rwkv_a_up"][0], w["rwkv_g_up"][0]
    return {"stream": _stream(i), "xin": np.ascontiguousarray(xin), "params": _params(i), "consts": _consts(), "lora": lora,
            "bada": np.ascontiguousarray(np.repeat(_columns(i["b_ada_2"][0], 72)[:, :, None], 2, axis=2)),
            "rope": _rope_table(), "dft": _dft_table(),
            "iota": np.ascontiguousarray(np.broadcast_to(np.arange(ROWS, dtype=np.float32)[None], (P, ROWS)))}


def kernel(**inputs):
    import concourse.bacc as bacc
    from concourse.bass_utils import run_bass_kernel_spmd

    nc = bacc.Bacc("TRN2", target_bir_lowering=False, num_devices=1)
    arrays = _arrays(inputs)
    aps = {n: nc.dram_tensor(n, a.shape, F32, kind="ExternalInput").ap() for n, a in arrays.items()}
    out = nc.dram_tensor("out", (P, KT, ROWS), F32, kind="ExternalOutput").ap()
    build(nc, out=out, **aps)
    got = run_bass_kernel_spmd(nc, [arrays], core_ids=[0]).results[0]["out"]
    return np.ascontiguousarray(got.transpose(1, 0, 2).reshape(DM, ROWS).T)[None]
```
